# Optimizing a Trainium2 kernel written in Bass

```python
import math
import jax, jax.numpy as jnp
from jax import lax
import numpy as np

D_MODEL = 1024
BATCH = 1
SEQ = 1024
DEPTH = 1

N_MEM = 256
MLSTM_HEADS = 4
MLSTM_HEAD_DIM = D_MODEL // 8
SB_HEADS = 4
SB_HEAD_DIM = D_MODEL // 16
MEM_HEADS = 4
MEM_HEAD_DIM = D_MODEL // 16
D_MLSTM = MLSTM_HEADS * MLSTM_HEAD_DIM
D_SB = SB_HEADS * SB_HEAD_DIM
D_MEMX = MEM_HEADS * MEM_HEAD_DIM
D_MIX = D_MLSTM + D_SB + D_MEMX
CONV_WIDTH = 4
CHUNK = 128
Q_BLOCK = 128
EPS = 1e-6
SPLIT_SIZES = (D_MLSTM,) * 5 + (MLSTM_HEADS, MLSTM_HEADS) + (D_SB,) * 4 + (D_MEMX,) * 2
D_IN = sum(SPLIT_SIZES)

kernel_name = "hybrid_mlstm_stickbreak_memxattn_layer"

def rmsnorm(x, g):
    xf = x.astype(jnp.float32)
    y = xf * lax.rsqrt(jnp.mean(xf * xf, axis=-1, keepdims=True) + EPS)
    return (y * g.astype(jnp.float32)).astype(x.dtype)

def head_rmsnorm(h, g):
    y = h * lax.rsqrt(jnp.mean(h * h, axis=-1, keepdims=True) + EPS)
    return y * g.astype(jnp.float32).reshape(h.shape[-2:])

def split_heads(a, n):
    return a.reshape(a.shape[:-1] + (n, a.shape[-1] // n))

def causal_dwconv(x, w, b):
    c = x.shape[-1]
    y = lax.conv_general_dilated(x, w[:, None, :], window_strides=(1,),
                                 padding=[(w.shape[0] - 1, 0)],
                                 dimension_numbers=("NWC", "WIO", "NWC"),
                                 feature_group_count=c)
    return y + b

def mlstm_chunkwise(q, k, v, i_pre, f_pre):
    B, S, H, d = q.shape
    nc = S // CHUNK
    k = k * (d ** -0.5)
    logf = jax.nn.log_sigmoid(f_pre)

    def chunks4(a):
        return a.reshape(B, nc, CHUNK, H, a.shape[-1]).transpose(1, 0, 3, 2, 4)

    def chunks3(a):
        return a.reshape(B, nc, CHUNK, H).transpose(1, 0, 3, 2)

    mask = jnp.tril(jnp.ones((CHUNK, CHUNK), dtype=bool))

    def step(carry, inp):
        C, n, m = carry
        qb, kb, vb, ib, fb = inp
        b = jnp.cumsum(fb, axis=-1)
        dmat = b[..., :, None] - b[..., None, :] + ib[..., None, :]
        dmat = jnp.where(mask, dmat, -jnp.inf)
        inter = b + m[..., None]
        m_t = jnp.maximum(inter, jnp.max(dmat, axis=-1))
        dexp = jnp.exp(dmat - m_t[..., None])
        inter_w = jnp.exp(inter - m_t)
        s = jnp.einsum("bhtd,bhsd->bhts", qb, kb) * dexp
        num = (jnp.einsum("bhts,bhse->bhte", s, vb)
               + inter_w[..., None] * jnp.einsum("bhtd,bhde->bhte", qb, C))
        den = jnp.sum(s, axis=-1) + inter_w * jnp.einsum("bhtd,bhd->bht", qb, n)
        h = num / jnp.maximum(jnp.abs(den), jnp.exp(-m_t))[..., None]
        b_last = b[..., -1]
        a_end = b_last[..., None] - b + ib
        m_new = jnp.maximum(b_last + m, jnp.max(a_end, axis=-1))
        w_end = jnp.exp(a_end - m_new[..., None])
        decay = jnp.exp(b_last + m - m_new)
        C_new = decay[..., None, None] * C + jnp.einsum("bhs,bhsd,bhse->bhde", w_end, kb, vb)
        n_new = decay[..., None] * n + jnp.einsum("bhs,bhsd->bhd", w_end, kb)
        return (C_new, n_new, m_new), h

    init = (jnp.zeros((B, H, d, v.shape[-1]), jnp.float32),
            jnp.zeros((B, H, d), jnp.float32),
            jnp.zeros((B, H), jnp.float32))
    _, hs = lax.scan(step, init, (chunks4(q), chunks4(k), chunks4(v), chunks3(i_pre), chunks3(logf)))
    return hs.transpose(1, 0, 3, 2, 4).reshape(B, S, H, v.shape[-1])

def stick_breaking_attention(q, k, v):
    B, S, H, d = q.shape
    scale = d ** -0.5
    outs = []
    for blk in range(S // Q_BLOCK):
        t0 = blk * Q_BLOCK
        t1 = t0 + Q_BLOCK
        qb, kb, vb = q[:, t0:t1], k[:, :t1], v[:, :t1]
        z = jnp.einsum("bthd,bshd->bhts", qb, kb) * scale
        strict = jnp.arange(t1)[None, :] < (t0 + jnp.arange(Q_BLOCK))[:, None]
        sp = jax.nn.softplus(z)
        log_beta = z - sp
        log_1m = jnp.where(strict, -sp, 0.0)
        suffix = lax.cumsum(log_1m, axis=3, reverse=True) - log_1m
        a = jnp.where(strict, jnp.exp(log_beta + suffix), 0.0)
        outs.append(jnp.einsum("bhts,bshd->bthd", a, vb))
    return jnp.concatenate(outs, axis=1)

def memory_cross_attention(q, k, v):
    scores = jnp.einsum("bthd,bmhd->bhtm", q, k) * (q.shape[-1] ** -0.5)
    p = jax.nn.softmax(scores, axis=-1)
    return jnp.einsum("bhtm,bmhd->bthd", p, v)

def setup_inputs(seed: int = 0) -> dict:
    key = jax.random.key(seed)
    ks = jax.random.split(key, 16)
    f32 = jnp.float32
    nrm = lambda k, s: jax.random.normal(k, s, f32)
    return {
        "x": nrm(ks[0], (BATCH, SEQ, D_MODEL)),
        "mem": nrm(ks[1], (BATCH, N_MEM, D_MODEL)),
        "g_pre": 1.0 + 0.05 * nrm(ks[2], (D_MODEL,)),
        "w_in": nrm(ks[3], (D_MODEL, D_IN)) * D_MODEL ** -0.5,
        "conv_w": nrm(ks[4], (CONV_WIDTH, 2 * D_MLSTM)) * CONV_WIDTH ** -0.5,
        "conv_b": 0.01 * nrm(ks[5], (2 * D_MLSTM,)),
        "i_bias": 0.1 * nrm(ks[6], (MLSTM_HEADS,)),
        "f_bias": jnp.linspace(3.0, 6.0, MLSTM_HEADS, dtype=f32) + 0.1 * nrm(ks[7], (MLSTM_HEADS,)),
        "g_mlstm_head": 1.0 + 0.05 * nrm(ks[8], (D_MLSTM,)),
        "g_sb_head": 1.0 + 0.05 * nrm(ks[9], (D_SB,)),
        "g_mem_head": 1.0 + 0.05 * nrm(ks[10], (D_MEMX,)),
        "g_mem": 1.0 + 0.05 * nrm(ks[11], (D_MODEL,)),
        "w_mem_kv": nrm(ks[12], (D_MODEL, 2 * D_MEMX)) * D_MODEL ** -0.5,
        "w_out": nrm(ks[13], (D_MIX, D_MODEL)) * D_MIX ** -0.5,
        "g_post": 1.0 + 0.05 * nrm(ks[14], (D_MODEL,)),
    }

def reference(x, mem, g_pre, w_in, conv_w, conv_b, i_bias, f_bias, g_mlstm_head, g_sb_head,
              g_mem_head, g_mem, w_mem_kv, w_out, g_post):
    f32 = jnp.float32
    dt = x.dtype
    B, S, _ = x.shape
    split_idx = [int(i) for i in np.cumsum(SPLIT_SIZES)[:-1]]
    for _layer in range(DEPTH):
        h = rmsnorm(x, g_pre)
        u = h @ w_in
        (q_m, k_m, v_m, o_m, z_m, i_m, f_m,
         q_s, k_s, v_s, z_s, q_c, z_c) = jnp.split(u, split_idx, axis=-1)

        qk = causal_dwconv(jnp.concatenate([q_m, k_m], axis=-1).astype(f32),
                           conv_w.astype(f32), conv_b.astype(f32))
        q_m2, k_m2 = jnp.split(jax.nn.silu(qk), 2, axis=-1)
        h_m = mlstm_chunkwise(split_heads(q_m2, MLSTM_HEADS), split_heads(k_m2, MLSTM_HEADS),
                              split_heads(v_m.astype(f32), MLSTM_HEADS),
                              i_m.astype(f32) + i_bias.astype(f32),
                              f_m.astype(f32) + f_bias.astype(f32))
        h_m = jax.nn.sigmoid(o_m.astype(f32)) * head_rmsnorm(h_m, g_mlstm_head).reshape(B, S, D_MLSTM)
        y_m = h_m * jax.nn.silu(z_m.astype(f32))

        h_s = stick_breaking_attention(split_heads(q_s.astype(f32), SB_HEADS),
                                       split_heads(k_s.astype(f32), SB_HEADS),
                                       split_heads(v_s.astype(f32), SB_HEADS))
        y_s = head_rmsnorm(h_s, g_sb_head).reshape(B, S, D_SB) * jax.nn.silu(z_s.astype(f32))

        kv = rmsnorm(mem, g_mem) @ w_mem_kv
        k_c, v_c = jnp.split(kv.astype(f32), 2, axis=-1)
        h_c = memory_cross_attention(split_heads(q_c.astype(f32), MEM_HEADS),
                                     split_heads(k_c, MEM_HEADS), split_heads(v_c, MEM_HEADS))
        y_c = head_rmsnorm(h_c, g_mem_head).reshape(B, S, D_MEMX) * jax.nn.silu(z_c.astype(f32))

        y = jnp.concatenate([y_m, y_s, y_c], axis=-1).astype(dt) @ w_out
        x = x + rmsnorm(y, g_post)
    return x


_drawn_inputs = setup_inputs


def setup_inputs(seed=0):
    import zlib

    import numpy as np

    out = dict(_drawn_inputs(seed))
    spreads = {}
    factors = {'conv_b': 21.575,
     'i_bias': 200.0,
     'g_mlstm_head': 15.199,
     'g_sb_head': 4.649,
     'g_mem_head': 4.639,
     'g_mem': 3.259}
    for name, (base, spread) in spreads.items():
        noise = np.random.default_rng([zlib.crc32(name.encode()), seed]).standard_normal(out[name].shape)
        drawn = base * np.exp(spread * noise) if base else spread * noise
        out[name] = __import__('jax').numpy.asarray(drawn.astype(out[name].dtype))
    for name, factor in factors.items():
        out[name] = (out[name] * factor).astype(out[name].dtype)
    return out
```

```python
from contextlib import ExitStack

import concourse.bass as bass
from concourse import mybir

ALU = mybir.AluOpType
ACT = mybir.ActivationFunctionType
AX_X = mybir.AxisListType.X
F32 = mybir.dt.float32
F32R = mybir.dt.float32r
BF16 = mybir.dt.bfloat16

P = 128
S = 1024
D = 1024
KT = D // P
NT = S // P
HALF = 512
NM = 256
H = 4
DH = 128
DA = 64
CW = 4
VW = DH + 1
EPS = 1e-6
NEG = -1e30

C_QM, C_KM, C_VM, C_OM, C_ZM, C_IF = 0, 512, 1024, 1536, 2048, 2560
C_QS, C_KS, C_VS, C_ZS, C_QC, C_ZC = 2568, 2824, 3080, 3336, 3592, 3848

PT_CW, PT_CB, PT_GPRE, PT_GMEM, PT_GM, PT_GS, PT_GC, N_PT = 0, 32, 40, 48, 56, 60, 62, 64

T_KS, T_VS, T_ZS, T_SB, T_CONV, T_VM, T_OUT, T_END = 4, 8, 10, 12, 24, 32, 36, 44
G_KS, G_VS, G_ZS, G_SB, G_CONV, G_VM, G_END = 4, 12, 20, 24, 48, 64, 80

CR = 4
ROUNDS = NT // 2


def after(reg, k):
    return reg + (k + 1 + CR)


def sb_order():
    part = 0
    out = []

    def third():
        nonlocal part
        if part < 36:
            out.append(("proj", part // 3, part % 3))
            part += 1

    for j in range(17):
        if j < 16:
            out.append(("scores", j, 0))
        third()
        if j:
            segs = 1 if (j - 1) // 2 < 4 else 2
            for seg in range(segs):
                out.append(("turn", j - 1, seg))
                third()
                out.append(("values", j - 1, seg))
    while part < 36:
        third()
    return out


def hybrid_layer(nc, x, mem, g_pre, w_in, conv_w, conv_b, i_bias, f_bias, g_mlstm_head, g_sb_head,
                 g_mem_head, g_mem, w_mem_kv, w_out, g_post, out, rows_dram):
    order = sb_order()
    seg_index = {}
    for what, j, seg in order:
        if what == "turn":
            seg_index[(j, seg)] = len(seg_index)
    NSEG = len(seg_index)
    assert NSEG % 2 == 0

    with ExitStack() as ctx:
        def sem(name):
            return ctx.enter_context(nc.semaphore(name))

        at = {"next": -(-nc.sbuf_base // 64) * 64}
        size = {F32: 4, F32R: 4, BF16: 2}

        def region(nbytes):
            base = at["next"]
            at["next"] = base + -(-nbytes // 64) * 64
            assert at["next"] <= nc.sbuf_top
            return {"at": base, "end": at["next"]}

        def place(reg, name, shape, dt=F32):
            n = size[dt]
            for d in shape[1:]:
                n *= d
            t = nc.alloc_sbuf_tensor_at(name, shape, dt, offset=reg["at"])
            reg["at"] += -(-n // 64) * 64
            assert reg["at"] <= reg["end"], name
            return t

        def again(reg, back):
            return {"at": back, "end": reg["end"]}

        r_ht = region(2 * KT * S * 4)
        r_yg = region(KT * S * 4)
        r_qk = region(KT * S * 4)
        r_vm = region(NT * H * VW * 4)
        r_w = region(3 * KT * 264 * 4)
        r_qc = region((2 * S + 2 * NM + 2 * H * DA) * 4)
        r_os = region(NT * H * DA * 4)
        r_wk = region(14 * 1024)
        r_c = {"at": at["next"], "end": nc.sbuf_top}
        b_yg, b_qk, b_vm, b_w, b_qc, b_os, b_wk = (r["at"] for r in (r_yg, r_qk, r_vm, r_w, r_qc, r_os, r_wk))

        ht_hi = place(r_ht, "ht_hi", [P, KT, S], F32R)
        ht_lo = place(r_ht, "ht_lo", [P, KT, S], F32R)
        yg = place(r_yg, "yg", [P, KT, S])
        xr = place(again(r_yg, b_yg), "xr", [P, NT, D])
        qkm = place(r_qk, "qkm", [P, KT, S])
        q = again(r_qk, b_qk)
        mt_hi = place(q, "mt_hi", [P, KT, NM], F32R)
        mt_lo = place(q, "mt_lo", [P, KT, NM], F32R)
        q = again(r_qk, b_qk)
        qk_s = place(q, "qk_s", [P, 4 * S])
        v_s = place(q, "v_s", [P, NT, H * DA])
        row_iw = place(q, "row_iw", [H, NT, P])
        q = again(r_qk, b_qk)
        xt = place(q, "xt", [P, 2, D])
        ot = place(q, "ot", [P, 2, D])
        gpost = place(q, "gpost", [P, D])
        sq_out = place(q, "sq_out", [P, D])
        vm = place(r_vm, "vm", [P, NT * H * VW])
        vm4 = vm[:, :].rearrange("p (c h e) -> p c h e", c=NT, h=H)
        q = again(r_vm, b_vm)
        mraw = place(q, "mraw", [P, 2, D])
        q = again(r_vm, b_vm)
        row_a = place(q, "row_a", [H, NT, P])
        row_m = place(q, "row_m", [H, NT, P])
        row_b = place(q, "row_b", [H, NT, P])
        row_d = place(q, "row_d", [H, NT, P])
        q = again(r_vm, b_vm)
        beta = place(q, "beta", [P, 2, S])
        keep = place(q, "keep", [P, 2, S])
        q = again(r_vm, b_vm)
        cb = place(q, "cb", [P, 2, S + 3])
        sg = place(q, "sg", [P, 2, S])
        wraw = place(r_w, "wraw", [P, KT, 264])
        whi = place(r_w, "whi", [P, KT, 264], F32R)
        wlo = place(r_w, "wlo", [P, KT, 264], F32R)
        q_c = place(r_qc, "q_c", [P, 2, S])
        k_c = place(r_qc, "k_c", [P, 2, NM])
        v_c = place(r_qc, "v_c", [P, 2, H * DA])
        os_ = place(r_os, "os", [P, NT, H, DA])
        q = again(r_wk, b_wk)
        at_ = place(q, "at", [P, 2, HALF])
        ts = place(q, "ts", [P, 2, HALF])
        sq_in = place(again(r_wk, b_wk + 4096), "sq_in", [P, D])
        qz = place(q, "qz", [P, 2, 2, P])
        q = again(r_wk, b_wk)
        pc = place(q, "pc", [P, H, NM])
        pct = place(q, "pct", [P, 2 * HALF])
        sqc = place(q, "sqc", [P, 2 * H, DA])
        hnc = place(q, "hnc", [P, 2 * H, DA])
        qcz = place(q, "qcz", [P, H, P])
        q = again(r_wk, b_wk)
        dm = place(q, "dm", [P, 2, H, P])
        iwb = place(q, "iwb", [P, 2, H, P])
        sd = place(q, "sd", [P, 2, H, P])
        sqm = place(q, "sqm", [P, H, P])
        q = again(r_os, b_os)
        kst = place(q, "kst", [P, 2, H, P])
        qs2 = place(q, "qs2", [P, 2, H, P])
        q = {"at": b_w + KT * 264 * 4, "end": r_w["end"]}
        kw = place(q, "kw", [P, 2, H, P])
        ns = place(q, "ns", [P, 2, H, VW])
        cst = place(q, "cst", [P, H, VW])
        hnm = place(q, "hnm", [P, 2, H, P])
        ident = place(r_c, "ident", [P, P])
        identb = place(r_c, "identb", [P, P], BF16)
        maskb = place(r_c, "maskb", [P, P], BF16)
        maskd = place(r_c, "maskd", [P, P])
        prow = place(r_c, "prow", [N_PT, P])
        pt = place(r_c, "pt", [P, N_PT])
        ifb = place(r_c, "ifb", [H, 2])
        gt = place(r_c, "gt", [P, NT, 2 * H])
        ks = place(r_c, "ks", [P, 2 * H])
        ones = place(r_c, "ones", [P, 1, 1])
        own = place(r_c, "own", [P, 2])
        epsc = place(r_c, "epsc", [P, 1])
        onec = place(r_c, "onec", [P, 1])
        ssx = place(r_c, "ssx", [P, 10])
        rsx = place(r_c, "rsx", [P, 10])
        bl_ = place(r_c, "bl", [H, NT])
        mp = place(r_c, "mp", [H, NT])
        ml = place(r_c, "ml", [H, NT])
        dec = place(r_c, "dec", [P, H, NT])
        cols = place(r_c, "cols", [P, 3, NT * H])
        mx = place(r_c, "mx", [P, H])
        nmx = place(r_c, "nmx", [P, H])
        sums = place(r_c, "sums", [P, H])
        r8 = place(r_c, "r8", [P, 2 * H])
        ss8 = place(r_c, "ss8", [P, 2 * H])
        u8 = place(r_c, "u8", [P, 2 * H])
        l8 = place(r_c, "l8", [P, 2 * H])
        cf8 = place(r_c, "cf8", [P, 2 * H])
        den = place(r_c, "den", [P, H])
        r4 = place(r_c, "r4", [P, H])
        ss4 = place(r_c, "ss4", [P, H])
        u4 = place(r_c, "u4", [P, H])
        l4 = place(r_c, "l4", [P, H])
        cf4 = place(r_c, "cf4", [P, H])
        sso = place(r_c, "sso", [P, 2])
        rso = place(r_c, "rso", [P, 2])

        ps = ctx.enter_context(nc.psum_tensor("ps", [P, 8 * HALF], F32))

        def bank(b, n=HALF, off=0, parts=P):
            return ps[0:parts, b * HALF + off:b * HALF + off + n]

        s_par = sem("s_par")
        s_mem = sem("s_mem")
        s_x = [sem(f"s_x{i}") for i in range(4)]
        s_raw = [sem("s_raw0"), sem("s_raw1")]
        s_gw = sem("s_gw")
        w_hi, w_lo = sem("w_hi"), sem("w_lo")
        gw_hi, gw_lo = sem("gw_hi"), sem("gw_lo")
        c_ready = sem("c_ready")
        pt_done, pt_ready = sem("pt_done"), sem("pt_ready")
        rs_ready = sem("rs_ready")
        xn_ready = sem("xn_ready")
        tr_done = sem("tr_done")
        hi_done, lo_done = sem("hi_done"), sem("lo_done")
        pj_done = sem("pj_done")
        pj_free = [sem("pj_free0"), sem("pj_free1")]
        gt_ready = sem("gt_ready")
        rt_done = sem("rt_done")
        row_act, row_dve = sem("row_act"), sem("row_dve")
        ct_done, ct_free = sem("ct_done"), sem("ct_free")
        s_rows = sem("s_rows")
        s_dec = sem("s_dec")
        zs_sig, zs_gate = sem("zs_sig"), sem("zs_gate")
        q_staged, z_ready, sg_ready = sem("q_staged"), sem("z_ready"), sem("sg_ready")
        a_ready, t_ready, t_ev = sem("a_ready"), sem("t_ready"), sem("t_ev")
        av_done, o_ready, o_ev = sem("av_done"), sem("o_ready"), sem("o_ev")
        gs_ready, ts_free = sem("gs_ready"), sem("ts_free")
        cv_first, cv_sum, cv_sig, cv_out = sem("cv_first"), sem("cv_sum"), sem("cv_sig"), sem("cv_out")
        qc_staged, sc_done, mx_ready, p_ready = sem("qc_staged"), sem("sc_done"), sem("mx_ready"), sem("p_ready")
        pt2_done, pa_ev, pd_ev, oc_done = sem("pt2_done"), sem("pa_ev"), sem("pd_ev"), sem("oc_done")
        sqc_ready, ssc_ready, rsc_ready, hn_ready = sem("sqc_ready"), sem("ssc_ready"), sem("rsc_ready"), sem("hn_ready")
        yt_done, y_done = sem("yt_done"), sem("y_done")
        s_nm = [sem("s_nm0"), sem("s_nm1")]
        s_iw = [sem("s_iw0"), sem("s_iw1")]
        nm_masked, k_staged, q_scaled = sem("nm_masked"), sem("k_staged"), sem("q_scaled")
        d_ready, st_done, kt_done = sem("d_ready"), sem("st_done"), sem("kt_done")
        sd_ready, kw_ready, n_done, kv_done = sem("sd_ready"), sem("kw_ready"), sem("n_done"), sem("kv_done")
        c_upd, ns_ready, sqm_ready, ssm_ready = sem("c_upd"), sem("ns_ready"), sem("sqm_ready"), sem("ssm_ready")
        rsm_ready, hnm_ready, ym_done, ygm_done = sem("rsm_ready"), sem("hnm_ready"), sem("ym_done"), sem("ygm_done")
        y_hi, y_lo, yo_done = sem("y_hi"), sem("y_lo"), sem("yo_done")
        s_xt = [sem("s_xt0"), sem("s_xt1")]
        s_gp = sem("s_gp")
        rso_ready, on_ready, ot_ready = sem("rso_ready"), sem("on_ready"), sem("ot_ready")
        s_out = [sem("s_out0"), sem("s_out1")]
        self_act, self_dve, self_pool = sem("self_act"), sem("self_dve"), sem("self_pool")

        cb_zero, cst_zero, waited = sem("cb_zero"), sem("cst_zero"), sem("waited")
        starts_at_cr = {
            "pe": (z_ready, t_ready, av_done, sc_done, pt2_done, oc_done, yt_done, st_done, kt_done, n_done,
                   kv_done, ym_done, yo_done),
            "act": (sg_ready, gs_ready, p_ready, pa_ev, sqc_ready, rsc_ready, d_ready, kw_ready, ns_ready,
                    sqm_ready, rsm_ready, y_hi, rso_ready, cv_first, cv_sig),
            "dve": (a_ready, t_ev, o_ev, ts_free, cv_sum, cv_out, mx_ready, pd_ev, ssc_ready, hn_ready, y_done,
                    sd_ready, c_upd, ssm_ready, hnm_ready, ygm_done, y_lo, on_ready),
            "pool": (q_staged, qc_staged, nm_masked, k_staged, q_scaled, ot_ready),
        }

        def start(eng, name):
            for s_ in starts_at_cr[name]:
                eng.sem_inc(s_, CR)

        class Chain:

            def __init__(self, eng, s):
                self.eng, self.s, self.n, self.it, self.per, self.base = eng, s, 0, None, 0, 0

            def __call__(self, ins):
                ins.then_inc(self.s, 1)
                self.n += 1
                self.eng.wait_ge(self.s, self.n if self.it is None else self.it * self.per + self.n)

            def loop(self, it, per):
                self.it, self.per, self.base = it, per, self.n

            def end(self, rounds):
                assert self.n - self.base == self.per, (self.n - self.base, self.per)
                self.n, self.it = self.base + self.per * rounds, None

        block = ctx.enter_context(nc.Block())

        @block.sync
        def _(sp):
            w_in3 = w_in.rearrange("(k p) n -> p k n", p=P)
            w_mem3 = w_mem_kv.rearrange("(k p) n -> p k n", p=P)
            w_out3 = w_out.rearrange("(k p) n -> p k n", p=P)
            x3 = x[0].rearrange("(t p) d -> p t d", p=P)

            def raw(n, slot, src):
                sp.wait_ge(w_hi, n - 1)
                sp.wait_ge(w_lo, n - 1)
                sp.dma_start(wraw[:, :, P * slot:P * slot + P], src).then_inc(s_raw[slot], 16)

            sp.dma_start(mraw[:, :, :], mem[0].rearrange("(t p) d -> p t d", p=P)).then_inc(s_mem, 16)
            for n in range(2):
                sp.dma_start(wraw[:, :, P * n:P * n + P], w_mem3[:, :, P * n:P * n + P]).then_inc(s_raw[n], 16)
            for i in range(4):
                sp.dma_start(xr[:, 2 * i:2 * i + 2, :], x3[:, 2 * i:2 * i + 2, :]).then_inc(s_x[i], 16)
            sp.dma_start(wraw[:, :, 256:264], w_in3[:, :, C_IF:C_IF + 8]).then_inc(s_gw, 16)
            for n in range(2, 4):
                raw(n, n % 2, w_mem3[:, :, P * n:P * n + P])
            for n in range(T_KS, T_SB):
                raw(n, n % 2, w_in3[:, :, C_QS + P * (n - T_KS):C_QS + P * (n - T_KS + 1)])
            with sp.Fori(0, 2) as hp:
                for j in range(6):
                    col = [C_OM + hp * 256, C_OM + hp * 256 + P, C_ZM + hp * 256, C_ZM + hp * 256 + P,
                           C_ZC + hp * P, C_QC + hp * P][j]
                    raw(T_SB + hp * 6 + j, j % 2, w_in3[:, :, bass.ds(col, P)])
            with sp.Fori(0, 4) as it:
                for a in range(2):
                    raw(T_CONV + it * 2 + a, a, w_in3[:, :, bass.ds(it * 256 + a * P, P)])
            with sp.Fori(0, 2) as u:
                for a in range(2):
                    raw(T_VM + u * 2 + a, a, w_in3[:, :, bass.ds(u * 256 + (C_VM + a * P), P)])
            sp.wait_ge(w_lo, T_OUT)
            for a in range(2):
                raw(T_OUT + a, a, w_out3[:, :, P * a:P * a + P])
            sp.wait_ge(y_done, after(0, NT - 1))

            def old_state_rows(it):
                for a in range(2):
                    sp.wait_ge(sd_ready, after(it * 2, a - 2))
                    sp.dma_start(dm[:, a, :, :], bass.AP(rows_dram.tensor, it * 256 + a * P, [[0, P], [S, H], [1, P]])
                                 ).then_inc(s_nm[a], 16)
                    sp.wait_ge(q_scaled, after(it * 2, a - 2))
                    sp.dma_start(iwb[:, a, :, :],
                                 bass.AP(rows_dram.tensor, it * 256 + (a * P + H * S), [[0, P], [S, H], [1, P]])
                                 ).then_inc(s_iw[a], 16)

            with sp.Fori(0, ROUNDS - 1) as it:
                old_state_rows(it)
                for a in range(2):
                    raw(T_OUT + 2 + it * 2 + a, a, w_out3[:, :, bass.ds(it * 256 + (2 + a) * P, P)])
            old_state_rows(ROUNDS - 1)
            sp.wait_ge(st_done, after(0, NT - 1))
            sp.wait_ge(k_staged, after(0, NT - 1))
            sp.wait_ge(q_scaled, after(0, NT - 1))
            for a in range(2):
                sp.sem_inc(s_out[a], 16)
            sp.dma_start(gpost[:, :], bass.AP(g_post.tensor, 0, [[0, P], [1, D]])).then_inc(s_gp, 16)
            with sp.Fori(0, ROUNDS) as it:
                for a in range(2):
                    sp.wait_ge(ot_ready, after(it * 2, a - 2))
                    sp.dma_start(xt[:, a, :], x[0][bass.ds(it * 256 + a * P, P), :]).then_inc(s_xt[a], 16)
                for a in range(2):
                    sp.wait_ge(ot_ready, after(it * 2, a))
                    sp.dma_start(out[0][bass.ds(it * 256 + a * P, P), :], ot[:, a, :]).then_inc(s_out[a], 16)
            for a in range(2):
                sp.wait_ge(s_out[a], 16 * (ROUNDS + 1))

        @block.gpsimd
        def _(pool):
            start(pool, "pool")
            chain = Chain(pool, self_pool)
            pool.memset(identb[:, :], 0.0)
            pool.memset(ident[:, :], 0.0)
            pool.memset(maskb[:, :], 0.0)
            pool.memset(maskd[:, :], 0.0)
            pool.memset(ones[:, :, :], 1.0)
            pool.memset(epsc[:, :], EPS)
            pool.memset(onec[:, :], 1.0)
            chain(pool.memset(own[:, :], 0.0))
            for hh in range(2):
                chain(pool.memset(own[DA * hh:DA * hh + DA, hh:hh + 1], 1.0))
            pool.memset(ks[:, 0:H], 1.0)
            chain(pool.memset(ks[:, H:2 * H], DH ** -0.5))
            for m in (ident, identb):
                pool.affine_select(out=m[:, :], in_=m[:, :], compare_op=ALU.not_equal, fill=1.0, base=0,
                                   pattern=[[-1, P]], channel_multiplier=1)
            pool.affine_select(out=maskb[:, :], in_=maskb[:, :], compare_op=ALU.is_gt, fill=NEG, base=0,
                               pattern=[[-1, P]], channel_multiplier=1)
            pool.affine_select(out=maskd[:, :], in_=maskd[:, :], compare_op=ALU.is_ge, fill=NEG, base=0,
                               pattern=[[1, P]], channel_multiplier=-1).then_inc(c_ready, 1)

            def low(n, slot, dst=None, col=None):
                pool.wait_ge(w_hi, n + 1)
                raw = wraw[:, :, P * slot:P * slot + P]
                if dst is None:
                    hi, lo = whi[:, :, P * slot:P * slot + P], wlo[:, :, P * slot:P * slot + P]
                else:
                    hi, lo = ht_hi[:, :, col], ht_lo[:, :, col]
                pool.tensor_tensor(lo, raw, hi.bitcast(F32), ALU.subtract).then_inc(w_lo, 1)

            for n in range(T_VS):
                low(n, n % 2)
            pool.wait_ge(gw_hi, 1)
            pool.tensor_tensor(wlo[:, :, 256:264], wraw[:, :, 256:264], whi[:, :, 256:264].bitcast(F32),
                               ALU.subtract).then_inc(gw_lo, 1)
            for n in range(T_VS, T_SB):
                low(n, n % 2)
            pool.wait_ge(lo_done, 24)
            for half in range(2):
                pool.wait_ge(pj_free[half], G_VS // 2)
            with pool.Fori(0, 2) as hp:
                for what, j, part in order:
                    if what == "scores" and j % 2 == 0:
                        i = j // 2
                        pool.wait_ge(z_ready, after(hp * 16, 2 * i - 3))
                        pool.tensor_tensor(qz[:, i % 2, :, :],
                                           qk_s[:, bass.ds(hp * S + i * P, P)].unsqueeze(1).broadcast_to([P, 2, P]),
                                           own[:, :].unsqueeze(2).broadcast_to([P, 2, P]), ALU.mult).then_inc(q_staged, 1)
                    if what == "proj" and j % 2 == 1 and part == 2:
                        low(T_SB + hp * 6 + j // 2, (j // 2) % 2)
            with pool.Fori(0, 4) as it:
                for a in range(2):
                    low(T_CONV + it * 2 + a, a)
            pool.wait_ge(cv_out, after(0, 7))
            pool.memset(vm4[:, :, :, DH:VW], 1.0)
            chain(pool.memset(r8[:, :], 1.0))
            with pool.Fori(0, 2) as u:
                for a in range(2):
                    low(T_VM + u * 2 + a, a)
                for b in range(4):
                    pool.wait_ge(sc_done, after(u * 4, b - 1))
                    for m in range(2):
                        c = pool.tensor_tensor(
                            qcz[:, 2 * m:2 * m + 2, :],
                            q_c[:, m, bass.ds(u * 512 + b * P, P)].unsqueeze(1).broadcast_to([P, 2, P]),
                            own[:, :].unsqueeze(2).broadcast_to([P, 2, P]), ALU.mult)
                    c.then_inc(qc_staged, 1)
            pool.wait_ge(y_done, after(0, NT - 1))
            with pool.Fori(0, ROUNDS) as it:
                for a in range(2):
                    tok = bass.ds(it * 256 + a * P, P)
                    pool.wait_ge(kt_done, after(it * 2, a - 2))
                    pool.tensor_tensor(kst[:, a, :, :], qkm[:, H:2 * H, tok],
                                       ones[:, :, :].broadcast_to([P, H, P]), ALU.mult).then_inc(k_staged, 1)
                    pool.wait_ge(s_iw[a], it * 16 + 16)
                    pool.wait_ge(n_done, after(it * 2, a - 2))
                    pool.tensor_tensor(qs2[:, a, :, :], qkm[:, 0:H, tok], iwb[:, a, :, :], ALU.mult).then_inc(q_scaled, 1)
                    pool.wait_ge(s_nm[a], it * 16 + 16)
                    pool.tensor_tensor(dm[:, a, :, :], dm[:, a, :, :],
                                       maskd[:, :].unsqueeze(1).broadcast_to([P, H, P]), ALU.add).then_inc(nm_masked, 1)
                for a in range(2):
                    low(T_OUT + it * 2 + a, a, True, bass.ds(it * 256 + a * P, P))
            with pool.Fori(0, ROUNDS) as it:
                for a in range(2):
                    pool.wait_ge(on_ready, after(it * 2, a))
                    pool.wait_ge(s_xt[a], it * 16 + 16)
                    pool.tensor_tensor(ot[:, a, :], ot[:, a, :], xt[:, a, :], ALU.add).then_inc(ot_ready, 1)

        @block.tensor
        def _(pe):
            def product(dst, stat, move, ks_):
                for k in ks_:
                    for s_, m_ in ((0, 0), (0, 1), (1, 0)):
                        last = pe.matmul(dst, stat(s_, k), move(m_, k), start=(k == 0 and not s_ and not m_),
                                         stop=(k == KT - 1 and s_ == 1))
                return last

            start(pe, "pe")
            htp, wp, mtp = (ht_hi, ht_lo), (whi, wlo), (mt_hi, mt_lo)

            def feature_group(slot, half, thirds=(0, 1, 2), src=htp, n=HALF):
                b = half
                for t in thirds:
                    last = product(bank(b, n), lambda i, k: wp[i][:, k, P * slot:P * slot + P],
                                   lambda i, k: src[i][:, k, half * n:half * n + n] if n == HALF else src[i][:, k, :],
                                   ((0, 1, 2), (3, 4, 5), (6, 7))[t])
                return last

            def token_group(tt, b, n, src=htp):
                return product(bank(b, n), lambda i, k: src[i][:, k, P * tt:P * tt + P],
                               lambda i, k: wp[i][:, k, 0:n], range(KT))

            pe.wait_ge(c_ready, 1)
            pe.wait_ge(s_par, 16 * 9)
            pe.transpose(bank(7, N_PT), prow[:, :], ident[0:N_PT, 0:N_PT]).then_inc(pt_done, 1)
            pe.wait_ge(pt_ready, 1)

            def turn_group(n, tiles, src, k):
                if n >= 6:
                    pe.wait_ge(lo_done, n - 5)
                b = 2 + n % 6
                for i, t in enumerate(tiles):
                    last = pe.transpose(bank(b, P, P * i), src[:, t, P * k:P * k + P], ident[:, :])
                last.then_inc(tr_done, 1)

            pe.wait_ge(xn_ready, 2)
            for k in range(KT):
                turn_group(k, (0, 1), mraw, k)
            pe.wait_ge(lo_done, 8)
            for n in range(2):
                pe.wait_ge(w_lo, n + 1)
                last = product(bank(n, NM), lambda i, k: wp[i][:, k, P * n:P * n + P],
                               lambda i, k: mtp[i][:, k, :], range(KT))
                last.then_inc(pj_done, 1)
            pe.wait_ge(w_lo, 4)
            for n in range(2):
                pe.wait_ge(pj_free[n], 1)
                token_group(n, n, NM, mtp).then_inc(pj_done, 1)
            for h2 in range(2):
                pe.wait_ge(xn_ready, 2 + 4 * (h2 + 1))
                for k in range(KT):
                    turn_group(8 + 8 * h2 + k, range(4 * h2, 4 * h2 + 4), xr, k)
            pe.wait_ge(lo_done, 24)

            with pe.Fori(0, 2) as it:
                for a in range(2):
                    pe.wait_ge(w_lo, it * 2 + (T_KS + a + 1))
                    for half in range(2):
                        pe.wait_ge(pj_free[half], it * 2 + (G_KS // 2 + a))
                        feature_group(a, half).then_inc(pj_done, 1)
            pe.wait_ge(w_lo, T_ZS)
            pe.wait_ge(gw_lo, 1)
            for tt in range(NT):
                pe.wait_ge(pj_free[tt % 2], G_VS // 2 + tt // 2)
                token_group(tt, tt % 2, 264).then_inc(pj_done, 1)
            for a in range(2):
                pe.wait_ge(w_lo, T_ZS + a + 1)
                for half in range(2):
                    pe.wait_ge(pj_free[half], G_ZS // 2 + a)
                    feature_group(a, half).then_inc(pj_done, 1)
                    if a == 0 and half == 0:
                        pe.wait_ge(gt_ready, NT)
                        for g in range(2):
                            for tt in range(NT):
                                last = pe.transpose(bank(2 + 2 * g + tt // 4, P, P * (tt % 4), H),
                                                    gt[:, tt, H * g:H * g + H], ident[:, :])
                        last.then_inc(rt_done, 1)
            pe.wait_ge(row_dve, 15)
            for r, row in enumerate((row_a, row_d, row_b)):
                for c in range(NT):
                    last = pe.transpose(bank(6, H, (r * NT + c) * H), row[:, c, :], ident[0:H, 0:H])
            last.then_inc(ct_done, 1)

            pe.wait_ge(ct_free, 1)
            with pe.Fori(0, 2) as hp:
                for what, j, part in order:
                    if what == "proj":
                        tile, half = j // 2, j % 2
                        if part == 0:
                            if half == 0:
                                pe.wait_ge(w_lo, hp * 6 + (T_SB + tile + 1))
                            pe.wait_ge(pj_free[half], hp * 6 + (G_SB // 2 + tile))
                        last = feature_group(tile % 2, half, (part,))
                        if part == 2:
                            last.then_inc(pj_done, 1)
                        continue
                    i, hh = j // 2, j % 2
                    if what == "scores":
                        n = P * (i + 1)
                        pe.wait_ge(q_staged, after(hp * 8, i))
                        pe.wait_ge(sg_ready, after(hp * 16, j - 2))
                        for lo in range(0, n, HALF):
                            w = min(HALF, n - lo)
                            pe.matmul(bank(2 + 2 * hh + lo // HALF, w), qz[:, i % 2, hh, :],
                                      qk_s[:, bass.ds(hp * S + (2 * S + lo), w)], start=True, stop=(lo + w < n))
                        pe.matmul(bank(2 + 2 * hh + i // 4, P, P * (i % 4)), identb[:, :], maskb[:, :],
                                  start=False, stop=True).then_inc(z_ready, 1)
                    elif what == "turn":
                        g = seg_index[(j, part)]
                        pe.wait_ge(a_ready, after(hp * 16, j))
                        pe.wait_ge(t_ev, after(hp * NSEG, g - 1))
                        for s_ in range(4 * part, min(4 * part + 4, i + 1)):
                            last = pe.transpose(bank(6, P, P * (s_ % 4)), beta[:, hh, P * s_:P * s_ + P], ident[:, :])
                        last.then_inc(t_ready, 1)
                    else:
                        g = seg_index[(j, part)]
                        pe.wait_ge(t_ev, after(hp * NSEG, g))
                        if part == 0:
                            pe.wait_ge(o_ev, after(hp * 16, j - 1))
                        for s_ in range(4 * part, min(4 * part + 4, i + 1)):
                            vs = v_s[:, s_, :]
                            last = pe.matmul(bank(7, DA), at_[:, g % 2, P * (s_ % 4):P * (s_ % 4) + P],
                                             vs[:, bass.ds(hp * P + hh * DA, DA)], start=(s_ == 0), stop=(s_ == i))
                        last.then_inc(av_done, 1)
            with pe.Fori(0, 4) as it:
                for a in range(2):
                    pe.wait_ge(w_lo, it * 2 + (T_CONV + a + 1))
                    for half in range(2):
                        pe.wait_ge(pj_free[half], it * 2 + (G_CONV // 2 + a))
                        feature_group(a, half).then_inc(pj_done, 1)
            with pe.Fori(0, 2) as u:
                def v_group(tt):
                    if tt == 0:
                        pe.wait_ge(w_lo, u * 2 + (T_VM + 2))
                    pe.wait_ge(pj_free[tt % 2], u * 4 + (G_VM // 2 + tt // 2))
                    token_group(tt, tt % 2, 256).then_inc(pj_done, 1)

                def turn_out(b):
                    pe.wait_ge(hn_ready, after(u * 4, b))
                    pe.wait_ge(y_done, after(u * 4, b - 1))
                    for m in range(4):
                        last = pe.transpose(bank(7, P, P * m), hnc[:, 2 * m:2 * m + 2, :].rearrange("p a b -> p (a b)"),
                                            ident[:, :])
                    last.then_inc(yt_done, 1)

                for b in range(4):
                    pe.wait_ge(qc_staged, after(u * 4, b))
                    pe.wait_ge(p_ready, after(u * 4, b - 1))
                    for h in range(H):
                        last = pe.matmul(bank(2 + h // 2, NM, NM * (h % 2)), qcz[:, h, :], k_c[:, h // 2, :],
                                         start=True, stop=True)
                    last.then_inc(sc_done, 1)
                    v_group(2 * b)
                    if b:
                        turn_out(b - 1)
                    pe.wait_ge(p_ready, after(u * 4, b))
                    pe.wait_ge(pa_ev, after(u * 4, b - 1))
                    pe.wait_ge(pd_ev, after(u * 4, b - 1))
                    for m in range(2 * H):
                        last = pe.transpose(bank(4 + m // 4, P, P * (m % 4)), pc[:, m // 2, P * (m % 2):P * (m % 2) + P],
                                            ident[:, :])
                    last.then_inc(pt2_done, 1)
                    v_group(2 * b + 1)
                    pe.wait_ge(pa_ev, after(u * 4, b))
                    pe.wait_ge(pd_ev, after(u * 4, b))
                    pe.wait_ge(hn_ready, after(u * 4, b - 1))
                    for h in range(H):
                        for m in range(2):
                            last = pe.matmul(bank(6, DA, DA * h), pct[:, P * (2 * h + m):P * (2 * h + m) + P],
                                             v_c[:, m, DA * h:DA * h + DA], start=(m == 0), stop=(m == 1))
                    last.then_inc(oc_done, 1)
                turn_out(3)
            pe.wait_ge(y_done, after(0, NT - 1))
            pe.wait_ge(cst_zero, 1)

            def m_scores(it, a):
                pe.wait_ge(k_staged, after(it * 2, a))
                pe.wait_ge(sd_ready, after(it * 2, a - 2))
                for h in range(H):
                    last = pe.matmul(bank(a, P, P * h), kst[:, a, h, :], qkm[:, h, bass.ds(it * 256 + a * P, P)],
                                     start=True, stop=True)
                last.then_inc(st_done, 1)
                pe.wait_ge(ygm_done, after(it * 2, a - 2))
                for h in range(H):
                    last = pe.transpose(bank(2 + a, P, P * h), kst[:, a, h, :], ident[:, :])
                last.then_inc(kt_done, 1)

            def m_outputs(it, a):
                pe.wait_ge(q_scaled, after(it * 2, a))
                pe.wait_ge(sd_ready, after(it * 2, a))
                pe.wait_ge(c_upd, after(it * 2, a - 1))
                pe.wait_ge(ns_ready, after(it * 2, a - 1))
                for h in range(H):
                    dst = bank(4 + h // 2, VW, VW * (h % 2))
                    pe.matmul(dst, qs2[:, a, h, :], cst[:, h, :], start=True, stop=False)
                    last = pe.matmul(dst, sd[:, a, h, :], vm[:, bass.ds(it * (2 * H * VW) + (a * H + h) * VW, VW)],
                                     start=False, stop=True)
                last.then_inc(n_done, 1)
                pe.wait_ge(kw_ready, after(it * 2, a))
                for h in range(H):
                    last = pe.matmul(bank(6 + h // 2, VW, VW * (h % 2)), kw[:, a, h, :],
                                     vm[:, bass.ds(it * (2 * H * VW) + (a * H + h) * VW, VW)], start=True, stop=True)
                last.then_inc(kv_done, 1)

            def m_turn(it, a):
                pe.wait_ge(hnm_ready, after(it * 2, a))
                for h in range(H):
                    last = pe.transpose(bank(2 + a, P, P * h), hnm[:, a, h, :], ident[:, :])
                last.then_inc(ym_done, 1)

            with pe.Fori(0, ROUNDS) as it:
                m_scores(it, 0)
                m_scores(it, 1)
                m_outputs(it, 0)
                m_outputs(it, 1)
                m_turn(it, 0)
                m_turn(it, 1)
            pe.wait_ge(w_lo, T_END)
            with pe.Fori(0, ROUNDS) as it:
                for a in range(2):
                    pe.wait_ge(y_lo, after(it * 2, a))
                    pe.wait_ge(on_ready, after(it * 2, a - 2))
                    for half in range(2):
                        last = product(bank(2 * a + half), lambda i, k: wp[i][:, k, P * a:P * a + P],
                                       lambda i, k: htp[i][:, k, HALF * half:HALF * half + HALF], range(KT))
                    last.then_inc(yo_done, 1)

        @block.scalar
        def _(act):
            start(act, "act")
            chain = Chain(act, self_act)

            def func(dst, src, f, **kw):
                return act.activation(dst, src, f, **kw)

            row = 0
            for src, n in ((conv_w.rearrange("j (c p) -> (j c) p", p=P), CW * KT), (conv_b, KT), (g_pre, KT),
                           (g_mem, KT), (g_mlstm_head, 4), (g_sb_head, 2), (g_mem_head, 2)):
                if n != CW * KT:
                    src = src.rearrange("(c p) -> c p", p=P)
                act.dma_start(prow[row:row + n, :], src).then_inc(s_par, 16)
                row += n
            for i, src in enumerate((i_bias, f_bias)):
                act.dma_start(ifb[:, i:i + 1], src.rearrange("(h o) -> h o", o=1)).then_inc(s_par, 16)
            act.preload_act_table_set("natural_log_exp_and_others")
            act.wait_ge(c_ready, 1)

            def high(n, slot, half_n, freed, col=None):
                act.wait_ge(s_raw[slot], half_n * 16 + 16)
                act.wait_ge(pj_done, freed)
                dst = whi[:, :, P * slot:P * slot + P] if col is None else ht_hi[:, :, col]
                func(dst, wraw[:, :, P * slot:P * slot + P], ACT.Copy).then_inc(w_hi, 1)

            def rms(tiles, src, at0):
                for i, t in enumerate(tiles):
                    chain(func(sq_in[:, :], src[:, t, :], ACT.Square, accum_out=ssx[:, at0 + i:at0 + i + 1]))
                chain(func(ssx[:, at0:at0 + 2], ssx[:, at0:at0 + 2], ACT.Ln, bias=epsc[:, :], scale=1.0 / D))
                func(rsx[:, at0:at0 + 2], ssx[:, at0:at0 + 2], ACT.Exp, scale=-0.5).then_inc(rs_ready, 1)

            act.wait_ge(s_mem, 16)
            rms((0, 1), mraw, 8)
            for n in range(2):
                act.wait_ge(s_raw[n], 16)
                func(whi[:, :, P * n:P * n + P], wraw[:, :, P * n:P * n + P], ACT.Copy).then_inc(w_hi, 1)
            act.wait_ge(pt_done, 1)
            func(pt[:, :], bank(7, N_PT), ACT.Copy).then_inc(pt_ready, 1)

            def split_high(n, dst, width, g):
                act.wait_ge(tr_done, n + 1)
                func(dst, bank(2 + n % 6, width), ACT.Copy, scale=g).then_inc(hi_done, 1)

            act.wait_ge(pt_ready, 1)
            for k in range(KT):
                split_high(k, mt_hi[:, k, :], NM, pt[:, PT_GMEM + k:PT_GMEM + k + 1])
            for i in range(4):
                act.wait_ge(s_x[i], 16)
                rms((2 * i, 2 * i + 1), xr, 2 * i)
                if i == 0:
                    high(2, 0, 1, 1)
                    high(3, 1, 1, 2)
            for h2 in range(2):
                for k in range(KT):
                    split_high(8 + 8 * h2 + k, ht_hi[:, k, HALF * h2:HALF * h2 + HALF], HALF,
                               pt[:, PT_GPRE + k:PT_GPRE + k + 1])
                if h2 == 0:
                    high(4, 0, 2, 4)
                    high(5, 1, 2, 4)
                    act.wait_ge(s_gw, 16)
                    func(whi[:, :, 256:264], wraw[:, :, 256:264], ACT.Copy).then_inc(gw_hi, 1)
            with act.Fori(0, 2) as it:
                for a in range(2):
                    for half in range(2):
                        act.wait_ge(pj_done, it * 4 + (G_KS + 2 * a + half + 1))
                        func(qk_s[:, bass.ds(it * (2 * S) + (a * S + half * HALF), HALF)], bank(half), ACT.Copy
                             ).then_inc(pj_free[half], 1)
                    high(T_KS + it * 2 + a + 2, a, it + (T_KS // 2 + 1), it * 4 + (G_KS + 2 * a + 2))
            for a in range(2):
                high(T_ZS + a, a, T_ZS // 2, G_ZS)
            act.wait_ge(rt_done, 1)
            flat = lambda r: r[:, :, :].rearrange("h c t -> h (c t)")
            func(flat(row_a), ps[0:H, 2 * HALF:4 * HALF], ACT.Identity, bias=ifb[:, 0:1]).then_inc(row_act, 1)
            func(flat(row_m), ps[0:H, 4 * HALF:6 * HALF], ACT.Identity, bias=ifb[:, 1:2]).then_inc(row_act, 1)
            act.wait_ge(row_dve, 1)
            func(flat(row_b), flat(row_b), ACT.Exp, scale=-1.0).then_inc(row_act, 1)
            act.wait_ge(row_act, 3)
            func(flat(row_b), flat(row_b), ACT.Ln, bias=onec[0:H, :]).then_inc(row_act, 1)
            high(T_SB, 0, T_SB // 2, G_ZS + 2)
            act.wait_ge(row_dve, 16)
            func(flat(row_iw), flat(row_iw), ACT.Exp).then_inc(row_act, 1)
            act.wait_ge(row_dve, 17)
            act.dma_start(rows_dram[0].rearrange("h (c t) -> h c t", c=NT), row_m[:, :, :]).then_inc(s_rows, 16)
            act.wait_ge(row_act, 5)
            act.dma_start(rows_dram[1].rearrange("h (c t) -> h c t", c=NT), row_iw[:, :, :]).then_inc(s_rows, 16)
            high(T_SB + 1, 1, T_SB // 2, G_SB)
            act.wait_ge(ct_done, 1)
            func(cols[:, 0, :], bank(6, NT * H), ACT.Copy)
            func(cols[:, 1:3, :].rearrange("p r n -> p (r n)"), bank(6, 2 * NT * H, NT * H), ACT.Exp).then_inc(ct_free, 1)
            for n in range(4):
                a, half = n // 2, n % 2
                act.wait_ge(pj_free[half], G_ZS // 2 + a + 1)
                if n >= 2:
                    act.wait_ge(zs_gate, n - 1)
                func(ts[:, n % 2, :], yg[:, 4 + a, HALF * half:HALF * half + HALF], ACT.Sigmoid).then_inc(zs_sig, 1)
            act.wait_ge(zs_gate, 4)
            act.wait_ge(s_rows, 32)
            act.dma_start(dec[:, :, :].rearrange("p h (c o) -> p (h c) o", o=1),
                          bass.AP(rows_dram.tensor, H * S + P - 1, [[0, P], [P, H * NT], [1, 1]]),
                          allow_slow_non_contiguous=True).then_inc(s_dec, 16)
            with act.Fori(0, 2) as hp:
                for what, j, part in order:
                    if what == "scores":
                        i, hh = j // 2, j % 2
                        n = P * (i + 1)
                        act.wait_ge(z_ready, after(hp * 16, j))
                        back = seg_index[((j - 2) % 16, 0 if (j - 2) % 16 < 8 else 1)] - (NSEG if j < 2 else 0)
                        act.wait_ge(t_ready, after(hp * NSEG, back))
                        act.wait_ge(a_ready, after(hp * 16, j - 2))
                        z = ps[:, (2 + 2 * hh) * HALF:(2 + 2 * hh) * HALF + n]
                        func(beta[:, hh, 0:n], z, ACT.Sigmoid, scale=DA ** -0.5)
                        func(keep[:, hh, 0:n], z, ACT.Sigmoid, scale=-(DA ** -0.5)).then_inc(sg_ready, 1)
                    if what == "proj" and part == 2:
                        tile, half = j // 2, j % 2
                        act.wait_ge(pj_done, hp * 12 + (G_SB + j + 1))
                        tok = slice(HALF * half, HALF * half + HALF)
                        ygf = yg[:, :, :].rearrange("p m t -> p (m t)")
                        if tile < 2:
                            func(ygf[:, bass.ds(hp * (2 * S) + (tile * S + half * HALF), HALF)], bank(half), ACT.Sigmoid
                                 ).then_inc(pj_free[half], 1)
                        elif tile < 4:
                            act.wait_ge(ts_free, after(hp * 4, j - 4 - 2))
                            func(ts[:, half, :], bank(half), ACT.Sigmoid).then_inc(gs_ready, 1)
                        elif tile == 4:
                            func(ygf[:, bass.ds(hp * S + (6 * S + half * HALF), HALF)], bank(half), ACT.Sigmoid
                                 ).then_inc(gs_ready, 1)
                        if half == 1:
                            high(None, tile % 2, hp * 3 + (T_SB + tile + 2) // 2, hp * 12 + (G_SB + j + 1))
            act.wait_ge(cb_zero, 1)

            def conv_round(it, more):
                for a in range(2):
                    m = it * 2 + a
                    for half in range(2):
                        act.wait_ge(pj_done, it * 4 + (G_CONV + 2 * a + half + 1))
                        act.wait_ge(cv_sum, after(it * 2, a - 2))
                        func(cb[:, a, 3 + HALF * half:3 + HALF * half + HALF], bank(half), ACT.Copy
                             ).then_inc(pj_free[half], 1)
                    for half in range(2):
                        act.wait_ge(pj_free[half], it * 2 + (G_CONV // 2 + a + 1))
                    qk = qkm[:, :, :].rearrange("p m t -> p (m t)")[:, bass.ds(m * S, S)]
                    func(qk, cb[:, a, 3:3 + S], ACT.Identity, bias=pt[:, bass.ds(m + PT_CB, 1)],
                         scale=pt[:, bass.ds(m + (PT_CW + 3 * KT), 1)]).then_inc(cv_first, 1)
                    if more:
                        high(None, a, it + (T_CONV // 2 + 1), it * 4 + (G_CONV + 2 * a + 2))
                    act.wait_ge(cv_sum, after(it * 2, a))
                    act.wait_ge(cv_out, after(it * 2, a - 2))
                    act.sem_inc(waited, 1)
                    func(sg[:, a, :], qk, ACT.Sigmoid).then_inc(cv_sig, 1)

            with act.Fori(0, 3) as it:
                conv_round(it, True)
            conv_round(3, False)
            act.preload_act_table_set("natural_log_exp_and_others")
            act.wait_ge(cv_out, after(0, 7))
            with act.Fori(0, 2) as u:
                for a in range(2):
                    high(None, a, u + T_VM // 2, u * 8 + G_VM)

                def v_copy(tt):
                    act.wait_ge(pj_done, u * 8 + (G_VM + tt + 1))
                    func(vm[:, :].rearrange("p (n e) -> p n e", e=VW)[:, bass.ds(u * 2 + tt * H, 2), 0:DH],
                         bank(tt % 2, 2 * DH).rearrange("p (a e) -> p a e", a=2), ACT.Copy).then_inc(pj_free[tt % 2], 1)

                for b in range(4):
                    act.wait_ge(mx_ready, after(u * 4, b))
                    act.wait_ge(pt2_done, after(u * 4, b - 1))
                    for h in range(H):
                        c = func(pc[:, h, :], bank(2 + h // 2, NM, NM * (h % 2)), ACT.Exp, bias=nmx[:, h:h + 1],
                                 scale=DA ** -0.5, accum_out=sums[:, h:h + 1])
                    c.then_inc(p_ready, 1)
                    v_copy(2 * b)
                    act.wait_ge(pt2_done, after(u * 4, b))
                    act.wait_ge(oc_done, after(u * 4, b - 1))
                    func(pct[:, HALF:2 * HALF], bank(5), ACT.Copy).then_inc(pa_ev, 1)
                    v_copy(2 * b + 1)
                    act.wait_ge(ssc_ready, after(u * 4, b - 1))
                    func(sqc[:, 0:H, :].rearrange("p h e -> p (h e)"),
                         os_[:, :, :, :].rearrange("p i h e -> p (i h e)")[:, bass.ds(u * 1024 + b * 256, 256)], ACT.Square)
                    act.wait_ge(oc_done, after(u * 4, b))
                    func(sqc[:, H:2 * H, :].rearrange("p h e -> p (h e)"), bank(6, H * DA), ACT.Square
                         ).then_inc(sqc_ready, 1)
                    act.wait_ge(ssc_ready, after(u * 4, b))
                    if b == 0:
                        chain.loop(u, 4)
                    chain(func(l8[:, :], u8[:, :], ACT.Ln, bias=epsc[:, :], scale=1.0 / DA))
                    func(l8[:, :], l8[:, :], ACT.Exp, scale=-0.5).then_inc(rsc_ready, 1)
            chain.end(2)
            act.wait_ge(y_done, after(0, NT - 1))
            with act.Fori(0, ROUNDS) as it:
                chain.loop(it, 2)

                def col(r, a, h):
                    return cols[:, :, :].rearrange("p r n -> p (r n)")[:, bass.ds(it * (2 * H) + (r * NT * H + a * H + h), 1)]

                for a in range(2):
                    act.wait_ge(nm_masked, after(it * 2, a))
                    for h in range(H):
                        c = func(dm[:, a, h, :], dm[:, a, h, :], ACT.Exp, bias=col(0, a, h))
                    c.then_inc(d_ready, 1)
                    act.wait_ge(kt_done, after(it * 2, a))
                    act.wait_ge(kv_done, after(it * 2, a - 2))
                    for h in range(H):
                        c = func(kw[:, a, h, :], bank(2 + a, P, P * h), ACT.Copy, scale=col(1, a, h))
                    c.then_inc(kw_ready, 1)
                for a in range(2):
                    act.wait_ge(n_done, after(it * 2, a))
                    act.wait_ge(hnm_ready, after(it * 2, a - 2))
                    func(ns[:, a, :, :].rearrange("p (b h) e -> p b (h e)", b=2),
                         ps[:, 4 * HALF:6 * HALF].rearrange("p (b n) -> p b n", b=2)[:, :, 0:2 * VW], ACT.Copy
                         ).then_inc(ns_ready, 1)
                    act.wait_ge(ns_ready, after(it * 2, a))
                    act.wait_ge(ssm_ready, after(it * 2, a - 1))
                    func(sqm[:, :, :], ns[:, a, :, 0:DH], ACT.Square).then_inc(sqm_ready, 1)
                    act.wait_ge(ssm_ready, after(it * 2, a))
                    chain(func(l4[:, :], u4[:, :], ACT.Ln, bias=epsc[:, :], scale=1.0 / DH))
                    func(l4[:, :], l4[:, :], ACT.Exp, scale=-0.5).then_inc(rsm_ready, 1)
                    high(None, a, it + T_OUT // 2, G_END, bass.ds(it * 256 + a * P, P))
            chain.end(ROUNDS)
            act.wait_ge(ygm_done, after(0, NT - 1))

            def y_high(reg, a):
                act.wait_ge(yo_done, after(reg * 2, a - 2))
                func(whi[:, :, P * a:P * a + P], yg[:, :, bass.ds(reg * 256 + a * P, P)], ACT.Copy).then_inc(y_hi, 1)

            def out_rms(it, a):
                act.wait_ge(yo_done, after(it * 2, a))
                chain(func(sq_out[:, :], ps[:, 2 * a * HALF:(2 * a + 2) * HALF], ACT.Square, accum_out=sso[:, a:a + 1]))
                chain(func(sso[:, a:a + 1], sso[:, a:a + 1], ACT.Ln, bias=epsc[:, :], scale=1.0 / D))
                act.wait_ge(on_ready, after(it * 2, a - 2))
                func(rso[:, a:a + 1], sso[:, a:a + 1], ACT.Exp, scale=-0.5).then_inc(rso_ready, 1)

            for a in range(2):
                y_high(0, a)
            act.wait_ge(s_gp, 16)
            with act.Fori(0, ROUNDS - 1) as it:
                chain.loop(it, 4)
                for a in range(2):
                    out_rms(it, a)
                    y_high(it + 1, a)
            chain.end(ROUNDS - 1)
            for a in range(2):
                out_rms(ROUNDS - 1, a)

        @block.vector
        def _(dve):
            start(dve, "dve")
            chain = Chain(dve, self_dve)
            for i, (src, t, at0) in enumerate([(mraw, 0, 8)] + [(xr, 2 * i, 2 * i) for i in range(4)]):
                dve.wait_ge(rs_ready, i + 1)
                for k in range(2):
                    dve.tensor_scalar(src[:, t + k, :], src[:, t + k, :], rsx[:, at0 + k:at0 + k + 1], None,
                                      ALU.mult).then_inc(xn_ready, 1)
                if i == 0:
                    dve.wait_ge(pt_ready, 1)
                    for k in range(KT):
                        dve.wait_ge(hi_done, k + 1)
                        dve.scalar_tensor_tensor(out=mt_lo[:, k, :], in0=bank(2 + k % 6, NM),
                                                 scalar=pt[:, PT_GMEM + k:PT_GMEM + k + 1],
                                                 in1=mt_hi[:, k, :].bitcast(F32), op0=ALU.mult, op1=ALU.subtract
                                                 ).then_inc(lo_done, 1)
                if i == 1:
                    for n in range(2):
                        dve.wait_ge(pj_done, n + 1)
                        dve.tensor_copy(k_c[:, n, :], bank(n, NM)).then_inc(pj_free[n], 1)
                if i == 2:
                    for n in range(2):
                        dve.wait_ge(pj_done, n + 3)
                        dve.tensor_copy(v_c[:, n, :], bank(n, NM)).then_inc(pj_free[n], 1)
            for n in range(16):
                h2, k = n // 8, n % 8
                dve.wait_ge(hi_done, 8 + n + 1)
                tok = slice(HALF * h2, HALF * h2 + HALF)
                dve.scalar_tensor_tensor(out=ht_lo[:, k, tok], in0=bank(2 + (8 + n) % 6),
                                         scalar=pt[:, PT_GPRE + k:PT_GPRE + k + 1],
                                         in1=ht_hi[:, k, tok].bitcast(F32), op0=ALU.mult, op1=ALU.subtract
                                         ).then_inc(lo_done, 1)
            for tt in range(NT):
                dve.wait_ge(pj_done, G_VS + tt + 1)
                dve.tensor_copy(gt[:, tt, :], bank(tt % 2, 8, 256)).then_inc(gt_ready, 1)
                dve.tensor_copy(v_s[:, tt, :], bank(tt % 2, 256)).then_inc(pj_free[tt % 2], 1)

            def raw_gate(n):
                a, half = n // 2, n % 2
                dve.wait_ge(pj_done, G_ZS + n + 1)
                dve.tensor_copy(yg[:, 4 + a, HALF * half:HALF * half + HALF], bank(half)).then_inc(pj_free[half], 1)

            raw_gate(0)
            step = Chain(dve, row_dve)
            flat = lambda r: r[:, :, :].rearrange("h c t -> h (c t)")
            dve.wait_ge(row_act, 2)
            step(dve.scalar_tensor_tensor(out=flat(row_b), in0=flat(row_m), scalar=-1.0, in1=flat(row_m),
                                          op0=ALU.mult, op1=ALU.max))
            step(dve.memset(flat(row_d), 1.0))
            step(dve.memset(row_d[:, :, 0:1], 0.0))
            raw_gate(1)
            dve.wait_ge(row_act, 4)
            step(dve.scalar_tensor_tensor(out=flat(row_m), in0=flat(row_m), scalar=0.0, in1=flat(row_b),
                                          op0=ALU.min, op1=ALU.subtract))
            step(dve.tensor_tensor_scan(flat(row_b), flat(row_d), flat(row_m), 0.0, ALU.mult, ALU.add))
            step(dve.tensor_tensor(flat(row_a), flat(row_a), flat(row_b), ALU.subtract))
            step(dve.tensor_copy(bl_[:, :], row_b[:, :, P - 1]))
            step(dve.memset(flat(row_d), 0.0))
            step(dve.tensor_copy(row_d[:, 1:NT, 0], bl_[:, 0:NT - 1]))
            raw_gate(2)
            step(dve.tensor_tensor_scan(flat(row_m), flat(row_d), flat(row_a), 0.0, ALU.add, ALU.max))
            step(dve.tensor_copy(ml[:, :], row_m[:, :, P - 1]))
            step(dve.memset(mp[:, 0:1], 0.0))
            step(dve.tensor_tensor(mp[:, 1:NT], bl_[:, 0:NT - 1], ml[:, 0:NT - 1], ALU.add))
            step(dve.tensor_tensor(row_d[:, :, :], row_a[:, :, :], ml[:, :].unsqueeze(2).broadcast_to([H, NT, P]),
                                   ALU.subtract))
            step(dve.scalar_tensor_tensor(out=flat(row_b), in0=flat(row_b), scalar=-1.0, in1=flat(row_m),
                                          op0=ALU.mult, op1=ALU.subtract))
            step(dve.tensor_tensor(row_iw[:, :, :], mp[:, :].unsqueeze(2).broadcast_to([H, NT, P]), row_m[:, :, :],
                                   ALU.subtract))
            step(dve.tensor_scalar(flat(row_m), flat(row_m), -1.0, None, ALU.mult))
            raw_gate(3)
            for n in range(4):
                a, half = n // 2, n % 2
                y = yg[:, 4 + a, HALF * half:HALF * half + HALF]
                dve.wait_ge(zs_sig, n + 1)
                dve.scalar_tensor_tensor(out=y, in0=y, scalar=pt[:, PT_GS + a:PT_GS + a + 1], in1=ts[:, n % 2, :],
                                         op0=ALU.mult, op1=ALU.mult).then_inc(zs_gate, 1)
            with dve.Fori(0, 2) as hp:
                chain.loop(hp, 16 + 4)
                ygf = yg[:, :, :].rearrange("p m t -> p (m t)")

                def shares(j):
                    hh, n = j % 2, P * (j // 2 + 1)
                    dve.wait_ge(sg_ready, after(hp * 16, j))
                    chain(dve.tensor_tensor_scan(keep[:, hh, n - 1::-1], keep[:, hh, n - 1::-1], keep[:, hh, n - 1::-1],
                                                 1.0, ALU.mult, ALU.bypass))
                    dve.tensor_tensor(beta[:, hh, 0:n - 1], beta[:, hh, 0:n - 1], keep[:, hh, 1:n], ALU.mult
                                      ).then_inc(a_ready, 1)

                for what, j, part in order:
                    i, hh = j // 2, j % 2
                    if what == "scores" and j == 0:
                        shares(0)
                    if what == "turn":
                        g = seg_index[(j, part)]
                        n = P * (min(4 * part + 4, i + 1) - 4 * part)
                        dve.wait_ge(t_ready, after(hp * NSEG, g))
                        dve.wait_ge(av_done, after(hp * NSEG, g - 2))
                        dve.tensor_copy(at_[:, g % 2, 0:n], bank(6, n)).then_inc(t_ev, 1)
                    if what == "values" and (i < 4 or part == 1):
                        if j < 15:
                            shares(j + 1)
                        g = seg_index[(j, part)]
                        dve.wait_ge(av_done, after(hp * NSEG, g))
                        dve.tensor_copy(os_[:, :, :, :].rearrange("p i h e -> p (i h e)")[
                            :, bass.ds(hp * (2 * DA) + (i * H * DA + hh * DA), DA)], bank(7, DA)).then_inc(o_ev, 1)
                    if what == "proj" and part == 2:
                        tile, half = j // 2, j % 2
                        if tile in (2, 3):
                            dve.wait_ge(gs_ready, after(hp * 6, j - 4))
                            m = hp * 2 + (tile - 2)
                            chain(dve.scalar_tensor_tensor(out=ts[:, half, :], in0=bank(half),
                                                           scalar=pt[:, bass.ds(m + PT_GM, 1)], in1=ts[:, half, :],
                                                           op0=ALU.mult, op1=ALU.mult))
                            dve.sem_inc(pj_free[half], 1)
                            y = ygf[:, bass.ds(hp * (2 * S) + ((tile - 2) * S + half * HALF), HALF)]
                            dve.tensor_tensor(y, y, ts[:, half, :], ALU.mult).then_inc(ts_free, 1)
                        elif tile == 4:
                            dve.wait_ge(gs_ready, after(hp * 6, j - 4))
                            y = ygf[:, bass.ds(hp * S + (6 * S + half * HALF), HALF)]
                            dve.scalar_tensor_tensor(out=y, in0=bank(half), scalar=pt[:, bass.ds(hp + PT_GC, 1)], in1=y,
                                                     op0=ALU.mult, op1=ALU.mult).then_inc(pj_free[half], 1)
                        elif tile == 5:
                            dve.wait_ge(pj_done, hp * 12 + (G_SB + j + 1))
                            dve.tensor_copy(q_c[:, :, :].rearrange("p m t -> p (m t)")[
                                :, bass.ds(hp * S + half * HALF, HALF)], bank(half)).then_inc(pj_free[half], 1)
            chain.end(2)
            dve.wait_ge(av_done, after(0, 2 * NSEG - 1))
            dve.memset(cb[:, :, 0:3], 0.0).then_inc(cb_zero, 1)
            with dve.Fori(0, 4) as it:
                chain.loop(it, 4)
                for a in range(2):
                    m = it * 2 + a
                    qk = qkm[:, :, :].rearrange("p m t -> p (m t)")[:, bass.ds(m * S, S)]
                    dve.wait_ge(cv_first, after(it * 2, a))
                    for j in (2, 1, 0):
                        c = dve.scalar_tensor_tensor(out=qk, in0=cb[:, a, j:j + S],
                                                     scalar=pt[:, bass.ds(m + (PT_CW + j * KT), 1)], in1=qk,
                                                     op0=ALU.mult, op1=ALU.add)
                        if j:
                            chain(c)
                    c.then_inc(cv_sum, 1)
                    dve.wait_ge(cv_sig, after(it * 2, a))
                    dve.scalar_tensor_tensor(out=qk, in0=qk, scalar=ks[:, bass.ds(m, 1)], in1=sg[:, a, :],
                                             op0=ALU.mult, op1=ALU.mult).then_inc(cv_out, 1)
            chain.end(4)
            with dve.Fori(0, 2) as u:
                chain.loop(u, 4 * 5)

                def gate(b):
                    dve.wait_ge(yt_done, after(u * 4, b))
                    y = yg[:, 4:8, bass.ds(u * 512 + b * P, P)]
                    dve.tensor_tensor(y, y, bank(7).rearrange("p (m t) -> p m t", m=4), ALU.mult).then_inc(y_done, 1)

                for b in range(4):
                    dve.wait_ge(sc_done, after(u * 4, b))
                    chain(dve.tensor_reduce(mx[:, :], ps[:, 2 * HALF:4 * HALF].rearrange("p (h m) -> p h m", h=H),
                                            AX_X, ALU.max))
                    dve.tensor_scalar(nmx[:, :], mx[:, :], -(DA ** -0.5), None, ALU.mult).then_inc(mx_ready, 1)
                    if b:
                        gate(b - 1)
                    dve.wait_ge(p_ready, after(u * 4, b))
                    chain(dve.reciprocal(r8[:, H:2 * H], sums[:, :]))
                    dve.wait_ge(pt2_done, after(u * 4, b))
                    dve.wait_ge(oc_done, after(u * 4, b - 1))
                    dve.tensor_copy(pct[:, 0:HALF], bank(4)).then_inc(pd_ev, 1)
                    dve.wait_ge(sqc_ready, after(u * 4, b))
                    chain(dve.tensor_reduce(ss8[:, :], sqc[:, :, :], AX_X, ALU.add))
                    chain(dve.tensor_tensor(ss8[:, :], ss8[:, :], r8[:, :], ALU.mult))
                    dve.tensor_tensor(u8[:, :], ss8[:, :], r8[:, :], ALU.mult).then_inc(ssc_ready, 1)
                    dve.wait_ge(rsc_ready, after(u * 4, b))
                    chain(dve.tensor_tensor(cf8[:, :], l8[:, :], r8[:, :], ALU.mult))
                    dve.wait_ge(yt_done, after(u * 4, b - 1))
                    dve.tensor_tensor(hnc[:, 0:H, :], os_[:, :, :, :].rearrange("p i h e -> p (i h) e")[
                        :, bass.ds(u * 16 + b * H, H), :], cf8[:, 0:H].unsqueeze(2).broadcast_to([P, H, DA]), ALU.mult)
                    dve.tensor_tensor(hnc[:, H:2 * H, :], bank(6, H * DA).rearrange("p (h e) -> p h e", h=H),
                                      cf8[:, H:2 * H].unsqueeze(2).broadcast_to([P, H, DA]), ALU.mult).then_inc(hn_ready, 1)
                gate(3)
            chain.end(2)
            dve.wait_ge(pj_done, G_END)
            chain(dve.memset(cst[:, :, :], 0.0))
            dve.sem_inc(cst_zero, 1)
            dve.wait_ge(s_dec, 16)
            with dve.Fori(0, ROUNDS) as it:
                chain.loop(it, 2 * 6)
                for a in range(2):
                    dve.wait_ge(d_ready, after(it * 2, a))
                    dve.wait_ge(st_done, after(it * 2, a))
                    dve.wait_ge(n_done, after(it * 2, a - 2))
                    dve.tensor_tensor(sd[:, a, :, :], bank(a).rearrange("p (h t) -> p h t", h=H), dm[:, a, :, :],
                                      ALU.mult).then_inc(sd_ready, 1)
                for a in range(2):
                    dve.wait_ge(kv_done, after(it * 2, a))
                    decf = dec[:, :, :].rearrange("p h c -> p (h c)")
                    for h in range(H):
                        c = dve.scalar_tensor_tensor(out=cst[:, h, :], in0=cst[:, h, :],
                                                     scalar=decf[:, bass.ds(it * 2 + (h * NT + a), 1)],
                                                     in1=bank(6 + h // 2, VW, VW * (h % 2)), op0=ALU.mult, op1=ALU.add)
                    c.then_inc(c_upd, 1)
                    dve.wait_ge(ns_ready, after(it * 2, a))
                    chain(dve.scalar_tensor_tensor(out=den[:, :], in0=ns[:, a, :, DH], scalar=-1.0, in1=ns[:, a, :, DH],
                                                   op0=ALU.mult, op1=ALU.max))
                    chain(dve.tensor_tensor(den[:, :], den[:, :], cols[:, 2, bass.ds(it * (2 * H) + a * H, H)], ALU.max))
                    chain(dve.reciprocal(r4[:, :], den[:, :]))
                    dve.wait_ge(sqm_ready, after(it * 2, a))
                    chain(dve.tensor_reduce(ss4[:, :], sqm[:, :, :], AX_X, ALU.add))
                    chain(dve.tensor_tensor(ss4[:, :], ss4[:, :], r4[:, :], ALU.mult))
                    dve.tensor_tensor(u4[:, :], ss4[:, :], r4[:, :], ALU.mult).then_inc(ssm_ready, 1)
                    dve.wait_ge(rsm_ready, after(it * 2, a))
                    chain(dve.tensor_tensor(cf4[:, :], l4[:, :], r4[:, :], ALU.mult))
                    dve.wait_ge(ym_done, after(it * 2, a - 2))
                    dve.tensor_tensor(hnm[:, a, :, :], ns[:, a, :, 0:DH], cf4[:, :].unsqueeze(2).broadcast_to([P, H, DH]),
                                      ALU.mult).then_inc(hnm_ready, 1)
                for a in range(2):
                    dve.wait_ge(ym_done, after(it * 2, a))
                    y = yg[:, 0:H, bass.ds(it * 256 + a * P, P)]
                    dve.tensor_tensor(y, y, bank(2 + a).rearrange("p (h t) -> p h t", h=H), ALU.mult).then_inc(ygm_done, 1)
            chain.end(ROUNDS)

            def y_low(reg, a):
                dve.wait_ge(y_hi, after(reg * 2, a))
                dve.tensor_tensor(wlo[:, :, P * a:P * a + P], yg[:, :, bass.ds(reg * 256 + a * P, P)],
                                  whi[:, :, P * a:P * a + P].bitcast(F32), ALU.subtract).then_inc(y_lo, 1)

            def out_norm(it, a):
                dve.wait_ge(rso_ready, after(it * 2, a))
                dve.wait_ge(s_out[a], it * 16 + 16)
                dve.scalar_tensor_tensor(out=ot[:, a, :], in0=ps[:, 2 * a * HALF:(2 * a + 2) * HALF],
                                         scalar=rso[:, a:a + 1], in1=gpost[:, :], op0=ALU.mult, op1=ALU.mult
                                         ).then_inc(on_ready, 1)

            for a in range(2):
                y_low(0, a)
            dve.wait_ge(s_gp, 16)
            with dve.Fori(0, ROUNDS - 1) as it:
                for a in range(2):
                    out_norm(it, a)
                    y_low(it + 1, a)
            for a in range(2):
                out_norm(ROUNDS - 1, a)


_INS = ["x", "mem", "g_pre", "w_in", "conv_w", "conv_b", "i_bias", "f_bias", "g_mlstm_head", "g_sb_head",
        "g_mem_head", "g_mem", "w_mem_kv", "w_out", "g_post"]


def kernel(**inputs):
    import numpy as _np
    import concourse.bacc as _bacc
    from concourse import mybir as _mybir
    from concourse.bass_utils import run_bass_kernel_spmd as _run

    nc = _bacc.Bacc("TRN2", target_bir_lowering=False, num_devices=1)
    arrays, args = {}, []
    for name in _INS:
        a = _np.ascontiguousarray(inputs[name])
        arrays[f"in_{name}_dram"] = a
        args.append(nc.dram_tensor(f"in_{name}_dram", a.shape, _mybir.dt.from_np(a.dtype), kind="ExternalInput").ap())
    args.append(nc.dram_tensor("out_dram", (1, S, D), _mybir.dt.float32, kind="ExternalOutput").ap())
    args.append(nc.dram_tensor("rows_dram", (2, H, S), _mybir.dt.float32, kind="Internal").ap())
    hybrid_layer(nc, *args)
    r = _run(nc, [arrays], core_ids=[0])
    return r.results[0]["out_dram"]
```

```python
from contextlib import ExitStack

import concourse.bass as bass
from concourse import mybir

ALU = mybir.AluOpType
ACT = mybir.ActivationFunctionType
AX_X = mybir.AxisListType.X
F32 = mybir.dt.float32
F32R = mybir.dt.float32r
BF16 = mybir.dt.bfloat16

P = 128
S = 1024
D = 1024
KT = D // P
NT = S // P
HALF = 512
NM = 256
H = 4
DH = 128
DA = 64
CW = 4
VW = DH + 1
EPS = 1e-6
NEG = -1e30

C_QM, C_KM, C_VM, C_OM, C_ZM, C_IF = 0, 512, 1024, 1536, 2048, 2560
C_QS, C_KS, C_VS, C_ZS, C_QC, C_ZC = 2568, 2824, 3080, 3336, 3592, 3848

PT_CW, PT_CB, PT_GPRE, PT_GMEM, PT_GM, PT_GS, PT_GC, N_PT = 0, 32, 40, 48, 56, 60, 62, 64

T_KS, T_VS, T_ZS, T_SB, T_CONV, T_VM, T_OUT, T_END = 4, 8, 10, 12, 24, 32, 36, 44
G_KS, G_VS, G_ZS, G_SB, G_CONV, G_VM, G_END = 4, 12, 20, 24, 48, 64, 80

CR = 4
PARTS = 4
ROUNDS = NT // 2


def after(reg, k):
    return reg + (k + 1 + CR)


def sb_order():
    todo = [("proj", group, part) for group in range(12) for part in range(PARTS)]
    slots = 1 + 16 + sum(1 if j // 2 < 4 else 2 for j in range(16))
    spare = len(todo) - slots
    out = []
    for j in range(17):
        if j < 16:
            out.append(("scores", j, 0))
        out.append(todo.pop(0))
        if 3 <= j < 3 + spare:
            out.append(todo.pop(0))
        if j:
            for seg in range(1 if (j - 1) // 2 < 4 else 2):
                out.append(("turn", j - 1, seg))
                out.append(todo.pop(0))
                out.append(("values", j - 1, seg))
    assert not todo
    return out


def hybrid_layer(nc, x, mem, g_pre, w_in, conv_w, conv_b, i_bias, f_bias, g_mlstm_head, g_sb_head,
                 g_mem_head, g_mem, w_mem_kv, w_out, g_post, out, rows_dram):
    order = sb_order()
    seg_index = {}
    for what, j, seg in order:
        if what == "turn":
            seg_index[(j, seg)] = len(seg_index)
    NSEG = len(seg_index)
    assert NSEG % 2 == 0

    with ExitStack() as ctx:
        def sem(name):
            return ctx.enter_context(nc.semaphore(name))

        at = {"next": -(-nc.sbuf_base // 64) * 64}
        size = {F32: 4, F32R: 4, BF16: 2}

        def region(nbytes):
            base = at["next"]
            at["next"] = base + -(-nbytes // 64) * 64
            assert at["next"] <= nc.sbuf_top
            return {"at": base, "end": at["next"]}

        def place(reg, name, shape, dt=F32):
            n = size[dt]
            for d in shape[1:]:
                n *= d
            t = nc.alloc_sbuf_tensor_at(name, shape, dt, offset=reg["at"])
            reg["at"] += -(-n // 64) * 64
            assert reg["at"] <= reg["end"], name
            return t

        def again(reg, back):
            return {"at": back, "end": reg["end"]}

        r_ht = region(2 * KT * S * 4)
        r_yg = region(KT * S * 4)
        r_qk = region(KT * S * 4)
        r_vm = region(NT * H * VW * 4)
        r_w = region(3 * KT * 264 * 4)
        r_qc = region((2 * S + 2 * NM + 2 * H * DA) * 4)
        r_os = region(NT * H * DA * 4)
        r_wk = region(14 * 1024)
        r_c = {"at": at["next"], "end": nc.sbuf_top}
        b_yg, b_qk, b_vm, b_w, b_qc, b_os, b_wk = (r["at"] for r in (r_yg, r_qk, r_vm, r_w, r_qc, r_os, r_wk))

        ht_hi = place(r_ht, "ht_hi", [P, KT, S], F32R)
        ht_lo = place(r_ht, "ht_lo", [P, KT, S], F32R)
        yg = place(r_yg, "yg", [P, KT, S])
        xr = place(again(r_yg, b_yg), "xr", [P, NT, D])
        qkm = place(r_qk, "qkm", [P, KT, S])
        q = again(r_qk, b_qk)
        mt_hi = place(q, "mt_hi", [P, KT, NM], F32R)
        mt_lo = place(q, "mt_lo", [P, KT, NM], F32R)
        q = again(r_qk, b_qk)
        qk_s = place(q, "qk_s", [P, 4 * S])
        v_s = place(q, "v_s", [P, NT, H * DA])
        row_iw = place(q, "row_iw", [H, NT, P])
        q = again(r_qk, b_qk)
        xt = place(q, "xt", [P, 2, D])
        ot = place(q, "ot", [P, 2, D])
        gpost = place(q, "gpost", [P, D])
        sq_out = place(q, "sq_out", [P, D])
        vm = place(r_vm, "vm", [P, NT * H * VW])
        vm4 = vm[:, :].rearrange("p (c h e) -> p c h e", c=NT, h=H)
        q = again(r_vm, b_vm)
        mraw = place(q, "mraw", [P, 2, D])
        q = again(r_vm, b_vm)
        row_a = place(q, "row_a", [H, NT, P])
        row_m = place(q, "row_m", [H, NT, P])
        row_b = place(q, "row_b", [H, NT, P])
        row_d = place(q, "row_d", [H, NT, P])
        q = again(r_vm, b_vm)
        beta = place(q, "beta", [P, 2, S])
        keep = place(q, "keep", [P, 2, S])
        q = again(r_vm, b_vm)
        cb = place(q, "cb", [P, 2, S + 3])
        sg = place(q, "sg", [P, 2, S])
        wraw = place(r_w, "wraw", [P, KT, 264])
        whi = place(r_w, "whi", [P, KT, 264], F32R)
        wlo = place(r_w, "wlo", [P, KT, 264], F32R)
        q_c = place(r_qc, "q_c", [P, 2, S])
        k_c = place(r_qc, "k_c", [P, 2, NM])
        v_c = place(r_qc, "v_c", [P, 2, H * DA])
        os_ = place(r_os, "os", [P, NT, H, DA])
        q = again(r_wk, b_wk)
        at_ = place(q, "at", [P, 2, HALF])
        ts = place(q, "ts", [P, 2, HALF])
        sq_in = place(again(r_wk, b_wk + 4096), "sq_in", [P, D])
        qz = place(q, "qz", [P, 2, 2, P])
        q = again(r_wk, b_wk)
        pc = place(q, "pc", [P, H, NM])
        pct = place(q, "pct", [P, 2 * HALF])
        sqc = place(q, "sqc", [P, 2 * H, DA])
        hnc = place(q, "hnc", [P, 2 * H, DA])
        qcz = place(q, "qcz", [P, H, P])
        q = again(r_wk, b_wk)
        dm = place(q, "dm", [P, 2, H, P])
        iwb = place(q, "iwb", [P, 2, H, P])
        sd = place(q, "sd", [P, 2, H, P])
        sqm = place(q, "sqm", [P, H, P])
        q = again(r_os, b_os)
        y_first = [place(q, name, [P, KT, P], F32R) for name in ("y_first_hi", "y_first_lo")]
        q = again(r_qc, b_qc)
        kst = place(q, "kst", [P, 2, H, P])
        qs2 = place(q, "qs2", [P, 2, H, P])
        q = {"at": b_w + KT * 264 * 4, "end": r_w["end"]}
        kw = place(q, "kw", [P, 2, H, P])
        ns = place(q, "ns", [P, 2, H, VW])
        cst = place(q, "cst", [P, H, VW])
        hnm = place(q, "hnm", [P, 2, H, P])
        ident = place(r_c, "ident", [P, P])
        identb = place(r_c, "identb", [P, P], BF16)
        maskb = place(r_c, "maskb", [P, P], BF16)
        maskd = place(r_c, "maskd", [P, P])
        prow = place(r_c, "prow", [N_PT, P])
        pt = place(r_c, "pt", [P, N_PT])
        ifb = place(r_c, "ifb", [H, 2])
        gt = place(r_c, "gt", [P, NT, 2 * H])
        ks = place(r_c, "ks", [P, 2 * H])
        ones = place(r_c, "ones", [P, 1, 1])
        own = place(r_c, "own", [P, 2])
        epsc = place(r_c, "epsc", [P, 1])
        onec = place(r_c, "onec", [P, 1])
        ssx = place(r_c, "ssx", [P, 10])
        rsx = place(r_c, "rsx", [P, 10])
        bl_ = place(r_c, "bl", [H, NT])
        mp = place(r_c, "mp", [H, NT])
        ml = place(r_c, "ml", [H, NT])
        dec = place(r_c, "dec", [P, H, NT])
        cols = place(r_c, "cols", [P, 3, NT * H])
        mx = place(r_c, "mx", [P, H])
        nmx = place(r_c, "nmx", [P, H])
        sums = place(r_c, "sums", [P, H])
        r8 = place(r_c, "r8", [P, 2 * H])
        ss8 = place(r_c, "ss8", [P, 2 * H])
        u8 = place(r_c, "u8", [P, 2 * H])
        l8 = place(r_c, "l8", [P, 2 * H])
        cf8 = place(r_c, "cf8", [P, 2 * H])
        den = place(r_c, "den", [P, H])
        r4 = place(r_c, "r4", [P, H])
        ss4 = place(r_c, "ss4", [P, H])
        u4 = place(r_c, "u4", [P, H])
        l4 = place(r_c, "l4", [P, H])
        cf4 = place(r_c, "cf4", [P, H])
        sso = place(r_c, "sso", [P, 2])
        rso = place(r_c, "rso", [P, 2])

        ps = ctx.enter_context(nc.psum_tensor("ps", [P, 8 * HALF], F32))

        def bank(b, n=HALF, off=0, parts=P):
            return ps[0:parts, b * HALF + off:b * HALF + off + n]

        s_par = sem("s_par")
        s_mem = sem("s_mem")
        s_x = [sem(f"s_x{i}") for i in range(4)]
        s_raw = [sem("s_raw0"), sem("s_raw1")]
        s_gw = sem("s_gw")
        w_hi, w_lo = sem("w_hi"), sem("w_lo")
        gw_hi, gw_lo = sem("gw_hi"), sem("gw_lo")
        c_ready = sem("c_ready")
        pt_done, pt_ready = sem("pt_done"), sem("pt_ready")
        rs_ready = sem("rs_ready")
        xn_ready = sem("xn_ready")
        tr_done = sem("tr_done")
        hi_done, lo_done = sem("hi_done"), sem("lo_done")
        pj_done = sem("pj_done")
        pj_free = [sem("pj_free0"), sem("pj_free1")]
        gt_ready = sem("gt_ready")
        rt_done = sem("rt_done")
        row_act, row_dve = sem("row_act"), sem("row_dve")
        ct_done, ct_free = sem("ct_done"), sem("ct_free")
        s_rows = sem("s_rows")
        s_dec = sem("s_dec")
        zs_sig, zs_gate = sem("zs_sig"), sem("zs_gate")
        q_staged, z_ready, sg_ready = sem("q_staged"), sem("z_ready"), sem("sg_ready")
        kp_ready = sem("kp_ready")
        a_ready, t_ready, t_ev = sem("a_ready"), sem("t_ready"), sem("t_ev")
        av_done, o_ready, o_ev = sem("av_done"), sem("o_ready"), sem("o_ev")
        gs_ready, ts_free = sem("gs_ready"), sem("ts_free")
        cv_first, cv_sum, cv_sig, cv_out = sem("cv_first"), sem("cv_sum"), sem("cv_sig"), sem("cv_out")
        qc_staged, sc_done, mx_ready, p_ready = sem("qc_staged"), sem("sc_done"), sem("mx_ready"), sem("p_ready")
        pt2_done, pa_ev, pd_ev, oc_done = sem("pt2_done"), sem("pa_ev"), sem("pd_ev"), sem("oc_done")
        sqc_ready, ssc_ready, rsc_ready, hn_ready = sem("sqc_ready"), sem("ssc_ready"), sem("rsc_ready"), sem("hn_ready")
        yt_done, y_done = sem("yt_done"), sem("y_done")
        s_nm = [sem("s_nm0"), sem("s_nm1")]
        s_iw = [sem("s_iw0"), sem("s_iw1")]
        nm_masked, k_staged, q_scaled = sem("nm_masked"), sem("k_staged"), sem("q_scaled")
        d_ready, st_done, kt_done = sem("d_ready"), sem("st_done"), sem("kt_done")
        sd_ready, kw_ready, n_done, kv_done = sem("sd_ready"), sem("kw_ready"), sem("n_done"), sem("kv_done")
        c_upd, ns_ready, sqm_ready, ssm_ready = sem("c_upd"), sem("ns_ready"), sem("sqm_ready"), sem("ssm_ready")
        rsm_ready, hnm_ready, ym_done, ygm_done = sem("rsm_ready"), sem("hnm_ready"), sem("ym_done"), sem("ygm_done")
        y_hi, y_lo, yo_done = sem("y_hi"), sem("y_lo"), sem("yo_done")
        s_xt = [sem("s_xt0"), sem("s_xt1")]
        s_gp = sem("s_gp")
        rso_ready, on_ready, ot_ready = sem("rso_ready"), sem("on_ready"), sem("ot_ready")
        s_out = [sem("s_out0"), sem("s_out1")]
        self_act, self_dve, self_pool = sem("self_act"), sem("self_dve"), sem("self_pool")

        vm_ones = sem("vm_ones")
        cb_zero, cst_zero, waited = sem("cb_zero"), sem("cst_zero"), sem("waited")
        starts_at_cr = {
            "pe": (z_ready, t_ready, av_done, sc_done, pt2_done, oc_done, yt_done, st_done, kt_done, n_done,
                   kv_done, ym_done, yo_done),
            "act": (sg_ready, kp_ready, gs_ready, p_ready, pa_ev, sqc_ready, rsc_ready, d_ready, kw_ready, ns_ready,
                    sqm_ready, rsm_ready, y_hi, rso_ready, cv_first, cv_sig),
            "dve": (a_ready, t_ev, o_ev, ts_free, cv_sum, cv_out, mx_ready, pd_ev, ssc_ready, hn_ready, y_done,
                    sd_ready, c_upd, ssm_ready, hnm_ready, ygm_done, y_lo, on_ready),
            "pool": (q_staged, qc_staged, nm_masked, k_staged, q_scaled, ot_ready),
        }

        def start(eng, name):
            for s_ in starts_at_cr[name]:
                eng.sem_inc(s_, CR)

        class Chain:

            def __init__(self, eng, s):
                self.eng, self.s, self.n, self.it, self.per, self.base = eng, s, 0, None, 0, 0

            def __call__(self, ins):
                ins.then_inc(self.s, 1)
                self.n += 1
                self.eng.wait_ge(self.s, self.n if self.it is None else self.it * self.per + self.n)

            def loop(self, it, per, first=0):
                self.n -= first * per
                self.it, self.per, self.base = it, per, self.n

            def end(self, end):
                assert self.n - self.base == self.per
                self.n, self.it = self.base + self.per * end, None

        block = ctx.enter_context(nc.Block())

        @block.sync
        def _(sp):
            w_in3 = w_in.rearrange("(k p) n -> p k n", p=P)
            w_mem3 = w_mem_kv.rearrange("(k p) n -> p k n", p=P)
            w_out3 = w_out.rearrange("(k p) n -> p k n", p=P)
            x3 = x[0].rearrange("(t p) d -> p t d", p=P)

            def raw(n, slot, src):
                sp.wait_ge(w_hi, n - 1)
                sp.wait_ge(w_lo, n - 1)
                sp.dma_start(wraw[:, :, P * slot:P * slot + P], src).then_inc(s_raw[slot], 16)

            sp.dma_start(mraw[:, :, :], mem[0].rearrange("(t p) d -> p t d", p=P)).then_inc(s_mem, 16)
            row = 0
            for src, n in ((conv_w.rearrange("j (c p) -> (j c) p", p=P), CW * KT), (conv_b, KT), (g_pre, KT),
                           (g_mem, KT), (g_mlstm_head, 4), (g_sb_head, 2), (g_mem_head, 2)):
                if n != CW * KT:
                    src = src.rearrange("(c p) -> c p", p=P)
                sp.dma_start(prow[row:row + n, :], src).then_inc(s_par, 16)
                row += n
            for i, src in enumerate((i_bias, f_bias)):
                sp.dma_start(ifb[:, i:i + 1], src.rearrange("(h o) -> h o", o=1)).then_inc(s_par, 16)
            for n in range(2):
                sp.dma_start(wraw[:, :, P * n:P * n + P], w_mem3[:, :, P * n:P * n + P]).then_inc(s_raw[n], 16)
            for i in range(4):
                sp.dma_start(xr[:, 2 * i:2 * i + 2, :], x3[:, 2 * i:2 * i + 2, :]).then_inc(s_x[i], 16)
            sp.dma_start(wraw[:, :, 256:264], w_in3[:, :, C_IF:C_IF + 8]).then_inc(s_gw, 16)
            for n in range(2, 4):
                raw(n, n % 2, w_mem3[:, :, P * n:P * n + P])
            for n in range(T_KS, T_SB):
                raw(n, n % 2, w_in3[:, :, C_QS + P * (n - T_KS):C_QS + P * (n - T_KS + 1)])
            with sp.Fori(0, 2) as hp:
                for j in range(6):
                    col = [C_OM + hp * 256, C_OM + hp * 256 + P, C_ZM + hp * 256, C_ZM + hp * 256 + P,
                           C_ZC + hp * P, C_QC + hp * P][j]
                    raw(T_SB + hp * 6 + j, j % 2, w_in3[:, :, bass.ds(col, P)])
            with sp.Fori(0, 4) as it:
                for a in range(2):
                    raw(T_CONV + it * 2 + a, a, w_in3[:, :, bass.ds(it * 256 + a * P, P)])
            with sp.Fori(0, 2) as u:
                for a in range(2):
                    raw(T_VM + u * 2 + a, a, w_in3[:, :, bass.ds(u * 256 + (C_VM + a * P), P)])
            sp.wait_ge(w_lo, T_OUT)
            for a in range(2):
                raw(T_OUT + a, a, w_out3[:, :, P * a:P * a + P])
            sp.wait_ge(pt2_done, after(0, NT - 1))

            def old_state_rows(c0, a):
                sp.wait_ge(sd_ready, after(c0, a - 2))
                sp.dma_start(dm[:, a % 2, :, :], bass.AP(rows_dram.tensor, c0 * P + a * P, [[0, P], [S, H], [1, P]])
                             ).then_inc(s_nm[a % 2], 16)
                sp.wait_ge(q_scaled, after(c0, a - 2))
                if isinstance(c0, int) and c0 == a == 0:
                    sp.wait_ge(oc_done, after(0, NT - 1))
                sp.dma_start(iwb[:, a % 2, :, :],
                             bass.AP(rows_dram.tensor, c0 * P + (a * P + H * S), [[0, P], [S, H], [1, P]])
                             ).then_inc(s_iw[a % 2], 16)

            for a in range(3):
                old_state_rows(0, a)
            with sp.Fori(1, ROUNDS - 1) as it:
                for a in range(2):
                    old_state_rows(it * 2, a + 1)
                    raw(T_OUT + it * 2 + a, a, w_out3[:, :, bass.ds(it * 256 + a * P, P)])
            old_state_rows(NT - 2, 1)
            for a in range(2):
                raw(T_OUT + NT - 2 + a, a, w_out3[:, :, D - 256 + P * a:D - 256 + P * a + P])
            sp.wait_ge(st_done, after(0, NT - 1))
            sp.wait_ge(k_staged, after(0, NT - 1))
            sp.wait_ge(q_scaled, after(0, NT - 1))
            for a in range(2):
                sp.sem_inc(s_out[a], 16)
            sp.dma_start(gpost[:, :], bass.AP(g_post.tensor, 0, [[0, P], [1, D]])).then_inc(s_gp, 16)
            with sp.Fori(0, ROUNDS) as it:
                for a in range(2):
                    sp.wait_ge(ot_ready, after(it * 2, a - 2))
                    sp.dma_start(xt[:, a, :], x[0][bass.ds(it * 256 + a * P, P), :]).then_inc(s_xt[a], 16)
                for a in range(2):
                    sp.wait_ge(ot_ready, after(it * 2, a))
                    sp.dma_start(out[0][bass.ds(it * 256 + a * P, P), :], ot[:, a, :]).then_inc(s_out[a], 16)
            for a in range(2):
                sp.wait_ge(s_out[a], 16 * (ROUNDS + 1))

        @block.gpsimd
        def _(pool):
            start(pool, "pool")
            chain = Chain(pool, self_pool)
            pool.memset(identb[:, :], 0.0)
            pool.memset(ident[:, :], 0.0)
            pool.memset(maskb[:, :], 0.0)
            pool.memset(maskd[:, :], 0.0)
            pool.memset(ones[:, :, :], 1.0)
            pool.memset(epsc[:, :], EPS)
            pool.memset(onec[:, :], 1.0)
            chain(pool.memset(own[:, :], 0.0))
            for hh in range(2):
                chain(pool.memset(own[DA * hh:DA * hh + DA, hh:hh + 1], 1.0))
            pool.memset(ks[:, 0:H], 1.0)
            chain(pool.memset(ks[:, H:2 * H], DH ** -0.5))
            for m in (ident, identb):
                pool.affine_select(out=m[:, :], in_=m[:, :], compare_op=ALU.not_equal, fill=1.0, base=0,
                                   pattern=[[-1, P]], channel_multiplier=1)
            pool.affine_select(out=maskb[:, :], in_=maskb[:, :], compare_op=ALU.is_gt, fill=NEG, base=0,
                               pattern=[[-1, P]], channel_multiplier=1)
            pool.affine_select(out=maskd[:, :], in_=maskd[:, :], compare_op=ALU.is_ge, fill=NEG, base=0,
                               pattern=[[1, P]], channel_multiplier=-1).then_inc(c_ready, 1)

            def low(n, slot, dst=None, col=None):
                pool.wait_ge(w_hi, n + 1)
                raw = wraw[:, :, P * slot:P * slot + P]
                if dst is None:
                    hi, lo = whi[:, :, P * slot:P * slot + P], wlo[:, :, P * slot:P * slot + P]
                else:
                    hi, lo = ht_hi[:, :, col], ht_lo[:, :, col]
                pool.tensor_tensor(lo, raw, hi.bitcast(F32), ALU.subtract).then_inc(w_lo, 1)

            for n in range(T_VS):
                low(n, n % 2)
            pool.wait_ge(gw_hi, 1)
            pool.tensor_tensor(wlo[:, :, 256:264], wraw[:, :, 256:264], whi[:, :, 256:264].bitcast(F32),
                               ALU.subtract).then_inc(gw_lo, 1)
            for n in range(T_VS, T_SB):
                low(n, n % 2)
            pool.wait_ge(lo_done, 24)
            for half in range(2):
                pool.wait_ge(pj_free[half], G_VS // 2)
            with pool.Fori(0, 2) as hp:
                for what, j, part in order:
                    if what == "scores" and j % 2 == 0:
                        i = j // 2
                        pool.wait_ge(z_ready, after(hp * 16, 2 * i - 3))
                        pool.tensor_tensor(qz[:, i % 2, :, :],
                                           qk_s[:, bass.ds(hp * S + i * P, P)].unsqueeze(1).broadcast_to([P, 2, P]),
                                           own[:, :].unsqueeze(2).broadcast_to([P, 2, P]), ALU.mult).then_inc(q_staged, 1)
                    if what == "proj" and j % 2 == 1 and part == PARTS - 1:
                        low(T_SB + hp * 6 + j // 2, (j // 2) % 2)
            with pool.Fori(0, 4) as it:
                for a in range(2):
                    low(T_CONV + it * 2 + a, a)
            pool.wait_ge(pj_free[0], G_CONV // 2)
            pool.wait_ge(pj_free[1], G_CONV // 2)
            pool.wait_ge(av_done, after(0, 2 * NSEG - 1))
            chain(pool.memset(r8[:, :], 1.0))
            for a in range(2):
                low(T_VM + a, a)
            for b in range(NT):
                pool.wait_ge(sc_done, after(0, b - 1))
                for m in range(2):
                    c = pool.tensor_tensor(qcz[:, 2 * m:2 * m + 2, :],
                                           q_c[:, m, P * b:P * b + P].unsqueeze(1).broadcast_to([P, 2, P]),
                                           own[:, :].unsqueeze(2).broadcast_to([P, 2, P]), ALU.mult)
                c.then_inc(qc_staged, 1)
                if b == 0:
                    pool.wait_ge(cv_out, after(0, 7))
                    pool.memset(vm4[:, :, :, DH:VW], 1.0).then_inc(vm_ones, 1)
                if b == NT // 2:
                    for a in range(2):
                        low(T_VM + 2 + a, a)

            def stage(c0, a):
                b = a % 2
                tok = bass.ds(c0 * P + a * P, P)
                pool.wait_ge(kt_done, after(c0, a - 2))
                pool.tensor_tensor(kst[:, b, :, :], qkm[:, H:2 * H, tok],
                                   ones[:, :, :].broadcast_to([P, H, P]), ALU.mult).then_inc(k_staged, 1)
                pool.wait_ge(s_nm[b], c0 * 8 + 16 * (a // 2 + 1))
                pool.tensor_tensor(dm[:, b, :, :], dm[:, b, :, :],
                                   maskd[:, :].unsqueeze(1).broadcast_to([P, H, P]), ALU.add).then_inc(nm_masked, 1)
                pool.wait_ge(s_iw[b], c0 * 8 + 16 * (a // 2 + 1))
                pool.wait_ge(n_done, after(c0, a - 2))
                pool.tensor_tensor(qs2[:, b, :, :], qkm[:, 0:H, tok], iwb[:, b, :, :], ALU.mult).then_inc(q_scaled, 1)

            def low_out(c0, a):
                low(T_OUT + c0 + a, a % 2, True, bass.ds(c0 * P + a * P, P))

            stage(0, 0)
            stage(0, 1)
            with pool.Fori(0, ROUNDS - 1) as it:
                for a in range(2):
                    stage(it * 2, a + 2)
                    low_out(it * 2, a)
            low_out(NT - 2, 0)
            low_out(NT - 2, 1)
            with pool.Fori(0, ROUNDS) as it:
                for a in range(2):
                    pool.wait_ge(on_ready, after(it * 2, a))
                    pool.wait_ge(s_xt[a], it * 16 + 16)
                    pool.tensor_tensor(ot[:, a, :], ot[:, a, :], xt[:, a, :], ALU.add).then_inc(ot_ready, 1)

        @block.tensor
        def _(pe):
            LOW = 2 * KT
            WEIGHTS_STAY = [(0, i, k) for k in range(KT) for i in range(2)] + [(1, 0, k) for k in range(KT)]
            WEIGHTS_MOVE = [(i, 0, k) for k in range(KT) for i in range(2)] + [(0, 1, k) for k in range(KT)]

            def product(dst, stat, move, passes, lo, first=0, end=3 * KT, before=None):
                for n in range(first, end):
                    i, j, k = passes[n]
                    if n == LOW and lo is not None:
                        pe.wait_ge(w_lo, lo)
                    if before is not None and n % 2 == 0 and n < LOW:
                        before(k)
                    last = pe.matmul(dst, stat(i, k), move(j, k), start=(n == 0), stop=(n == 3 * KT - 1))
                return last

            start(pe, "pe")
            htp, wp, mtp = (ht_hi, ht_lo), (whi, wlo), (mt_hi, mt_lo)

            def feature_group(slot, half, lo, part=None, b=None, before=None):
                size = 3 * KT // PARTS
                first, end = (0, 3 * KT) if part is None else (size * part, size * (part + 1))
                return product(bank(half if b is None else b), lambda i, k: wp[i][:, k, P * slot:P * slot + P],
                               lambda j, k: htp[j][:, k, half * HALF:half * HALF + HALF],
                               WEIGHTS_STAY, lo, first, end, before)

            def token_group(tt, b, n, lo, src=htp):
                return product(bank(b, n), lambda i, k: src[i][:, k, P * tt:P * tt + P],
                               lambda j, k: wp[j][:, k, 0:n], WEIGHTS_MOVE, lo)

            pe.wait_ge(c_ready, 1)
            pe.wait_ge(s_par, 16 * 9)
            pe.transpose(bank(7, N_PT), prow[:, :], ident[0:N_PT, 0:N_PT]).then_inc(pt_done, 1)
            pe.wait_ge(pt_ready, 1)

            def turn_group(n, tiles, src, k):
                if n >= 6:
                    pe.wait_ge(lo_done, n - 5)
                b = 2 + n % 6
                for i, t in enumerate(tiles):
                    last = pe.transpose(bank(b, P, P * i), src[:, t, P * k:P * k + P], ident[:, :])
                last.then_inc(tr_done, 1)

            pe.wait_ge(xn_ready, 2)
            for k in range(KT):
                turn_group(k, (0, 1), mraw, k)
            pe.wait_ge(lo_done, 8)
            for n in range(2):
                pe.wait_ge(w_hi, n + 1)
                product(bank(n, NM), lambda i, k: wp[i][:, k, P * n:P * n + P], lambda j, k: mtp[j][:, k, :],
                        WEIGHTS_STAY, n + 1).then_inc(pj_done, 1)

            def turn_half(h2):
                for k in range(KT):
                    turn_group(8 + 8 * h2 + k, range(4 * h2, 4 * h2 + 4), xr, k)

            pe.wait_ge(xn_ready, 6)
            turn_half(0)
            pe.wait_ge(w_hi, 4)
            for n in range(2):
                pe.wait_ge(pj_free[n], 1)
                token_group(n, n, NM, 4, mtp).then_inc(pj_done, 1)
            for g in range(4):
                half, a = g // 2, g % 2
                if half == 0:
                    pe.wait_ge(w_hi, T_KS + a + 1)
                pe.wait_ge(pj_free[a], G_KS // 2 + half)
                feature_group(a, half, T_KS + a + 1 if half == 0 else None, b=a,
                              before=(lambda k: pe.wait_ge(lo_done, 8 + 8 * half + k + 1)) if a == 0 else None
                              ).then_inc(pj_done, 1)
                if g == 0:
                    pe.wait_ge(xn_ready, 10)
                    turn_half(1)
            for a in range(2):
                pe.wait_ge(w_hi, T_KS + 2 + a + 1)
                for half in range(2):
                    pe.wait_ge(pj_free[half], G_KS // 2 + 2 + a)
                    feature_group(a, half, T_KS + 2 + a + 1).then_inc(pj_done, 1)
            pe.wait_ge(w_hi, T_ZS)
            pe.wait_ge(gw_lo, 1)
            for tt in range(NT):
                pe.wait_ge(pj_free[tt % 2], G_VS // 2 + tt // 2)
                token_group(tt, tt % 2, 264, T_ZS).then_inc(pj_done, 1)
            pe.wait_ge(gt_ready, NT)
            for g in range(2):
                for tt in range(NT):
                    last = pe.transpose(bank(2 + 2 * g + tt // 4, P, P * (tt % 4), H),
                                        gt[:, tt, H * g:H * g + H], ident[:, :])
            last.then_inc(rt_done, 1)
            for a in range(2):
                pe.wait_ge(w_hi, T_ZS + a + 1)
                for half in range(2):
                    pe.wait_ge(pj_free[half], G_ZS // 2 + a)
                    feature_group(a, half, T_ZS + a + 1).then_inc(pj_done, 1)
            pe.wait_ge(row_dve, 15)
            for r, row in enumerate((row_a, row_d, row_b)):
                for c in range(NT):
                    last = pe.transpose(bank(6, H, (r * NT + c) * H), row[:, c, :], ident[0:H, 0:H])
            last.then_inc(ct_done, 1)

            pe.wait_ge(ct_free, 1)
            with pe.Fori(0, 2) as hp:
                for what, j, part in order:
                    if what == "proj":
                        tile, half = j // 2, j % 2
                        if part == 0:
                            if half == 0:
                                pe.wait_ge(w_hi, hp * 6 + (T_SB + tile + 1))
                            pe.wait_ge(pj_free[half], hp * 6 + (G_SB // 2 + tile))
                        last = feature_group(tile % 2, half, hp * 6 + (T_SB + tile + 1), part)
                        if part == PARTS - 1:
                            last.then_inc(pj_done, 1)
                        continue
                    i, hh = j // 2, j % 2
                    if what == "scores":
                        n = P * (i + 1)
                        pe.wait_ge(q_staged, after(hp * 8, i))
                        pe.wait_ge(sg_ready, after(hp * 16, j - 2))
                        for lo in range(0, n, HALF):
                            w = min(HALF, n - lo)
                            pe.matmul(bank(2 + 2 * hh + lo // HALF, w), qz[:, i % 2, hh, :],
                                      qk_s[:, bass.ds(hp * S + (2 * S + lo), w)], start=True, stop=(lo + w < n))
                        pe.matmul(bank(2 + 2 * hh + i // 4, P, P * (i % 4)), identb[:, :], maskb[:, :],
                                  start=False, stop=True).then_inc(z_ready, 1)
                    elif what == "turn":
                        g = seg_index[(j, part)]
                        pe.wait_ge(a_ready, after(hp * 16, j))
                        pe.wait_ge(t_ev, after(hp * NSEG, g - 1))
                        for s_ in range(4 * part, min(4 * part + 4, i + 1)):
                            last = pe.transpose(bank(6, P, P * (s_ % 4)), beta[:, hh, P * s_:P * s_ + P], ident[:, :])
                        last.then_inc(t_ready, 1)
                    else:
                        g = seg_index[(j, part)]
                        pe.wait_ge(t_ev, after(hp * NSEG, g))
                        if part == 0:
                            pe.wait_ge(o_ev, after(hp * 16, j - 1))
                        for s_ in range(4 * part, min(4 * part + 4, i + 1)):
                            vs = v_s[:, s_, :]
                            last = pe.matmul(bank(7, DA), at_[:, g % 2, P * (s_ % 4):P * (s_ % 4) + P],
                                             vs[:, bass.ds(hp * P + hh * DA, DA)], start=(s_ == 0), stop=(s_ == i))
                        last.then_inc(av_done, 1)
            with pe.Fori(0, 4) as it:
                for a in range(2):
                    pe.wait_ge(w_hi, it * 2 + (T_CONV + a + 1))
                    for half in range(2):
                        pe.wait_ge(pj_free[half], it * 2 + (G_CONV // 2 + a))
                        feature_group(a, half, it * 2 + (T_CONV + a + 1)).then_inc(pj_done, 1)
            def v_group(n):
                if n % NT == 0:
                    pe.wait_ge(w_hi, T_VM + 2 * (n // NT) + 2)
                pe.wait_ge(pj_free[n % 2], G_VM // 2 + n // 2)
                token_group(n % NT, n % 2, 256, T_VM + 2 * (n // NT) + 2).then_inc(pj_done, 1)

            def turn_out(b):
                pe.wait_ge(hn_ready, after(0, b))
                pe.wait_ge(y_done, after(0, b - 1))
                for m in range(4):
                    last = pe.transpose(bank(7, P, P * m), hnc[:, 2 * m:2 * m + 2, :].rearrange("p a b -> p (a b)"),
                                        ident[:, :])
                last.then_inc(yt_done, 1)

            def scores(b):
                pe.wait_ge(qc_staged, after(0, b))
                pe.wait_ge(p_ready, after(0, b - 1))
                for h in range(H):
                    last = pe.matmul(bank(2 + h // 2, NM, NM * (h % 2)), qcz[:, h, :], k_c[:, h // 2, :],
                                     start=True, stop=True)
                last.then_inc(sc_done, 1)

            scores(0)
            for b in range(NT):
                v_group(2 * b)
                if b:
                    turn_out(b - 1)
                pe.wait_ge(p_ready, after(0, b))
                pe.wait_ge(pa_ev, after(0, b - 1))
                pe.wait_ge(pd_ev, after(0, b - 1))
                for m in range(2 * H):
                    last = pe.transpose(bank(4 + m // 4, P, P * (m % 4)), pc[:, m // 2, P * (m % 2):P * (m % 2) + P],
                                        ident[:, :])
                last.then_inc(pt2_done, 1)
                if b < NT - 1:
                    scores(b + 1)
                v_group(2 * b + 1)
                pe.wait_ge(pa_ev, after(0, b))
                pe.wait_ge(pd_ev, after(0, b))
                pe.wait_ge(hn_ready, after(0, b - 1))
                for h in range(H):
                    for m in range(2):
                        last = pe.matmul(bank(6, DA, DA * h), pct[:, P * (2 * h + m):P * (2 * h + m) + P],
                                         v_c[:, m, DA * h:DA * h + DA], start=(m == 0), stop=(m == 1))
                last.then_inc(oc_done, 1)
            for half in range(2):
                pe.wait_ge(pj_free[half], G_END // 2)

            def m_scores(c0, a):
                pe.wait_ge(k_staged, after(c0, a))
                pe.wait_ge(sd_ready, after(c0, a - 1))
                for h in range(H):
                    last = pe.matmul(bank(0, P, P * h), kst[:, a % 2, h, :], qkm[:, h, bass.ds(c0 * P + a * P, P)],
                                     start=True, stop=True)
                last.then_inc(st_done, 1)
                pe.wait_ge(kw_ready, after(c0, a - 1))
                for h in range(H):
                    last = pe.transpose(bank(1, P, P * h), kst[:, a % 2, h, :], ident[:, :])
                last.then_inc(kt_done, 1)

            def m_outputs(c0, a):
                pe.wait_ge(q_scaled, after(c0, a))
                pe.wait_ge(sd_ready, after(c0, a))
                pe.wait_ge(c_upd, after(c0, a - 1))
                pe.wait_ge(ns_ready, after(c0, a - 1))
                for h in range(H):
                    dst = bank(4 + h // 2, VW, VW * (h % 2))
                    pe.matmul(dst, qs2[:, a, h, :], cst[:, h, :], start=True, stop=False)
                    last = pe.matmul(dst, sd[:, a, h, :], vm[:, bass.ds(c0 * (H * VW) + (a * H + h) * VW, VW)],
                                     start=False, stop=True)
                last.then_inc(n_done, 1)
                pe.wait_ge(kw_ready, after(c0, a))
                for h in range(H):
                    last = pe.matmul(bank(6 + h // 2, VW, VW * (h % 2)), kw[:, a, h, :],
                                     vm[:, bass.ds(c0 * (H * VW) + (a * H + h) * VW, VW)], start=True, stop=True)
                last.then_inc(kv_done, 1)

            def m_turn(c0, a):
                b = a % 2
                pe.wait_ge(hnm_ready, after(c0, a))
                pe.wait_ge(ygm_done, after(c0, a - 2))
                for h in range(H):
                    last = pe.transpose(bank(2 + b, P, P * h), hnm[:, b, h, :], ident[:, :])
                last.then_inc(ym_done, 1)

            def chunk_round(c0, first=False, final=False):
                m_outputs(c0, 0)
                m_scores(c0, 1)
                if not first:
                    m_turn(c0, -1)
                m_outputs(c0, 1)
                if not final:
                    m_scores(c0, 2)
                m_turn(c0, 0)

            m_scores(0, 0)
            turn_out(NT - 1)
            pe.wait_ge(y_done, after(0, NT - 1))
            pe.wait_ge(cst_zero, 1)
            pe.wait_ge(vm_ones, 1)
            chunk_round(0, first=True)
            with pe.Fori(1, ROUNDS - 1) as it:
                chunk_round(it * 2)
            chunk_round(NT - 2, final=True)

            def output(reg, a, half):
                y = (y_first[0][:, :, :], y_first[1][:, :, :]) if a == 0 else (whi[:, :, P:2 * P], wlo[:, :, P:2 * P])
                return product(bank(2 * a + half), lambda i, k: y[i][:, k, :],
                               lambda j, k: htp[j][:, k, HALF * half:HALF * half + HALF], WEIGHTS_MOVE,
                               T_OUT + 4 * half + 4 if isinstance(reg, int) and reg == 0 else None)

            pe.wait_ge(y_lo, after(0, 0))
            pe.wait_ge(w_hi, T_OUT + 4)
            output(0, 0, 0)
            m_turn(NT - 2, 1)
            pe.wait_ge(w_hi, T_END)
            output(0, 0, 1).then_inc(yo_done, 1)
            pe.wait_ge(y_lo, after(0, 1))
            pe.wait_ge(ygm_done, after(0, NT - 1))
            output(0, 1, 0)
            output(0, 1, 1).then_inc(yo_done, 1)
            with pe.Fori(1, ROUNDS) as it:
                for a in range(2):
                    pe.wait_ge(y_lo, after(it * 2, a))
                    pe.wait_ge(on_ready, after(it * 2, a - 2))
                    output(it, a, 0)
                    output(it, a, 1).then_inc(yo_done, 1)

        @block.scalar
        def _(act):
            start(act, "act")
            chain = Chain(act, self_act)

            def func(dst, src, f, **kw):
                return act.activation(dst, src, f, **kw)

            act.preload_act_table_set("natural_log_exp_and_others")
            act.wait_ge(c_ready, 1)

            def high(n, slot, half_n, freed, col=None):
                act.wait_ge(s_raw[slot], half_n * 16 + 16)
                act.wait_ge(pj_done, freed)
                dst = whi[:, :, P * slot:P * slot + P] if col is None else ht_hi[:, :, col]
                func(dst, wraw[:, :, P * slot:P * slot + P], ACT.Copy).then_inc(w_hi, 1)

            def rms(tiles, src, at0):
                for i, t in enumerate(tiles):
                    chain(func(sq_in[:, :], src[:, t, :], ACT.Square, accum_out=ssx[:, at0 + i:at0 + i + 1]))
                chain(func(ssx[:, at0:at0 + 2], ssx[:, at0:at0 + 2], ACT.Ln, bias=epsc[:, :], scale=1.0 / D))
                func(rsx[:, at0:at0 + 2], ssx[:, at0:at0 + 2], ACT.Exp, scale=-0.5).then_inc(rs_ready, 1)

            act.wait_ge(s_mem, 16)
            rms((0, 1), mraw, 8)
            for n in range(2):
                act.wait_ge(s_raw[n], 16)
                func(whi[:, :, P * n:P * n + P], wraw[:, :, P * n:P * n + P], ACT.Copy).then_inc(w_hi, 1)
            act.wait_ge(pt_done, 1)
            func(pt[:, :], bank(7, N_PT), ACT.Copy).then_inc(pt_ready, 1)

            def split_high(n, dst, width, g):
                act.wait_ge(tr_done, n + 1)
                func(dst, bank(2 + n % 6, width), ACT.Copy, scale=g).then_inc(hi_done, 1)

            act.wait_ge(pt_ready, 1)
            for k in range(KT):
                split_high(k, mt_hi[:, k, :], NM, pt[:, PT_GMEM + k:PT_GMEM + k + 1])

            def x_rms(i):
                act.wait_ge(s_x[i], 16)
                rms((2 * i, 2 * i + 1), xr, 2 * i)

            def x_high(h2):
                for k in range(KT):
                    split_high(8 + 8 * h2 + k, ht_hi[:, k, HALF * h2:HALF * h2 + HALF], HALF,
                               pt[:, PT_GPRE + k:PT_GPRE + k + 1])

            x_rms(0)
            x_rms(1)
            high(2, 0, 1, 1)
            high(3, 1, 1, 2)
            x_high(0)
            x_rms(2)
            x_rms(3)
            act.wait_ge(s_gw, 16)
            func(whi[:, :, 256:264], wraw[:, :, 256:264], ACT.Copy).then_inc(gw_hi, 1)
            high(4, 0, 2, 4)
            high(5, 1, 2, 4)

            def sb_copy(g, tile, half, b):
                act.wait_ge(pj_done, g + 1)
                func(qk_s[:, tile * S + half * HALF:tile * S + half * HALF + HALF], bank(b), ACT.Copy
                     ).then_inc(pj_free[b], 1)

            sb_copy(G_KS, 0, 0, 0)
            x_high(1)
            sb_copy(G_KS + 1, 1, 0, 1)
            sb_copy(G_KS + 2, 0, 1, 0)
            high(T_KS + 2, 0, T_KS // 2 + 1, G_KS + 3)
            sb_copy(G_KS + 3, 1, 1, 1)
            high(T_KS + 3, 1, T_KS // 2 + 1, G_KS + 4)
            for a in range(2):
                for half in range(2):
                    sb_copy(G_KS + 4 + 2 * a + half, 2 + a, half, half)
                high(T_VS + a, a, T_VS // 2, G_KS + 4 + 2 * a + 2)
            for a in range(2):
                high(T_ZS + a, a, T_ZS // 2, G_ZS)
            act.wait_ge(rt_done, 1)
            flat = lambda r: r[:, :, :].rearrange("h c t -> h (c t)")
            func(flat(row_a), ps[0:H, 2 * HALF:4 * HALF], ACT.Identity, bias=ifb[:, 0:1]).then_inc(row_act, 1)
            func(flat(row_m), ps[0:H, 4 * HALF:6 * HALF], ACT.Identity, bias=ifb[:, 1:2]).then_inc(row_act, 1)
            act.wait_ge(row_dve, 1)
            func(flat(row_b), flat(row_b), ACT.Exp, scale=-1.0).then_inc(row_act, 1)
            act.wait_ge(row_act, 3)
            func(flat(row_b), flat(row_b), ACT.Ln, bias=onec[0:H, :]).then_inc(row_act, 1)
            high(T_SB, 0, T_SB // 2, G_ZS + 2)
            act.wait_ge(row_dve, 16)
            func(flat(row_iw), flat(row_iw), ACT.Exp).then_inc(row_act, 1)
            act.wait_ge(row_dve, 17)
            act.dma_start(rows_dram[0].rearrange("h (c t) -> h c t", c=NT), row_m[:, :, :]).then_inc(s_rows, 16)
            act.wait_ge(row_act, 5)
            act.dma_start(rows_dram[1].rearrange("h (c t) -> h c t", c=NT), row_iw[:, :, :]).then_inc(s_rows, 16)
            high(T_SB + 1, 1, T_SB // 2, G_SB)
            act.wait_ge(ct_done, 1)
            func(cols[:, 0, :], bank(6, NT * H), ACT.Copy)
            func(cols[:, 1:3, :].rearrange("p r n -> p (r n)"), bank(6, 2 * NT * H, NT * H), ACT.Exp).then_inc(ct_free, 1)
            for n in range(4):
                a, half = n // 2, n % 2
                act.wait_ge(pj_free[half], G_ZS // 2 + a + 1)
                if n >= 2:
                    act.wait_ge(zs_gate, n - 1)
                func(ts[:, n % 2, :], yg[:, 4 + a, HALF * half:HALF * half + HALF], ACT.Sigmoid).then_inc(zs_sig, 1)
            act.wait_ge(zs_gate, 4)
            act.wait_ge(s_rows, 32)
            act.dma_start(dec[:, :, :].rearrange("p h (c o) -> p (h c) o", o=1),
                          bass.AP(rows_dram.tensor, H * S + P - 1, [[0, P], [P, H * NT], [1, 1]]),
                          allow_slow_non_contiguous=True).then_inc(s_dec, 16)
            with act.Fori(0, 2) as hp:
                for what, j, part in order:
                    if what == "scores":
                        i, hh = j // 2, j % 2
                        n = P * (i + 1)
                        act.wait_ge(z_ready, after(hp * 16, j))
                        back = seg_index[((j - 2) % 16, 0 if (j - 2) % 16 < 8 else 1)] - (NSEG if j < 2 else 0)
                        act.wait_ge(t_ready, after(hp * NSEG, back))
                        act.wait_ge(a_ready, after(hp * 16, j - 2))
                        z = ps[:, (2 + 2 * hh) * HALF:(2 + 2 * hh) * HALF + n]
                        func(keep[:, hh, 0:n], z, ACT.Sigmoid, scale=-(DA ** -0.5)).then_inc(kp_ready, 1)
                        func(beta[:, hh, 0:n], z, ACT.Sigmoid, scale=DA ** -0.5).then_inc(sg_ready, 1)
                    if what == "proj" and part == PARTS - 1:
                        tile, half = j // 2, j % 2
                        act.wait_ge(pj_done, hp * 12 + (G_SB + j + 1))
                        tok = slice(HALF * half, HALF * half + HALF)
                        ygf = yg[:, :, :].rearrange("p m t -> p (m t)")
                        if tile < 2:
                            func(ygf[:, bass.ds(hp * (2 * S) + (tile * S + half * HALF), HALF)], bank(half), ACT.Sigmoid
                                 ).then_inc(pj_free[half], 1)
                        elif tile < 4:
                            act.wait_ge(ts_free, after(hp * 4, j - 4 - 2))
                            func(ts[:, half, :], bank(half), ACT.Sigmoid).then_inc(gs_ready, 1)
                        elif tile == 4:
                            func(ygf[:, bass.ds(hp * S + (6 * S + half * HALF), HALF)], bank(half), ACT.Sigmoid
                                 ).then_inc(gs_ready, 1)
                        if half == 1:
                            high(None, tile % 2, hp * 3 + (T_SB + tile + 2) // 2, hp * 12 + (G_SB + j + 1))
            act.wait_ge(cb_zero, 1)

            with act.Fori(0, 4) as it:
                for a in range(2):
                    m = it * 2 + a
                    for half in range(2):
                        act.wait_ge(pj_done, it * 4 + (G_CONV + 2 * a + half + 1))
                        act.wait_ge(cv_sum, after(it * 2, a - 2))
                        func(cb[:, a, 3 + HALF * half:3 + HALF * half + HALF], bank(half), ACT.Copy
                             ).then_inc(pj_free[half], 1)
                    for half in range(2):
                        act.wait_ge(pj_free[half], it * 2 + (G_CONV // 2 + a + 1))
                    qk = qkm[:, :, :].rearrange("p m t -> p (m t)")[:, bass.ds(m * S, S)]
                    func(qk, cb[:, a, 3:3 + S], ACT.Identity, bias=pt[:, bass.ds(m + PT_CB, 1)],
                         scale=pt[:, bass.ds(m + (PT_CW + 3 * KT), 1)]).then_inc(cv_first, 1)
                    high(None, a, it + (T_CONV // 2 + 1), it * 4 + (G_CONV + 2 * a + 2))
                    act.wait_ge(cv_sum, after(it * 2, a))
                    act.wait_ge(cv_out, after(it * 2, a - 2))
                    act.sem_inc(waited, 1)
                    func(sg[:, a, :], qk, ACT.Sigmoid).then_inc(cv_sig, 1)

            act.preload_act_table_set("natural_log_exp_and_others")

            def probabilities(b):
                act.wait_ge(mx_ready, after(0, b))
                act.wait_ge(pt2_done, after(0, b - 1))
                for h in range(H):
                    c = func(pc[:, h, :], bank(2 + h // 2, NM, NM * (h % 2)), ACT.Exp, bias=nmx[:, h:h + 1],
                             scale=DA ** -0.5, accum_out=sums[:, h:h + 1])
                c.then_inc(p_ready, 1)

            def v_copy(n):
                u, tt = n // NT, n % NT
                act.wait_ge(pj_done, G_VM + n + 1)
                func(vm4[:, tt, 2 * u:2 * u + 2, 0:DH],
                     bank(n % 2, 2 * DH).rearrange("p (a e) -> p a e", a=2), ACT.Copy).then_inc(pj_free[n % 2], 1)

            probabilities(0)
            act.wait_ge(cv_out, after(0, 7))
            for b in range(NT):
                v_copy(2 * b)
                act.wait_ge(pt2_done, after(0, b))
                act.wait_ge(oc_done, after(0, b - 1))
                func(pct[:, HALF:2 * HALF], bank(5), ACT.Copy).then_inc(pa_ev, 1)
                v_copy(2 * b + 1)
                if b == NT // 2 - 1:
                    for a in range(2):
                        high(None, a, 1 + T_VM // 2, G_VM + NT)
                if b < NT - 1:
                    probabilities(b + 1)
                act.wait_ge(ssc_ready, after(0, b - 1))
                func(sqc[:, 0:H, :].rearrange("p h e -> p (h e)"), os_[:, b, :, :].rearrange("p h e -> p (h e)"),
                     ACT.Square)
                act.wait_ge(oc_done, after(0, b))
                func(sqc[:, H:2 * H, :].rearrange("p h e -> p (h e)"), bank(6, H * DA), ACT.Square
                     ).then_inc(sqc_ready, 1)
                act.wait_ge(ssc_ready, after(0, b))
                chain(func(l8[:, :], u8[:, :], ACT.Ln, bias=epsc[:, :], scale=1.0 / DA))
                func(l8[:, :], l8[:, :], ACT.Exp, scale=-0.5).then_inc(rsc_ready, 1)
            act.wait_ge(y_done, after(0, NT - 1))

            def decays(c0, a):
                b = a % 2
                act.wait_ge(nm_masked, after(c0, a))
                for h in range(H):
                    c = func(dm[:, b, h, :], dm[:, b, h, :], ACT.Exp, bias=col(c0, 0, a, h))
                c.then_inc(d_ready, 1)

            def col(c0, r, a, h):
                return cols[:, :, :].rearrange("p r n -> p (r n)")[:, bass.ds(c0 * H + (r * NT * H + a * H + h), 1)]

            def weighted_keys(c0, a):
                b = a % 2
                act.wait_ge(kt_done, after(c0, a))
                act.wait_ge(kv_done, after(c0, a - 2))
                for h in range(H):
                    c = func(kw[:, b, h, :], bank(1, P, P * h), ACT.Copy, scale=col(c0, 1, a, h))
                c.then_inc(kw_ready, 1)

            def numerators(c0, a):
                act.wait_ge(n_done, after(c0, a))
                act.wait_ge(hnm_ready, after(c0, a - 2))
                func(ns[:, a, :, :].rearrange("p (b h) e -> p b (h e)", b=2),
                     ps[:, 4 * HALF:6 * HALF].rearrange("p (b n) -> p b n", b=2)[:, :, 0:2 * VW], ACT.Copy
                     ).then_inc(ns_ready, 1)
                act.wait_ge(ns_ready, after(c0, a))
                act.wait_ge(ssm_ready, after(c0, a - 1))
                func(sqm[:, :, :], ns[:, a, :, 0:DH], ACT.Square).then_inc(sqm_ready, 1)

            def head_rms(c0, a):
                act.wait_ge(ssm_ready, after(c0, a))
                chain(func(l4[:, :], u4[:, :], ACT.Ln, bias=epsc[:, :], scale=1.0 / DH))
                func(l4[:, :], l4[:, :], ACT.Exp, scale=-0.5).then_inc(rsm_ready, 1)

            def chunk_round(c0, half_tile, final=False):
                for a in range(2):
                    more = not (final and a == 1)
                    if more:
                        decays(c0, a + 1)
                    numerators(c0, a)
                    if more:
                        weighted_keys(c0, a + 1)
                    high(None, a, half_tile, G_END, bass.ds(c0 * P + a * P, P))
                    head_rms(c0, a)

            decays(0, 0)
            weighted_keys(0, 0)
            chunk_round(0, T_OUT // 2)
            with act.Fori(1, ROUNDS - 1) as it:
                chain.loop(it, 2, 1)
                chunk_round(it * 2, it + T_OUT // 2)
            chain.end(ROUNDS - 1)

            def y_high(reg, a):
                act.wait_ge(yo_done, after(reg * 2, a - 2))
                func(y_first[0][:, :, :] if a == 0 else whi[:, :, P:2 * P], yg[:, :, bass.ds(reg * 256 + a * P, P)],
                     ACT.Copy).then_inc(y_hi, 1)

            y_high(0, 0)
            chunk_round(NT - 2, ROUNDS - 1 + T_OUT // 2, final=True)
            act.wait_ge(ygm_done, after(0, NT - 1))

            def out_rms(it, a):
                act.wait_ge(yo_done, after(it * 2, a))
                chain(func(sq_out[:, :], ps[:, 2 * a * HALF:(2 * a + 2) * HALF], ACT.Square, accum_out=sso[:, a:a + 1]))
                chain(func(sso[:, a:a + 1], sso[:, a:a + 1], ACT.Ln, bias=epsc[:, :], scale=1.0 / D))
                act.wait_ge(on_ready, after(it * 2, a - 2))
                func(rso[:, a:a + 1], sso[:, a:a + 1], ACT.Exp, scale=-0.5).then_inc(rso_ready, 1)

            y_high(0, 1)
            act.wait_ge(s_gp, 16)
            with act.Fori(0, ROUNDS - 1) as it:
                chain.loop(it, 4)
                for a in range(2):
                    out_rms(it, a)
                    y_high(it + 1, a)
            chain.end(ROUNDS - 1)
            for a in range(2):
                out_rms(ROUNDS - 1, a)

        @block.vector
        def _(dve):
            start(dve, "dve")
            chain = Chain(dve, self_dve)

            def scale(i, src, t, at0):
                dve.wait_ge(rs_ready, i + 1)
                for k in range(2):
                    dve.tensor_scalar(src[:, t + k, :], src[:, t + k, :], rsx[:, at0 + k:at0 + k + 1], None,
                                      ALU.mult).then_inc(xn_ready, 1)

            def x_low(h2):
                for k in range(KT):
                    n = 8 + 8 * h2 + k
                    dve.wait_ge(hi_done, n + 1)
                    tok = slice(HALF * h2, HALF * h2 + HALF)
                    dve.scalar_tensor_tensor(out=ht_lo[:, k, tok], in0=bank(2 + n % 6),
                                             scalar=pt[:, PT_GPRE + k:PT_GPRE + k + 1],
                                             in1=ht_hi[:, k, tok].bitcast(F32), op0=ALU.mult, op1=ALU.subtract
                                             ).then_inc(lo_done, 1)

            scale(0, mraw, 0, 8)
            dve.wait_ge(pt_ready, 1)
            for k in range(KT):
                dve.wait_ge(hi_done, k + 1)
                dve.scalar_tensor_tensor(out=mt_lo[:, k, :], in0=bank(2 + k % 6, NM),
                                         scalar=pt[:, PT_GMEM + k:PT_GMEM + k + 1],
                                         in1=mt_hi[:, k, :].bitcast(F32), op0=ALU.mult, op1=ALU.subtract
                                         ).then_inc(lo_done, 1)
            scale(1, xr, 0, 0)
            scale(2, xr, 2, 2)
            for n in range(2):
                dve.wait_ge(pj_done, n + 1)
                dve.tensor_copy(k_c[:, n, :], bank(n, NM)).then_inc(pj_free[n], 1)
            x_low(0)
            scale(3, xr, 4, 4)
            for n in range(2):
                dve.wait_ge(pj_done, n + 3)
                dve.tensor_copy(v_c[:, n, :], bank(n, NM)).then_inc(pj_free[n], 1)
            scale(4, xr, 6, 6)
            x_low(1)
            for tt in range(NT):
                dve.wait_ge(pj_done, G_VS + tt + 1)
                dve.tensor_copy(gt[:, tt, :], bank(tt % 2, 8, 256)).then_inc(gt_ready, 1)
                dve.tensor_copy(v_s[:, tt, :], bank(tt % 2, 256)).then_inc(pj_free[tt % 2], 1)

            def raw_gate(n):
                a, half = n // 2, n % 2
                dve.wait_ge(pj_done, G_ZS + n + 1)
                dve.tensor_copy(yg[:, 4 + a, HALF * half:HALF * half + HALF], bank(half)).then_inc(pj_free[half], 1)

            raw_gate(0)
            step = Chain(dve, row_dve)
            flat = lambda r: r[:, :, :].rearrange("h c t -> h (c t)")
            dve.wait_ge(row_act, 2)
            step(dve.scalar_tensor_tensor(out=flat(row_b), in0=flat(row_m), scalar=-1.0, in1=flat(row_m),
                                          op0=ALU.mult, op1=ALU.max))
            step(dve.memset(flat(row_d), 1.0))
            step(dve.memset(row_d[:, :, 0:1], 0.0))
            raw_gate(1)
            dve.wait_ge(row_act, 4)
            step(dve.scalar_tensor_tensor(out=flat(row_m), in0=flat(row_m), scalar=0.0, in1=flat(row_b),
                                          op0=ALU.min, op1=ALU.subtract))
            step(dve.tensor_tensor_scan(flat(row_b), flat(row_d), flat(row_m), 0.0, ALU.mult, ALU.add))
            step(dve.tensor_tensor(flat(row_a), flat(row_a), flat(row_b), ALU.subtract))
            step(dve.tensor_copy(bl_[:, :], row_b[:, :, P - 1]))
            step(dve.memset(flat(row_d), 0.0))
            step(dve.tensor_copy(row_d[:, 1:NT, 0], bl_[:, 0:NT - 1]))
            raw_gate(2)
            step(dve.tensor_tensor_scan(flat(row_m), flat(row_d), flat(row_a), 0.0, ALU.add, ALU.max))
            step(dve.tensor_copy(ml[:, :], row_m[:, :, P - 1]))
            step(dve.memset(mp[:, 0:1], 0.0))
            step(dve.tensor_tensor(mp[:, 1:NT], bl_[:, 0:NT - 1], ml[:, 0:NT - 1], ALU.add))
            step(dve.tensor_tensor(row_d[:, :, :], row_a[:, :, :], ml[:, :].unsqueeze(2).broadcast_to([H, NT, P]),
                                   ALU.subtract))
            step(dve.scalar_tensor_tensor(out=flat(row_b), in0=flat(row_b), scalar=-1.0, in1=flat(row_m),
                                          op0=ALU.mult, op1=ALU.subtract))
            step(dve.tensor_tensor(row_iw[:, :, :], mp[:, :].unsqueeze(2).broadcast_to([H, NT, P]), row_m[:, :, :],
                                   ALU.subtract))
            step(dve.tensor_scalar(flat(row_m), flat(row_m), -1.0, None, ALU.mult))
            raw_gate(3)
            for n in range(4):
                a, half = n // 2, n % 2
                y = yg[:, 4 + a, HALF * half:HALF * half + HALF]
                dve.wait_ge(zs_sig, n + 1)
                dve.scalar_tensor_tensor(out=y, in0=y, scalar=pt[:, PT_GS + a:PT_GS + a + 1], in1=ts[:, n % 2, :],
                                         op0=ALU.mult, op1=ALU.mult).then_inc(zs_gate, 1)
            with dve.Fori(0, 2) as hp:
                chain.loop(hp, 16 + 4)
                ygf = yg[:, :, :].rearrange("p m t -> p (m t)")

                def shares(j):
                    hh, n = j % 2, P * (j // 2 + 1)
                    dve.wait_ge(kp_ready, after(hp * 16, j))
                    chain(dve.tensor_tensor_scan(keep[:, hh, n - 1::-1], keep[:, hh, n - 1::-1], keep[:, hh, n - 1::-1],
                                                 1.0, ALU.mult, ALU.bypass))
                    dve.wait_ge(sg_ready, after(hp * 16, j))
                    dve.tensor_tensor(beta[:, hh, 0:n - 1], beta[:, hh, 0:n - 1], keep[:, hh, 1:n], ALU.mult
                                      ).then_inc(a_ready, 1)

                def gates(j):
                    tile, half = j // 2, j % 2
                    if tile in (2, 3):
                        dve.wait_ge(gs_ready, after(hp * 6, j - 4))
                        m = hp * 2 + (tile - 2)
                        chain(dve.scalar_tensor_tensor(out=ts[:, half, :], in0=bank(half),
                                                       scalar=pt[:, bass.ds(m + PT_GM, 1)], in1=ts[:, half, :],
                                                       op0=ALU.mult, op1=ALU.mult))
                        dve.sem_inc(pj_free[half], 1)
                        y = ygf[:, bass.ds(hp * (2 * S) + ((tile - 2) * S + half * HALF), HALF)]
                        dve.tensor_tensor(y, y, ts[:, half, :], ALU.mult).then_inc(ts_free, 1)
                    elif tile == 4:
                        dve.wait_ge(gs_ready, after(hp * 6, j - 4))
                        y = ygf[:, bass.ds(hp * S + (6 * S + half * HALF), HALF)]
                        dve.scalar_tensor_tensor(out=y, in0=bank(half), scalar=pt[:, bass.ds(hp + PT_GC, 1)], in1=y,
                                                 op0=ALU.mult, op1=ALU.mult).then_inc(pj_free[half], 1)
                    elif tile == 5:
                        dve.wait_ge(pj_done, hp * 12 + (G_SB + j + 1))
                        dve.tensor_copy(q_c[:, :, :].rearrange("p m t -> p (m t)")[
                            :, bass.ds(hp * S + half * HALF, HALF)], bank(half)).then_inc(pj_free[half], 1)

                late = None
                for what, j, part in order:
                    i, hh = j // 2, j % 2
                    if what == "scores" and j == 0:
                        shares(0)
                    if what == "turn":
                        g = seg_index[(j, part)]
                        n = P * (min(4 * part + 4, i + 1) - 4 * part)
                        dve.wait_ge(t_ready, after(hp * NSEG, g))
                        dve.wait_ge(av_done, after(hp * NSEG, g - 2))
                        dve.tensor_copy(at_[:, g % 2, 0:n], bank(6, n)).then_inc(t_ev, 1)
                        if late is not None:
                            gates(late)
                            late = None
                    if what == "values" and (i < 4 or part == 1):
                        if j < 15:
                            shares(j + 1)
                        g = seg_index[(j, part)]
                        dve.wait_ge(av_done, after(hp * NSEG, g))
                        dve.tensor_copy(os_[:, :, :, :].rearrange("p i h e -> p (i h e)")[
                            :, bass.ds(hp * (2 * DA) + (i * H * DA + hh * DA), DA)], bank(7, DA)).then_inc(o_ev, 1)
                    if what == "proj" and part == PARTS - 1:
                        if late is not None:
                            gates(late)
                        late = j
                if late is not None:
                    gates(late)
            chain.end(2)
            dve.wait_ge(av_done, after(0, 2 * NSEG - 1))
            dve.memset(cb[:, :, 0:3], 0.0).then_inc(cb_zero, 1)
            with dve.Fori(0, 4) as it:
                chain.loop(it, 4)
                for a in range(2):
                    m = it * 2 + a
                    qk = qkm[:, :, :].rearrange("p m t -> p (m t)")[:, bass.ds(m * S, S)]
                    dve.wait_ge(cv_first, after(it * 2, a))
                    for j in (2, 1, 0):
                        c = dve.scalar_tensor_tensor(out=qk, in0=cb[:, a, j:j + S],
                                                     scalar=pt[:, bass.ds(m + (PT_CW + j * KT), 1)], in1=qk,
                                                     op0=ALU.mult, op1=ALU.add)
                        if j:
                            chain(c)
                    c.then_inc(cv_sum, 1)
                    dve.wait_ge(cv_sig, after(it * 2, a))
                    dve.scalar_tensor_tensor(out=qk, in0=qk, scalar=ks[:, bass.ds(m, 1)], in1=sg[:, a, :],
                                             op0=ALU.mult, op1=ALU.mult).then_inc(cv_out, 1)
            chain.end(4)
            def gate(b):
                dve.wait_ge(yt_done, after(0, b))
                y = yg[:, 4:8, P * b:P * b + P]
                dve.tensor_tensor(y, y, bank(7).rearrange("p (m t) -> p m t", m=4), ALU.mult).then_inc(y_done, 1)

            def maximum(b):
                dve.wait_ge(sc_done, after(0, b))
                chain(dve.tensor_reduce(mx[:, :], ps[:, 2 * HALF:4 * HALF].rearrange("p (h m) -> p h m", h=H),
                                        AX_X, ALU.max))
                dve.tensor_scalar(nmx[:, :], mx[:, :], -(DA ** -0.5), None, ALU.mult).then_inc(mx_ready, 1)

            maximum(0)
            for b in range(NT):
                if b:
                    gate(b - 1)
                dve.wait_ge(p_ready, after(0, b))
                chain(dve.reciprocal(r8[:, H:2 * H], sums[:, :]))
                dve.wait_ge(pt2_done, after(0, b))
                dve.wait_ge(oc_done, after(0, b - 1))
                dve.tensor_copy(pct[:, 0:HALF], bank(4)).then_inc(pd_ev, 1)
                if b < NT - 1:
                    maximum(b + 1)
                dve.wait_ge(sqc_ready, after(0, b))
                chain(dve.tensor_reduce(ss8[:, :], sqc[:, :, :], AX_X, ALU.add))
                chain(dve.tensor_tensor(ss8[:, :], ss8[:, :], r8[:, :], ALU.mult))
                dve.tensor_tensor(u8[:, :], ss8[:, :], r8[:, :], ALU.mult).then_inc(ssc_ready, 1)
                dve.wait_ge(rsc_ready, after(0, b))
                chain(dve.tensor_tensor(cf8[:, :], l8[:, :], r8[:, :], ALU.mult))
                dve.wait_ge(yt_done, after(0, b - 1))
                dve.tensor_tensor(hnc[:, 0:H, :], os_[:, :, :, :].rearrange("p i h e -> p (i h) e")[
                    :, H * b:H * b + H, :], cf8[:, 0:H].unsqueeze(2).broadcast_to([P, H, DA]), ALU.mult)
                dve.tensor_tensor(hnc[:, H:2 * H, :], bank(6, H * DA).rearrange("p (h e) -> p h e", h=H),
                                  cf8[:, H:2 * H].unsqueeze(2).broadcast_to([P, H, DA]), ALU.mult).then_inc(hn_ready, 1)
            gate(NT - 1)
            dve.wait_ge(pj_done, G_END)
            chain(dve.memset(cst[:, :, :], 0.0))
            dve.sem_inc(cst_zero, 1)
            dve.wait_ge(s_dec, 16)

            def decayed_scores(c0, a):
                b = a % 2
                dve.wait_ge(d_ready, after(c0, a))
                dve.wait_ge(st_done, after(c0, a))
                dve.wait_ge(n_done, after(c0, a - 2))
                dve.tensor_tensor(sd[:, b, :, :], bank(0).rearrange("p (h t) -> p h t", h=H), dm[:, b, :, :],
                                  ALU.mult).then_inc(sd_ready, 1)

            def denominators(c0, a):
                dve.wait_ge(ns_ready, after(c0, a))
                chain(dve.scalar_tensor_tensor(out=den[:, :], in0=ns[:, a, :, DH], scalar=-1.0, in1=ns[:, a, :, DH],
                                               op0=ALU.mult, op1=ALU.max))
                chain(dve.tensor_tensor(den[:, :], den[:, :], cols[:, 2, bass.ds(c0 * H + a * H, H)], ALU.max))
                chain(dve.reciprocal(r4[:, :], den[:, :]))

            def new_state(c0, a):
                dve.wait_ge(kv_done, after(c0, a))
                decf = dec[:, :, :].rearrange("p h c -> p (h c)")
                for h in range(H):
                    c = dve.scalar_tensor_tensor(out=cst[:, h, :], in0=cst[:, h, :],
                                                 scalar=decf[:, bass.ds(c0 + (h * NT + a), 1)],
                                                 in1=bank(6 + h // 2, VW, VW * (h % 2)), op0=ALU.mult, op1=ALU.add)
                c.then_inc(c_upd, 1)

            def mean_squares(c0, a):
                dve.wait_ge(sqm_ready, after(c0, a))
                chain(dve.tensor_reduce(ss4[:, :], sqm[:, :, :], AX_X, ALU.add))
                chain(dve.tensor_tensor(ss4[:, :], ss4[:, :], r4[:, :], ALU.mult))
                dve.tensor_tensor(u4[:, :], ss4[:, :], r4[:, :], ALU.mult).then_inc(ssm_ready, 1)

            def normed(c0, a):
                dve.wait_ge(rsm_ready, after(c0, a))
                chain(dve.tensor_tensor(cf4[:, :], l4[:, :], r4[:, :], ALU.mult))
                dve.wait_ge(ym_done, after(c0, a - 2))
                dve.tensor_tensor(hnm[:, a, :, :], ns[:, a, :, 0:DH], cf4[:, :].unsqueeze(2).broadcast_to([P, H, DH]),
                                  ALU.mult).then_inc(hnm_ready, 1)

            def gated(c0, a):
                b = a % 2
                dve.wait_ge(ym_done, after(c0, a))
                y = yg[:, 0:H, bass.ds(c0 * P + a * P, P)]
                dve.tensor_tensor(y, y, bank(2 + b).rearrange("p (h t) -> p h t", h=H), ALU.mult).then_inc(ygm_done, 1)

            def chunk_round(c0, first=False, final=False):
                for a in range(2):
                    new_state(c0, a)
                    if not (final and a == 1):
                        decayed_scores(c0, a + 1)
                    denominators(c0, a)
                    mean_squares(c0, a)
                    if not (first and a == 0):
                        gated(c0, a - 1)
                    normed(c0, a)

            decayed_scores(0, 0)
            chunk_round(0, first=True)
            with dve.Fori(1, ROUNDS - 1) as it:
                chain.loop(it, 2 * 6, 1)
                chunk_round(it * 2)
            chain.end(ROUNDS - 1)

            def y_low(reg, a):
                hi, lo = (y_first[0][:, :, :], y_first[1][:, :, :]) if a == 0 else (whi[:, :, P:2 * P], wlo[:, :, P:2 * P])
                dve.wait_ge(y_hi, after(reg * 2, a))
                dve.tensor_tensor(lo, yg[:, :, bass.ds(reg * 256 + a * P, P)], hi.bitcast(F32), ALU.subtract
                                  ).then_inc(y_lo, 1)

            y_low(0, 0)
            chunk_round(NT - 2, final=True)
            gated(NT - 2, 1)

            def out_norm(it, a):
                dve.wait_ge(rso_ready, after(it * 2, a))
                dve.wait_ge(s_out[a], it * 16 + 16)
                dve.scalar_tensor_tensor(out=ot[:, a, :], in0=ps[:, 2 * a * HALF:(2 * a + 2) * HALF],
                                         scalar=rso[:, a:a + 1], in1=gpost[:, :], op0=ALU.mult, op1=ALU.mult
                                         ).then_inc(on_ready, 1)

            y_low(0, 1)
            dve.wait_ge(s_gp, 16)
            with dve.Fori(0, ROUNDS - 1) as it:
                for a in range(2):
                    out_norm(it, a)
                    y_low(it + 1, a)
            for a in range(2):
                out_norm(ROUNDS - 1, a)


_INS = ["x", "mem", "g_pre", "w_in", "conv_w", "conv_b", "i_bias", "f_bias", "g_mlstm_head", "g_sb_head",
        "g_mem_head", "g_mem", "w_mem_kv", "w_out", "g_post"]


def kernel(**inputs):
    import numpy as _np
    import concourse.bacc as _bacc
    from concourse import mybir as _mybir
    from concourse.bass_utils import run_bass_kernel_spmd as _run

    nc = _bacc.Bacc("TRN2", target_bir_lowering=False, num_devices=1)
    arrays, args = {}, []
    for name in _INS:
        a = _np.ascontiguousarray(inputs[name])
        arrays[f"in_{name}_dram"] = a
        args.append(nc.dram_tensor(f"in_{name}_dram", a.shape, _mybir.dt.from_np(a.dtype), kind="ExternalInput").ap())
    args.append(nc.dram_tensor("out_dram", (1, S, D), _mybir.dt.float32, kind="ExternalOutput").ap())
    args.append(nc.dram_tensor("rows_dram", (2, H, S), _mybir.dt.float32, kind="Internal").ap())
    hybrid_layer(nc, *args)
    r = _run(nc, [arrays], core_ids=[0])
    return r.results[0]["out_dram"]
```

```python
from contextlib import ExitStack

import concourse.bass as bass
from concourse import mybir

ALU = mybir.AluOpType
ACT = mybir.ActivationFunctionType
AX_X = mybir.AxisListType.X
F32 = mybir.dt.float32
F32R = mybir.dt.float32r
BF16 = mybir.dt.bfloat16

P = 128
S = 1024
D = 1024
KT = D // P
NT = S // P
HALF = 512
NM = 256
H = 4
DH = 128
DA = 64
CW = 4
VW = DH + 1
EPS = 1e-6
NEG = -1e30

C_QM, C_KM, C_VM, C_OM, C_ZM, C_IF = 0, 512, 1024, 1536, 2048, 2560
C_QS, C_KS, C_VS, C_ZS, C_QC, C_ZC = 2568, 2824, 3080, 3336, 3592, 3848

PT_CW, PT_CB, PT_GPRE, PT_GMEM, PT_GM, PT_GS, PT_GC, N_PT = 0, 32, 40, 48, 56, 60, 62, 64

T_KS, T_VS, T_ZS, T_SB, T_CONV, T_VM, T_OUT, T_END = 4, 8, 10, 12, 24, 32, 36, 44
G_KS, G_VS, G_ZS, G_SB, G_CONV, G_VM, G_END = 4, 12, 20, 24, 48, 64, 80

CR = 4
PARTS = 4
ROUNDS = NT // 2


def after(reg, k):
    return reg + (k + 1 + CR)


def sb_order():
    todo = [("proj", group, part) for group in range(12) for part in range(PARTS)]
    slots = 1 + 16 + sum(1 if j // 2 < 4 else 2 for j in range(16))
    spare = len(todo) - slots
    out = []
    for j in range(17):
        if j < 16:
            out.append(("scores", j, 0))
        out.append(todo.pop(0))
        if 3 <= j < 3 + spare:
            out.append(todo.pop(0))
        if j:
            for seg in range(1 if (j - 1) // 2 < 4 else 2):
                out.append(("turn", j - 1, seg))
                out.append(todo.pop(0))
                out.append(("values", j - 1, seg))
    assert not todo
    return out


def hybrid_layer(nc, x, mem, g_pre, w_in, conv_w, conv_b, i_bias, f_bias, g_mlstm_head, g_sb_head,
                 g_mem_head, g_mem, w_mem_kv, w_out, g_post, out, rows_dram):
    order = sb_order()
    seg_index = {}
    for what, j, seg in order:
        if what == "turn":
            seg_index[(j, seg)] = len(seg_index)
    NSEG = len(seg_index)
    assert NSEG % 2 == 0

    with ExitStack() as ctx:
        def sem(name):
            return ctx.enter_context(nc.semaphore(name))

        at = {"next": -(-nc.sbuf_base // 64) * 64}
        size = {F32: 4, F32R: 4, BF16: 2}

        def region(nbytes):
            base = at["next"]
            at["next"] = base + -(-nbytes // 64) * 64
            assert at["next"] <= nc.sbuf_top
            return {"at": base, "end": at["next"]}

        def place(reg, name, shape, dt=F32):
            n = size[dt]
            for d in shape[1:]:
                n *= d
            t = nc.alloc_sbuf_tensor_at(name, shape, dt, offset=reg["at"])
            reg["at"] += -(-n // 64) * 64
            assert reg["at"] <= reg["end"], name
            return t

        def again(reg, back):
            return {"at": back, "end": reg["end"]}

        r_ht = region(2 * KT * S * 4)
        r_yg = region(KT * S * 4)
        r_qk = region(KT * S * 4)
        r_vm = region(NT * H * VW * 4)
        r_w = region(3 * KT * 264 * 4)
        r_qc = region((2 * S + 2 * NM + 2 * H * DA) * 4)
        r_os = region(NT * H * DA * 4)
        r_wk = region(14 * 1024)
        r_c = {"at": at["next"], "end": nc.sbuf_top}
        b_yg, b_qk, b_vm, b_w, b_qc, b_os, b_wk = (r["at"] for r in (r_yg, r_qk, r_vm, r_w, r_qc, r_os, r_wk))

        ht_hi = place(r_ht, "ht_hi", [P, KT, S], F32R)
        ht_lo = place(r_ht, "ht_lo", [P, KT, S], F32R)
        yg = place(r_yg, "yg", [P, KT, S])
        xr = place(again(r_yg, b_yg), "xr", [P, NT, D])
        qkm = place(r_qk, "qkm", [P, KT, S])
        q = again(r_qk, b_qk)
        mt_hi = place(q, "mt_hi", [P, KT, NM], F32R)
        mt_lo = place(q, "mt_lo", [P, KT, NM], F32R)
        q = again(r_qk, b_qk)
        q_s = place(q, "q_s", [P, 2 * S])
        k_s_hi = place(q, "k_s_hi", [P, 2 * S], F32R)
        k_s_lo = place(q, "k_s_lo", [P, 2 * S], F32R)
        v_s = place(q, "v_s", [P, NT, H * DA])
        q = again(r_qk, b_qk)
        xt = place(q, "xt", [P, 2, D])
        ot = place(q, "ot", [P, 2, D])
        gpost = place(q, "gpost", [P, D])
        sq_out = place(q, "sq_out", [P, D])
        vm = place(r_vm, "vm", [P, NT * H * VW])
        vm4 = vm[:, :].rearrange("p (c h e) -> p c h e", c=NT, h=H)
        q = again(r_vm, b_vm)
        mraw = place(q, "mraw", [P, 2, D])
        q = again(r_vm, b_vm)
        row_a = place(q, "row_a", [H, NT, P])
        row_m = place(q, "row_m", [H, NT, P])
        row_b = place(q, "row_b", [H, NT, P])
        row_d = place(q, "row_d", [H, NT, P])
        q = again(r_vm, b_vm)
        beta = place(q, "beta", [P, 2, S])
        keep = place(q, "keep", [P, 2, S])
        q = again(r_vm, b_vm)
        cb = place(q, "cb", [P, 2, S + 3])
        sg = place(q, "sg", [P, 2, S])
        wraw = place(r_w, "wraw", [P, KT, 264])
        whi = place(r_w, "whi", [P, KT, 264], F32R)
        wlo = place(r_w, "wlo", [P, KT, 264], F32R)
        q_c = place(r_qc, "q_c", [P, 2, S])
        k_c = place(r_qc, "k_c", [P, 2, NM])
        v_c = place(r_qc, "v_c", [P, 2, H * DA])
        os_ = place(r_os, "os", [P, NT, H, DA])
        q = again(r_wk, b_wk)
        at_ = place(q, "at", [P, 2, HALF])
        ts = place(q, "ts", [P, 2, HALF])
        sq_in = place(again(r_wk, b_wk + 4096), "sq_in", [P, D])
        sq_odd_out = place(again(r_wk, b_wk + 8192), "sq_odd_out", [P, D])
        qf = place(q, "qf", [P, 2, 2, P])
        qz = [place(q, name, [P, 2, 2, P], F32R) for name in ("qz_hi", "qz_lo")]
        q = again(r_wk, b_wk)
        row_iw = place(q, "row_iw", [H, NT, P])
        row_e = place(q, "row_e", [H, NT, P])
        q = again(r_wk, b_wk)
        pc = place(q, "pc", [P, H, NM])
        pct = place(q, "pct", [P, 2 * HALF])
        sqc = place(q, "sqc", [P, 2 * H, DA])
        hnc = place(q, "hnc", [P, 2 * H, DA])
        qcz = place(q, "qcz", [P, H, P])
        q = again(r_wk, b_wk)
        dm = place(q, "dm", [P, 2, H, P])
        iwb = place(q, "iwb", [P, 2, H, P])
        sqm = place(q, "sqm", [P, H, P])
        q = again(r_os, b_os)
        y_first = [place(q, name, [P, KT, P], F32R) for name in ("y_first_hi", "y_first_lo")]
        q = again(r_qc, b_qc)
        kst = place(q, "kst", [P, 2, H, P])
        qs2 = place(q, "qs2", [P, 2, H, P])
        sd = place(q, "sd", [P, 2, H, P])
        q = {"at": b_w + KT * 264 * 4, "end": r_w["end"]}
        kw = place(q, "kw", [P, 2, H, P])
        ns = place(q, "ns", [P, 2, H, VW])
        cst = place(q, "cst", [P, H, VW])
        hnm = place(q, "hnm", [P, 2, H, P])
        ident = place(r_c, "ident", [P, P])
        identb = place(r_c, "identb", [P, P], BF16)
        maskb = place(r_c, "maskb", [P, P], BF16)
        maskd = place(r_c, "maskd", [P, P])
        prow = place(r_c, "prow", [N_PT, P])
        pt = place(r_c, "pt", [P, N_PT])
        ifb = place(r_c, "ifb", [H, 2])
        gt = place(r_c, "gt", [P, NT, 2 * H])
        ks = place(r_c, "ks", [P, 2 * H])
        ones = place(r_c, "ones", [P, 1, 1])
        own = place(r_c, "own", [P, 2])
        epsc = place(r_c, "epsc", [P, 1])
        onec = place(r_c, "onec", [P, 1])
        ssx = place(r_c, "ssx", [P, 10])
        rsx = place(r_c, "rsx", [P, 10])
        bl_ = place(r_c, "bl", [H, NT])
        mp = place(r_c, "mp", [H, NT])
        ml = place(r_c, "ml", [H, NT])
        dec = place(r_c, "dec", [P, H, NT])
        cols = place(r_c, "cols", [P, 3, NT * H])
        mx = place(r_c, "mx", [P, H])
        nmx = place(r_c, "nmx", [P, H])
        sums = place(r_c, "sums", [P, H])
        r8 = place(r_c, "r8", [P, 2 * H])
        ss8 = place(r_c, "ss8", [P, 2 * H])
        u8 = place(r_c, "u8", [P, 2 * H])
        l8 = place(r_c, "l8", [P, 2 * H])
        cf8 = place(r_c, "cf8", [P, 2 * H])
        den = place(r_c, "den", [P, H])
        r4 = place(r_c, "r4", [P, H])
        ss4 = place(r_c, "ss4", [P, H])
        u4 = place(r_c, "u4", [P, H])
        l4 = place(r_c, "l4", [P, H])
        cf4 = place(r_c, "cf4", [P, H])
        sso = place(r_c, "sso", [P, 2])
        sso_half = place(r_c, "sso_half", [P, 1])
        rso = place(r_c, "rso", [P, 2])

        ps = ctx.enter_context(nc.psum_tensor("ps", [P, 8 * HALF], F32))

        def bank(b, n=HALF, off=0, parts=P):
            return ps[0:parts, b * HALF + off:b * HALF + off + n]

        s_par = sem("s_par")
        s_mem = [sem("s_mem0"), sem("s_mem1")]
        s_x = [sem(f"s_x{i}") for i in range(4)]
        s_raw = [sem("s_raw0"), sem("s_raw1")]
        s_gw = sem("s_gw")
        w_hi, w_lo = sem("w_hi"), sem("w_lo")
        gw_hi, gw_lo = sem("gw_hi"), sem("gw_lo")
        c_ready = sem("c_ready")
        pt_done, pt_ready = sem("pt_done"), sem("pt_ready")
        rs_ready = sem("rs_ready")
        xn_ready = sem("xn_ready")
        ks_high = sem("ks_high")
        sq_odd = sem("sq_odd")
        tr_done = sem("tr_done")
        hi_done, lo_done = sem("hi_done"), sem("lo_done")
        pj_done = sem("pj_done")
        pj_free = [sem("pj_free0"), sem("pj_free1")]
        gt_ready = sem("gt_ready")
        rt_done = sem("rt_done")
        row_act, row_dve = sem("row_act"), sem("row_dve")
        ct_done, ct_free = sem("ct_done"), sem("ct_free")
        s_rows = [sem("s_rows0"), sem("s_rows1")]
        s_dec = sem("s_dec")
        zs_sig, zs_gate = sem("zs_sig"), sem("zs_gate")
        q_staged, z_ready = sem("q_staged"), sem("z_ready")
        kp_ready, sg_ready = sem("kp_ready"), sem("sg_ready")
        a_ready, t_ready, t_ev = sem("a_ready"), sem("t_ready"), sem("t_ev")
        av_done, o_ev = sem("av_done"), sem("o_ev")
        gs_ready, ts_free = sem("gs_ready"), sem("ts_free")
        cb_zero = sem("cb_zero")
        cv_first, cv_sum, cv_sig, cv_out = sem("cv_first"), sem("cv_sum"), sem("cv_sig"), sem("cv_out")
        qc_staged, sc_done, mx_ready, p_ready = sem("qc_staged"), sem("sc_done"), sem("mx_ready"), sem("p_ready")
        pt2_done, pa_ev, pd_ev, oc_done = sem("pt2_done"), sem("pa_ev"), sem("pd_ev"), sem("oc_done")
        sqc_ready, ssc_ready, rsc_ready, hn_ready = sem("sqc_ready"), sem("ssc_ready"), sem("rsc_ready"), sem("hn_ready")
        yt_done, y_done = sem("yt_done"), sem("y_done")
        s_nm = [sem("s_nm0"), sem("s_nm1")]
        s_iw = [sem("s_iw0"), sem("s_iw1")]
        nm_masked, k_staged, q_scaled = sem("nm_masked"), sem("k_staged"), sem("q_scaled")
        d_ready, st_done, kt_done = sem("d_ready"), sem("st_done"), sem("kt_done")
        sd_ready, kw_ready, n_done, kv_done = sem("sd_ready"), sem("kw_ready"), sem("n_done"), sem("kv_done")
        c_upd, ns_ready, sqm_ready, ssm_ready = sem("c_upd"), sem("ns_ready"), sem("sqm_ready"), sem("ssm_ready")
        rsm_ready, hnm_ready, ym_done, ygm_done = sem("rsm_ready"), sem("hnm_ready"), sem("ym_done"), sem("ygm_done")
        cst_zero = sem("cst_zero")
        y_hi, y_lo, yo_done = sem("y_hi"), sem("y_lo"), sem("yo_done")
        yo_half = sem("yo_half")
        s_xt = [sem("s_xt0"), sem("s_xt1")]
        s_gp = sem("s_gp")
        rso_ready, on_ready, ot_ready, ot_last = sem("rso_ready"), sem("on_ready"), sem("ot_ready"), sem("ot_last")
        s_out = [sem("s_out0"), sem("s_out1")]
        self_act, self_dve, self_pool = sem("self_act"), sem("self_dve"), sem("self_pool")
        waited = sem("waited")
        dve_low = sem("dve_low")
        vm_ones = sem("vm_ones")
        starts_at_cr = {
            "pe": (z_ready, t_ready, av_done, sc_done, pt2_done, oc_done, yt_done, st_done, kt_done, n_done,
                   kv_done, ym_done, yo_done),
            "act": (sg_ready, kp_ready, gs_ready, p_ready, pa_ev, sqc_ready, rsc_ready, d_ready, kw_ready, ns_ready,
                    sqm_ready, rsm_ready, y_hi, rso_ready, cv_first, cv_sig),
            "dve": (a_ready, t_ev, o_ev, ts_free, cv_sum, cv_out, mx_ready, pd_ev, ssc_ready, hn_ready, y_done,
                    sd_ready, c_upd, ssm_ready, hnm_ready, ygm_done, y_lo, on_ready),
            "pool": (q_staged, qc_staged, nm_masked, k_staged, q_scaled, ot_ready),
        }

        def start(eng, name):
            for s_ in starts_at_cr[name]:
                eng.sem_inc(s_, CR)

        class Chain:

            def __init__(self, eng, s):
                self.eng, self.s, self.n, self.it, self.per, self.base = eng, s, 0, None, 0, 0

            def __call__(self, ins):
                ins.then_inc(self.s, 1)
                self.n += 1
                self.eng.wait_ge(self.s, self.n if self.it is None else self.it * self.per + self.n)

            def loop(self, it, per, first=0):
                self.n -= first * per
                self.it, self.per, self.base = it, per, self.n

            def end(self, end):
                assert self.n - self.base == self.per
                self.n, self.it = self.base + self.per * end, None

        block = ctx.enter_context(nc.Block())

        @block.sync
        def _(sp):
            w_in3 = w_in.rearrange("(k p) n -> p k n", p=P)
            w_mem3 = w_mem_kv.rearrange("(k p) n -> p k n", p=P)
            w_out3 = w_out.rearrange("(k p) n -> p k n", p=P)
            x3 = x[0].rearrange("(t p) d -> p t d", p=P)

            def raw(n, slot, src):
                sp.wait_ge(w_hi, n - 1)
                sp.wait_ge(w_lo, n - 1)
                sp.dma_start(wraw[:, :, P * slot:P * slot + P], src).then_inc(s_raw[slot], 16)

            for t in range(2):
                sp.dma_start(mraw[:, t, :], mem[0][P * t:P * t + P, :]).then_inc(s_mem[t], 16)
            row = 0
            for src, n in ((conv_w.rearrange("j (c p) -> (j c) p", p=P), CW * KT), (conv_b, KT), (g_pre, KT),
                           (g_mem, KT), (g_mlstm_head, 4), (g_sb_head, 2), (g_mem_head, 2)):
                if n != CW * KT:
                    src = src.rearrange("(c p) -> c p", p=P)
                sp.dma_start(prow[row:row + n, :], src).then_inc(s_par, 16)
                row += n
            for i, src in enumerate((i_bias, f_bias)):
                sp.dma_start(ifb[:, i:i + 1], src.rearrange("(h o) -> h o", o=1)).then_inc(s_par, 16)
            for n in range(2):
                sp.dma_start(wraw[:, :, P * n:P * n + P], w_mem3[:, :, P * n:P * n + P]).then_inc(s_raw[n], 16)
            for i in range(4):
                if i >= 2:
                    raw(i, i % 2, w_mem3[:, :, P * i:P * i + P])
                sp.dma_start(xr[:, 2 * i:2 * i + 2, :], x3[:, 2 * i:2 * i + 2, :]).then_inc(s_x[i], 16)
            sp.dma_start(wraw[:, :, 256:264], w_in3[:, :, C_IF:C_IF + 8]).then_inc(s_gw, 16)
            for n in range(T_KS, T_SB):
                raw(n, n % 2, w_in3[:, :, C_QS + P * (n - T_KS):C_QS + P * (n - T_KS + 1)])
            with sp.Fori(0, 2) as hp:
                for j in range(6):
                    col = [C_OM + hp * 256, C_OM + hp * 256 + P, C_ZM + hp * 256, C_ZM + hp * 256 + P,
                           C_ZC + hp * P, C_QC + hp * P][j]
                    raw(T_SB + hp * 6 + j, j % 2, w_in3[:, :, bass.ds(col, P)])
            with sp.Fori(0, 4) as it:
                for a in range(2):
                    raw(T_CONV + it * 2 + a, a, w_in3[:, :, bass.ds(it * 256 + a * P, P)])
            with sp.Fori(0, 2) as u:
                for a in range(2):
                    raw(T_VM + u * 2 + a, a, w_in3[:, :, bass.ds(u * 256 + (C_VM + a * P), P)])
            for row in range(2):
                sp.wait_ge(s_rows[row], 16)
            sp.dma_start(dec[:, :, :].rearrange("p h (c o) -> p (h c) o", o=1),
                         bass.AP(rows_dram.tensor, H * S + P - 1, [[0, P], [P, H * NT], [1, 1]]),
                         allow_slow_non_contiguous=True).then_inc(s_dec, 16)
            sp.wait_ge(w_lo, T_OUT)
            for a in range(2):
                raw(T_OUT + a, a, w_out3[:, :, P * a:P * a + P])
            sp.wait_ge(pt2_done, after(0, NT - 1))

            def old_state_rows(c0, a, first=False):
                sp.wait_ge(sd_ready, after(c0, a - 2))
                sp.dma_start(dm[:, a % 2, :, :], bass.AP(rows_dram.tensor, c0 * P + a * P, [[0, P], [S, H], [1, P]])
                             ).then_inc(s_nm[a % 2], 16)
                sp.wait_ge(q_scaled, after(c0, a - 2))
                if first:
                    sp.wait_ge(oc_done, after(0, NT - 1))
                sp.dma_start(iwb[:, a % 2, :, :],
                             bass.AP(rows_dram.tensor, c0 * P + (a * P + H * S), [[0, P], [S, H], [1, P]])
                             ).then_inc(s_iw[a % 2], 16)

            for a in range(3):
                old_state_rows(0, a, first=(a == 0))
            with sp.Fori(1, ROUNDS - 1) as it:
                for a in range(2):
                    old_state_rows(it * 2, a + 1)
                    raw(T_OUT + it * 2 + a, a, w_out3[:, :, bass.ds(it * 256 + a * P, P)])
            old_state_rows(NT - 2, 1)
            for a in range(2):
                raw(T_OUT + NT - 2 + a, a, w_out3[:, :, D - 256 + P * a:D - 256 + P * a + P])
            sp.wait_ge(st_done, after(0, NT - 1))
            sp.wait_ge(k_staged, after(0, NT - 1))
            sp.wait_ge(q_scaled, after(0, NT - 1))
            for a in range(2):
                sp.sem_inc(s_out[a], 16)
            sp.dma_start(gpost[:, :], bass.AP(g_post.tensor, 0, [[0, P], [1, D]])).then_inc(s_gp, 16)

            def residual_in(it, a):
                sp.wait_ge(ot_ready, after(it * 2, a - 2))
                sp.dma_start(xt[:, a, :], x[0][bass.ds(it * 256 + a * P, P), :]).then_inc(s_xt[a], 16)

            def result_out(it, a):
                sp.wait_ge(ot_ready, after(it * 2, a))
                sp.dma_start(out[0][bass.ds(it * 256 + a * P, P), :], ot[:, a, :]).then_inc(s_out[a], 16)

            with sp.Fori(0, ROUNDS - 1) as it:
                for a in range(2):
                    residual_in(it, a)
                for a in range(2):
                    result_out(it, a)
            for a in range(2):
                residual_in(ROUNDS - 1, a)
            result_out(ROUNDS - 1, 0)
            for half, added, count in ((1, ot_ready, after(0, NT - 1)), (0, ot_last, 1)):
                sp.wait_ge(added, count)
                cols_ = slice(HALF * half, HALF * half + HALF)
                sp.dma_start(out[0][S - P:S, cols_], ot[:, 1, cols_]).then_inc(s_out[1], 16)
            for a in range(2):
                sp.wait_ge(s_out[a], 16 * (ROUNDS + 1 + a))

        @block.gpsimd
        def _(pool):
            start(pool, "pool")
            chain = Chain(pool, self_pool)
            pool.memset(identb[:, :], 0.0)
            pool.memset(ident[:, :], 0.0)
            pool.memset(maskb[:, :], 0.0)
            pool.memset(maskd[:, :], 0.0)
            pool.memset(ones[:, :, :], 1.0)
            pool.memset(epsc[:, :], EPS)
            pool.memset(onec[:, :], 1.0)
            chain(pool.memset(own[:, :], 0.0))
            for hh in range(2):
                chain(pool.memset(own[DA * hh:DA * hh + DA, hh:hh + 1], 1.0))
            pool.memset(ks[:, 0:H], 1.0)
            chain(pool.memset(ks[:, H:2 * H], DH ** -0.5))
            for m in (ident, identb):
                pool.affine_select(out=m[:, :], in_=m[:, :], compare_op=ALU.not_equal, fill=1.0, base=0,
                                   pattern=[[-1, P]], channel_multiplier=1)
            pool.affine_select(out=maskb[:, :], in_=maskb[:, :], compare_op=ALU.is_gt, fill=NEG, base=0,
                               pattern=[[-1, P]], channel_multiplier=1)
            pool.affine_select(out=maskd[:, :], in_=maskd[:, :], compare_op=ALU.is_ge, fill=NEG, base=0,
                               pattern=[[1, P]], channel_multiplier=-1).then_inc(c_ready, 1)

            def low(n, slot, dst=None, col=None):
                pool.wait_ge(w_hi, n + 1)
                raw = wraw[:, :, P * slot:P * slot + P]
                if dst is None:
                    hi, lo = whi[:, :, P * slot:P * slot + P], wlo[:, :, P * slot:P * slot + P]
                else:
                    hi, lo = ht_hi[:, :, col], ht_lo[:, :, col]
                pool.tensor_tensor(lo, raw, hi.bitcast(F32), ALU.subtract).then_inc(w_lo, 1)

            def low_by_dve(n, count):
                pool.wait_ge(w_lo, n)
                pool.wait_ge(dve_low, count)
                pool.sem_inc(w_lo, 1)

            for n in range(T_VS):
                low(n, n % 2)
            pool.wait_ge(gw_hi, 1)
            pool.tensor_tensor(wlo[:, :, 256:264], wraw[:, :, 256:264], whi[:, :, 256:264].bitcast(F32),
                               ALU.subtract).then_inc(gw_lo, 1)
            low(T_VS, 0)
            low_by_dve(T_VS + 1, 1)
            for n in range(T_ZS, T_SB):
                low(n, n % 2)
            pool.wait_ge(lo_done, 24)
            for half in range(2):
                pool.wait_ge(pj_free[half], G_VS // 2)
            with pool.Fori(0, 2) as hp:
                chain.loop(hp, 16)
                for what, j, part in order:
                    if what == "scores" and j % 2 == 0:
                        i = j // 2
                        pool.wait_ge(z_ready, after(hp * 16, 2 * i - 3))
                        chain(pool.tensor_tensor(
                            qf[:, i % 2, :, :], q_s[:, bass.ds(hp * S + i * P, P)].unsqueeze(1).broadcast_to([P, 2, P]),
                            own[:, :].unsqueeze(2).broadcast_to([P, 2, P]), ALU.mult))
                        chain(pool.tensor_tensor(qz[0][:, i % 2, :, :], qf[:, i % 2, :, :],
                                                 ones[:, :, :].broadcast_to([P, 2, P]), ALU.mult))
                        pool.tensor_tensor(qz[1][:, i % 2, :, :], qf[:, i % 2, :, :], qz[0][:, i % 2, :, :].bitcast(F32),
                                           ALU.subtract).then_inc(q_staged, 1)
                    if what == "proj" and j % 2 == 1 and part == PARTS - 1:
                        low(T_SB + hp * 6 + j // 2, (j // 2) % 2)
            chain.end(2)
            with pool.Fori(0, 4) as it:
                for a in range(2):
                    low(T_CONV + it * 2 + a, a)
            pool.wait_ge(pj_free[0], G_CONV // 2)
            pool.wait_ge(pj_free[1], G_CONV // 2)
            pool.wait_ge(av_done, after(0, 2 * NSEG - 1))
            pool.memset(r8[:, :], 1.0)
            for b in range(NT):
                pool.wait_ge(sc_done, after(0, b - 1))
                for m in range(2):
                    c = pool.tensor_tensor(qcz[:, 2 * m:2 * m + 2, :],
                                           q_c[:, m, P * b:P * b + P].unsqueeze(1).broadcast_to([P, 2, P]),
                                           own[:, :].unsqueeze(2).broadcast_to([P, 2, P]), ALU.mult)
                c.then_inc(qc_staged, 1)
                if b == 0:
                    for a in range(2):
                        low(T_VM + a, a)
                    pool.wait_ge(cv_out, after(0, 7))
                    pool.memset(vm4[:, :, :, DH:VW], 1.0).then_inc(vm_ones, 1)
                if b == NT // 2:
                    low(T_VM + 2, 0)
                    low_by_dve(T_VM + 3, 2)

            def stage(c0, a):
                b = a % 2
                tok = bass.ds(c0 * P + a * P, P)
                pool.wait_ge(kt_done, after(c0, a - 2))
                pool.tensor_tensor(kst[:, b, :, :], qkm[:, H:2 * H, tok],
                                   ones[:, :, :].broadcast_to([P, H, P]), ALU.mult).then_inc(k_staged, 1)
                pool.wait_ge(s_nm[b], c0 * 8 + 16 * (a // 2 + 1))
                pool.tensor_tensor(dm[:, b, :, :], dm[:, b, :, :],
                                   maskd[:, :].unsqueeze(1).broadcast_to([P, H, P]), ALU.add).then_inc(nm_masked, 1)
                pool.wait_ge(s_iw[b], c0 * 8 + 16 * (a // 2 + 1))
                pool.wait_ge(n_done, after(c0, a - 2))
                pool.tensor_tensor(qs2[:, b, :, :], qkm[:, 0:H, tok], iwb[:, b, :, :], ALU.mult).then_inc(q_scaled, 1)

            def low_out(c0, a):
                low(T_OUT + c0 + a, a % 2, True, bass.ds(c0 * P + a * P, P))

            stage(0, 0)
            stage(0, 1)
            with pool.Fori(0, ROUNDS - 1) as it:
                for a in range(2):
                    stage(it * 2, a + 2)
                    low_out(it * 2, a)
            low_out(NT - 2, 0)
            low_out(NT - 2, 1)

            def residual(it, a, first=0):
                pool.wait_ge(on_ready, after(it * 2, a))
                pool.wait_ge(s_xt[a], it * 16 + 16)
                pool.tensor_tensor(ot[:, a, first:D], ot[:, a, first:D], xt[:, a, first:D], ALU.add).then_inc(ot_ready, 1)

            with pool.Fori(0, ROUNDS - 1) as it:
                for a in range(2):
                    residual(it, a)
            residual(ROUNDS - 1, 0)
            residual(ROUNDS - 1, 1, HALF)

        @block.tensor
        def _(pe):
            LOW = 2 * KT
            WEIGHTS_STAY = [(0, i, k) for k in range(KT) for i in range(2)] + [(1, 0, k) for k in range(KT)]
            WEIGHTS_MOVE = [(i, 0, k) for k in range(KT) for i in range(2)] + [(0, 1, k) for k in range(KT)]

            def product(dst, stat, move, passes, lo, first=0, end=3 * KT, before=None):
                for n in range(first, end):
                    i, j, k = passes[n]
                    if n == LOW and lo is not None:
                        pe.wait_ge(w_lo, lo)
                    if before is not None and n % 2 == 0 and n < LOW:
                        before(k)
                    last = pe.matmul(dst, stat(i, k), move(j, k), start=(n == 0), stop=(n == 3 * KT - 1))
                return last

            start(pe, "pe")
            htp, wp, mtp = (ht_hi, ht_lo), (whi, wlo), (mt_hi, mt_lo)

            def feature_group(slot, half, lo, part=None, b=None, before=None):
                size = 3 * KT // PARTS
                first, end = (0, 3 * KT) if part is None else (size * part, size * (part + 1))
                return product(bank(half if b is None else b), lambda i, k: wp[i][:, k, P * slot:P * slot + P],
                               lambda j, k: htp[j][:, k, half * HALF:half * HALF + HALF],
                               WEIGHTS_STAY, lo, first, end, before)

            def token_group(tt, b, n, lo, src=htp):
                return product(bank(b, n), lambda i, k: src[i][:, k, P * tt:P * tt + P],
                               lambda j, k: wp[j][:, k, 0:n], WEIGHTS_MOVE, lo)

            pe.wait_ge(c_ready, 1)
            pe.wait_ge(s_par, 16 * 9)
            pe.transpose(bank(7, N_PT), prow[:, :], ident[0:N_PT, 0:N_PT]).then_inc(pt_done, 1)

            def turn_group(n, tiles, src, k):
                if n == 5:
                    pe.wait_ge(pt_ready, 1)
                if n >= 6:
                    pe.wait_ge(lo_done, n - 5)
                b = 2 + n % 6
                for i, t in enumerate(tiles):
                    last = pe.transpose(bank(b, P, P * i), src[:, t, P * k:P * k + P], ident[:, :])
                last.then_inc(tr_done, 1)

            pe.wait_ge(xn_ready, 2)
            for k in range(KT):
                turn_group(k, (0, 1), mraw, k)
            for n in range(2):
                pe.wait_ge(w_hi, n + 1)
                product(bank(n, NM), lambda i, k: wp[i][:, k, P * n:P * n + P], lambda j, k: mtp[j][:, k, :],
                        WEIGHTS_STAY, n + 1, before=None if n else (lambda k: pe.wait_ge(lo_done, k + 1))
                        ).then_inc(pj_done, 1)

            def turn_half(h2, first=0, end=KT):
                for k in range(first, end):
                    turn_group(8 + 8 * h2 + k, range(4 * h2, 4 * h2 + 4), xr, k)

            pe.wait_ge(xn_ready, 6)
            turn_half(0)
            pe.wait_ge(w_hi, 4)
            for n in range(2):
                pe.wait_ge(pj_free[n], 1)
                token_group(n, n, NM, 4, mtp).then_inc(pj_done, 1)
            pe.wait_ge(xn_ready, 10)
            turn_half(1, 0, 6)
            for g in range(4):
                half, a = g // 2, g % 2
                if half == 0:
                    pe.wait_ge(w_hi, T_KS + a + 1)
                pe.wait_ge(pj_free[a], G_KS // 2 + half)
                feature_group(a, half, T_KS + a + 1 if half == 0 else None, b=a,
                              before=(lambda k: pe.wait_ge(lo_done, 8 + 8 * half + k + 1)) if a == 0 else None
                              ).then_inc(pj_done, 1)
                if g == 0:
                    turn_half(1, 6, KT)
            for a in range(2):
                pe.wait_ge(w_hi, T_KS + 2 + a + 1)
                for half in range(2):
                    pe.wait_ge(pj_free[half], G_KS // 2 + 2 + a)
                    feature_group(a, half, T_KS + 2 + a + 1).then_inc(pj_done, 1)
            pe.wait_ge(w_hi, T_ZS)
            pe.wait_ge(gw_lo, 1)
            for tt in range(NT):
                pe.wait_ge(pj_free[tt % 2], G_VS // 2 + tt // 2)
                token_group(tt, tt % 2, 264, T_ZS).then_inc(pj_done, 1)
            pe.wait_ge(gt_ready, NT)
            for g in range(2):
                for tt in range(NT):
                    last = pe.transpose(bank(2 + 2 * g + tt // 4, P, P * (tt % 4), H),
                                        gt[:, tt, H * g:H * g + H], ident[:, :])
            last.then_inc(rt_done, 1)
            def turn_rows():
                pe.wait_ge(row_dve, 15)
                for r, row in enumerate((row_a, row_d, row_b)):
                    for c in range(NT):
                        last = pe.transpose(bank(6, H, (r * NT + c) * H), row[:, c, :], ident[0:H, 0:H])
                last.then_inc(ct_done, 1)

            for a in range(2):
                pe.wait_ge(w_hi, T_ZS + a + 1)
                for half in range(2):
                    pe.wait_ge(pj_free[half], G_ZS // 2 + a)
                    for part in range(PARTS):
                        if a == half == 1 and part == PARTS - 1:
                            turn_rows()
                        last = feature_group(a, half, T_ZS + a + 1, part)
                    last.then_inc(pj_done, 1)

            pe.wait_ge(ct_free, 1)
            with pe.Fori(0, 2) as hp:
                for what, j, part in order:
                    if what == "proj":
                        tile, half = j // 2, j % 2
                        if part == 0:
                            if half == 0:
                                pe.wait_ge(w_hi, hp * 6 + (T_SB + tile + 1))
                            pe.wait_ge(pj_free[half], hp * 6 + (G_SB // 2 + tile))
                        last = feature_group(tile % 2, half, hp * 6 + (T_SB + tile + 1), part)
                        if part == PARTS - 1:
                            last.then_inc(pj_done, 1)
                        continue
                    i, hh = j // 2, j % 2
                    if what == "scores":
                        n = P * (i + 1)
                        pe.wait_ge(q_staged, after(hp * 8, i))
                        pe.wait_ge(sg_ready, after(hp * 16, j - 2))
                        for lo in range(0, n, HALF):
                            w = min(HALF, n - lo)
                            for a, b in ((0, 0), (0, 1), (1, 0)):
                                pe.matmul(bank(2 + 2 * hh + lo // HALF, w), qz[a][:, i % 2, hh, :],
                                          (k_s_hi, k_s_lo)[b][:, bass.ds(hp * S + lo, w)], start=(a == b == 0),
                                          stop=(a == 1 and lo + w < n))
                        pe.matmul(bank(2 + 2 * hh + i // 4, P, P * (i % 4)), identb[:, :], maskb[:, :],
                                  start=False, stop=True).then_inc(z_ready, 1)
                    elif what == "turn":
                        g = seg_index[(j, part)]
                        pe.wait_ge(a_ready, after(hp * 16, j))
                        pe.wait_ge(t_ev, after(hp * NSEG, g - 1))
                        for s_ in range(4 * part, min(4 * part + 4, i + 1)):
                            last = pe.transpose(bank(6, P, P * (s_ % 4)), beta[:, hh, P * s_:P * s_ + P], ident[:, :])
                        last.then_inc(t_ready, 1)
                    else:
                        g = seg_index[(j, part)]
                        pe.wait_ge(t_ev, after(hp * NSEG, g))
                        if part == 0:
                            pe.wait_ge(o_ev, after(hp * 16, j - 1))
                        for s_ in range(4 * part, min(4 * part + 4, i + 1)):
                            vs = v_s[:, s_, :]
                            last = pe.matmul(bank(7, DA), at_[:, g % 2, P * (s_ % 4):P * (s_ % 4) + P],
                                             vs[:, bass.ds(hp * P + hh * DA, DA)], start=(s_ == 0), stop=(s_ == i))
                        last.then_inc(av_done, 1)
            with pe.Fori(0, 4) as it:
                for a in range(2):
                    pe.wait_ge(w_hi, it * 2 + (T_CONV + a + 1))
                    for half in range(2):
                        pe.wait_ge(pj_free[half], it * 2 + (G_CONV // 2 + a))
                        feature_group(a, half, it * 2 + (T_CONV + a + 1)).then_inc(pj_done, 1)
            def v_group(n):
                if n % NT == 0:
                    pe.wait_ge(w_hi, T_VM + 2 * (n // NT) + 2)
                pe.wait_ge(pj_free[n % 2], G_VM // 2 + n // 2)
                token_group(n % NT, n % 2, 256, T_VM + 2 * (n // NT) + 2).then_inc(pj_done, 1)

            def turn_out(b):
                pe.wait_ge(hn_ready, after(0, b))
                pe.wait_ge(y_done, after(0, b - 1))
                for m in range(4):
                    last = pe.transpose(bank(7, P, P * m), hnc[:, 2 * m:2 * m + 2, :].rearrange("p a b -> p (a b)"),
                                        ident[:, :])
                last.then_inc(yt_done, 1)

            def scores(b):
                pe.wait_ge(qc_staged, after(0, b))
                pe.wait_ge(p_ready, after(0, b - 1))
                for h in range(H):
                    last = pe.matmul(bank(2 + h // 2, NM, NM * (h % 2)), qcz[:, h, :], k_c[:, h // 2, :],
                                     start=True, stop=True)
                last.then_inc(sc_done, 1)

            scores(0)
            for b in range(NT):
                v_group(2 * b)
                if b == 0:
                    v_group(1)
                pe.wait_ge(p_ready, after(0, b))
                pe.wait_ge(pa_ev, after(0, b - 1))
                pe.wait_ge(pd_ev, after(0, b - 1))
                for m in range(2 * H):
                    last = pe.transpose(bank(4 + m // 4, P, P * (m % 4)), pc[:, m // 2, P * (m % 2):P * (m % 2) + P],
                                        ident[:, :])
                last.then_inc(pt2_done, 1)
                if b < NT - 1:
                    scores(b + 1)
                if 0 < b < NT - 1:
                    v_group(2 * b + 1)
                if b:
                    turn_out(b - 1)
                pe.wait_ge(pa_ev, after(0, b))
                pe.wait_ge(pd_ev, after(0, b))
                pe.wait_ge(hn_ready, after(0, b - 1))
                for h in range(H):
                    for m in range(2):
                        last = pe.matmul(bank(6, DA, DA * h), pct[:, P * (2 * h + m):P * (2 * h + m) + P],
                                         v_c[:, m, DA * h:DA * h + DA], start=(m == 0), stop=(m == 1))
                last.then_inc(oc_done, 1)
            v_group(2 * NT - 1)
            for half in range(2):
                pe.wait_ge(pj_free[half], G_END // 2)

            def m_scores(c0, a):
                pe.wait_ge(k_staged, after(c0, a))
                pe.wait_ge(sd_ready, after(c0, a - 1))
                for h in range(H):
                    last = pe.matmul(bank(0, P, P * h), kst[:, a % 2, h, :], qkm[:, h, bass.ds(c0 * P + a * P, P)],
                                     start=True, stop=True)
                last.then_inc(st_done, 1)
                pe.wait_ge(kw_ready, after(c0, a - 1))
                for h in range(H):
                    last = pe.transpose(bank(1, P, P * h), kst[:, a % 2, h, :], ident[:, :])
                last.then_inc(kt_done, 1)

            def m_outputs(c0, a):
                pe.wait_ge(q_scaled, after(c0, a))
                pe.wait_ge(sd_ready, after(c0, a))
                pe.wait_ge(c_upd, after(c0, a - 1))
                pe.wait_ge(ns_ready, after(c0, a - 1))
                for h in range(H):
                    dst = bank(4 + h // 2, VW, VW * (h % 2))
                    pe.matmul(dst, qs2[:, a, h, :], cst[:, h, :], start=True, stop=False)
                    last = pe.matmul(dst, sd[:, a, h, :], vm[:, bass.ds(c0 * (H * VW) + (a * H + h) * VW, VW)],
                                     start=False, stop=True)
                last.then_inc(n_done, 1)
                pe.wait_ge(kw_ready, after(c0, a))
                for h in range(H):
                    last = pe.matmul(bank(6 + h // 2, VW, VW * (h % 2)), kw[:, a, h, :],
                                     vm[:, bass.ds(c0 * (H * VW) + (a * H + h) * VW, VW)], start=True, stop=True)
                last.then_inc(kv_done, 1)

            def m_turn(c0, a):
                b = a % 2
                pe.wait_ge(hnm_ready, after(c0, a))
                pe.wait_ge(ygm_done, after(c0, a - 2))
                for h in range(H):
                    last = pe.transpose(bank(2 + b, P, P * h), hnm[:, b, h, :], ident[:, :])
                last.then_inc(ym_done, 1)

            def chunk_round(c0, first=False, final=False):
                m_outputs(c0, 0)
                m_scores(c0, 1)
                if not first:
                    m_turn(c0, -1)
                m_outputs(c0, 1)
                if not final:
                    m_scores(c0, 2)
                m_turn(c0, 0)

            m_scores(0, 0)
            turn_out(NT - 1)
            pe.wait_ge(y_done, after(0, NT - 1))
            pe.wait_ge(cst_zero, 1)
            pe.wait_ge(vm_ones, 1)
            chunk_round(0, first=True)
            with pe.Fori(1, ROUNDS - 1) as it:
                chunk_round(it * 2)
            chunk_round(NT - 2, final=True)

            def output(a, half, lo=None):
                y = (y_first[0][:, :, :], y_first[1][:, :, :]) if a == 0 else (whi[:, :, P:2 * P], wlo[:, :, P:2 * P])
                return product(bank(2 * a + half), lambda i, k: y[i][:, k, :],
                               lambda j, k: htp[j][:, k, HALF * half:HALF * half + HALF], WEIGHTS_MOVE, lo)

            pe.wait_ge(y_lo, after(0, 0))
            pe.wait_ge(w_hi, T_OUT + 4)
            output(0, 0, lo=T_OUT + NT // 2)
            m_turn(NT - 2, 1)
            pe.wait_ge(w_hi, T_END)
            output(0, 1, lo=T_END).then_inc(yo_done, 1)
            pe.wait_ge(y_lo, after(0, 1))
            pe.wait_ge(ygm_done, after(0, NT - 1))
            output(1, 0)
            output(1, 1).then_inc(yo_done, 1)
            with pe.Fori(1, ROUNDS) as it:
                for a in range(2):
                    pe.wait_ge(y_lo, after(it * 2, a))
                    pe.wait_ge(on_ready, after(it * 2, a - 2))
                    output(a, 0).then_inc(yo_half, 1)
                    output(a, 1).then_inc(yo_done, 1)

        @block.scalar
        def _(act):
            start(act, "act")
            chain = Chain(act, self_act)

            def func(dst, src, f, **kw):
                return act.activation(dst, src, f, **kw)

            act.preload_act_table_set("natural_log_exp_and_others")
            act.wait_ge(c_ready, 1)

            def high(slot, half_n, freed, col=None):
                act.wait_ge(s_raw[slot], half_n * 16 + 16)
                act.wait_ge(pj_done, freed)
                dst = whi[:, :, P * slot:P * slot + P] if col is None else ht_hi[:, :, col]
                func(dst, wraw[:, :, P * slot:P * slot + P], ACT.Copy).then_inc(w_hi, 1)

            def rms(tiles, src, at0, landed=None):
                for i, t in enumerate(tiles):
                    if landed is not None:
                        act.wait_ge(landed[i], 16)
                    chain(func(sq_in[:, :], src[:, t, :], ACT.Square, accum_out=ssx[:, at0 + i:at0 + i + 1]))
                chain(func(ssx[:, at0:at0 + 2], ssx[:, at0:at0 + 2], ACT.Ln, bias=epsc[:, :], scale=1.0 / D))
                func(rsx[:, at0:at0 + 2], ssx[:, at0:at0 + 2], ACT.Exp, scale=-0.5).then_inc(rs_ready, 1)

            rms((0, 1), mraw, 8, s_mem)
            act.wait_ge(pt_done, 1)
            func(pt[:, :], bank(7, N_PT), ACT.Copy).then_inc(pt_ready, 1)

            def split_high(n, dst, width, g):
                act.wait_ge(tr_done, n + 1)
                func(dst, bank(2 + n % 6, width), ACT.Copy, scale=g).then_inc(hi_done, 1)

            act.wait_ge(pt_ready, 1)
            for k in range(KT):
                split_high(k, mt_hi[:, k, :], NM, pt[:, PT_GMEM + k:PT_GMEM + k + 1])
                if k % 4 == 3:
                    n = k // 4
                    act.wait_ge(s_raw[n], 16)
                    func(whi[:, :, P * n:P * n + P], wraw[:, :, P * n:P * n + P], ACT.Copy).then_inc(w_hi, 1)

            def x_rms(i):
                act.wait_ge(s_x[i], 16)
                if i == 2:
                    rms((4, 5), xr, 4)
                    return
                chain(func(sq_in[:, :], xr[:, 2 * i, :], ACT.Square, accum_out=ssx[:, 2 * i:2 * i + 1]))
                act.wait_ge(sq_odd, min(i, 2) + 1)
                chain(func(ssx[:, 2 * i:2 * i + 2], ssx[:, 2 * i:2 * i + 2], ACT.Ln, bias=epsc[:, :], scale=1.0 / D))
                func(rsx[:, 2 * i:2 * i + 2], ssx[:, 2 * i:2 * i + 2], ACT.Exp, scale=-0.5).then_inc(rs_ready, 1)

            def x_high(h2, ks_=range(KT)):
                for k in ks_:
                    split_high(8 + 8 * h2 + k, ht_hi[:, k, HALF * h2:HALF * h2 + HALF], HALF,
                               pt[:, PT_GPRE + k:PT_GPRE + k + 1])

            x_rms(0)
            x_rms(1)
            high(0, 1, 1)
            x_high(0, range(0, 4))
            high(1, 1, 2)
            x_high(0, range(4, KT))
            x_rms(2)
            x_rms(3)
            high(0, 2, 4)
            high(1, 2, 4)
            act.wait_ge(s_gw, 16)
            func(whi[:, :, 256:264], wraw[:, :, 256:264], ACT.Copy).then_inc(gw_hi, 1)

            def sb_copy(g, tile, half, b):
                act.wait_ge(pj_done, g + 1)
                cols_ = slice(tile % 2 * S + half * HALF, tile % 2 * S + half * HALF + HALF)
                if tile < 2:
                    func(q_s[:, cols_], bank(b), ACT.Copy).then_inc(pj_free[b], 1)
                else:
                    func(k_s_hi[:, cols_], bank(b), ACT.Copy).then_inc(ks_high, 1)

            x_high(1, range(0, 6))
            sb_copy(G_KS, 0, 0, 0)
            x_high(1, range(6, KT))
            sb_copy(G_KS + 1, 1, 0, 1)
            sb_copy(G_KS + 2, 0, 1, 0)
            high(0, T_KS // 2 + 1, G_KS + 3)
            high(1, T_KS // 2 + 1, G_KS + 4)
            sb_copy(G_KS + 3, 1, 1, 1)
            for a in range(2):
                sb_copy(G_KS + 4 + 2 * a, 2 + a, 0, 0)
                high(a, T_VS // 2, G_KS + 4 + 2 * a + 2)
                sb_copy(G_KS + 5 + 2 * a, 2 + a, 1, 1)
            for a in range(2):
                high(a, T_ZS // 2, G_ZS)
            act.wait_ge(rt_done, 1)
            flat = lambda r: r[:, :, :].rearrange("h c t -> h (c t)")
            func(flat(row_a), ps[0:H, 2 * HALF:4 * HALF], ACT.Identity, bias=ifb[:, 0:1]).then_inc(row_act, 1)
            func(flat(row_m), ps[0:H, 4 * HALF:6 * HALF], ACT.Identity, bias=ifb[:, 1:2]).then_inc(row_act, 1)

            def raw_gate(n):
                a, half = n // 2, n % 2
                act.wait_ge(pj_done, G_ZS + n + 1)
                func(yg[:, 4 + a, HALF * half:HALF * half + HALF], bank(half), ACT.Copy).then_inc(pj_free[half], 1)

            raw_gate(0)
            act.wait_ge(row_dve, 1)
            func(flat(row_b), flat(row_b), ACT.Exp, scale=-1.0).then_inc(row_act, 1)
            act.wait_ge(row_act, 3)
            func(flat(row_b), flat(row_b), ACT.Ln, bias=onec[0:H, :]).then_inc(row_act, 1)
            raw_gate(1)
            high(0, T_SB // 2, G_ZS + 2)
            raw_gate(2)
            act.wait_ge(row_dve, 16)
            func(flat(row_iw), flat(row_iw), ACT.Exp).then_inc(row_act, 1)
            act.wait_ge(row_dve, 17)
            act.dma_start(rows_dram[0].rearrange("h (c t) -> h c t", c=NT), row_m[:, :, :]).then_inc(s_rows[0], 16)
            act.wait_ge(row_act, 5)
            act.dma_start(rows_dram[1].rearrange("h (c t) -> h c t", c=NT), row_iw[:, :, :]).then_inc(s_rows[1], 16)
            act.wait_ge(ct_done, 1)
            func(cols[:, 0, :], bank(6, NT * H), ACT.Copy)
            func(cols[:, 1:3, :].rearrange("p r n -> p (r n)"), bank(6, 2 * NT * H, NT * H), ACT.Exp).then_inc(ct_free, 1)
            high(1, T_SB // 2, G_SB)
            raw_gate(3)
            act.preload_act_table_set("sigmoid_and_others")
            act.wait_ge(s_rows[0], 16)
            with act.Fori(0, 2) as hp:
                for what, j, part in order:
                    if what == "scores":
                        i, hh = j // 2, j % 2
                        n = P * (i + 1)
                        act.wait_ge(z_ready, after(hp * 16, j))
                        back = seg_index[((j - 2) % 16, 0 if (j - 2) % 16 < 8 else 1)] - (NSEG if j < 2 else 0)
                        act.wait_ge(t_ready, after(hp * NSEG, back))
                        act.wait_ge(a_ready, after(hp * 16, j - 2))
                        z = ps[:, (2 + 2 * hh) * HALF:(2 + 2 * hh) * HALF + n]
                        func(keep[:, hh, 0:n], z, ACT.Sigmoid, scale=-(DA ** -0.5)).then_inc(kp_ready, 1)
                        func(beta[:, hh, 0:n], z, ACT.Sigmoid, scale=DA ** -0.5).then_inc(sg_ready, 1)
                    if what == "proj" and part == PARTS - 1:
                        tile, half = j // 2, j % 2
                        act.wait_ge(pj_done, hp * 12 + (G_SB + j + 1))
                        tok = slice(HALF * half, HALF * half + HALF)
                        ygf = yg[:, :, :].rearrange("p m t -> p (m t)")
                        if tile < 2:
                            func(ygf[:, bass.ds(hp * (2 * S) + (tile * S + half * HALF), HALF)], bank(half), ACT.Sigmoid
                                 ).then_inc(pj_free[half], 1)
                        elif tile < 4:
                            act.wait_ge(ts_free, after(hp * 4, j - 4 - 2))
                            func(ts[:, half, :], bank(half), ACT.Sigmoid).then_inc(gs_ready, 1)
                        elif tile == 4:
                            func(ygf[:, bass.ds(hp * S + (6 * S + half * HALF), HALF)], bank(half), ACT.Sigmoid
                                 ).then_inc(gs_ready, 1)
                        if half == 1:
                            high(tile % 2, hp * 3 + (T_SB + tile + 2) // 2, hp * 12 + (G_SB + j + 1))
            for n in range(4):
                a, half = n // 2, n % 2
                act.wait_ge(pj_free[half], G_ZS // 2 + a + 1)
                if n < 2:
                    act.wait_ge(ts_free, after(0, 2 * 4 - 1))
                else:
                    act.wait_ge(zs_gate, n - 1)
                func(ts[:, n % 2, :], yg[:, 4 + a, HALF * half:HALF * half + HALF], ACT.Sigmoid).then_inc(zs_sig, 1)
            act.wait_ge(cb_zero, 1)

            with act.Fori(0, 4) as it:
                for a in range(2):
                    m = it * 2 + a
                    for half in range(2):
                        act.wait_ge(pj_done, it * 4 + (G_CONV + 2 * a + half + 1))
                        act.wait_ge(cv_sum, after(it * 2, a - 2))
                        func(cb[:, a, 3 + HALF * half:3 + HALF * half + HALF], bank(half), ACT.Copy
                             ).then_inc(pj_free[half], 1)
                    high(a, it + (T_CONV // 2 + 1), it * 4 + (G_CONV + 2 * a + 2))
                    for half in range(2):
                        act.wait_ge(pj_free[half], it * 2 + (G_CONV // 2 + a + 1))
                    qk = qkm[:, :, :].rearrange("p m t -> p (m t)")[:, bass.ds(m * S, S)]
                    func(qk, cb[:, a, 3:3 + S], ACT.Identity, bias=pt[:, bass.ds(m + PT_CB, 1)],
                         scale=pt[:, bass.ds(m + (PT_CW + 3 * KT), 1)]).then_inc(cv_first, 1)
                    act.wait_ge(cv_sum, after(it * 2, a))
                    act.wait_ge(cv_out, after(it * 2, a - 2))
                    act.sem_inc(waited, 1)
                    func(sg[:, a, :], qk, ACT.Sigmoid).then_inc(cv_sig, 1)

            act.preload_act_table_set("natural_log_exp_and_others")

            def probabilities(b):
                act.wait_ge(mx_ready, after(0, b))
                act.wait_ge(pt2_done, after(0, b - 1))
                for h in range(H):
                    c = func(pc[:, h, :], bank(2 + h // 2, NM, NM * (h % 2)), ACT.Exp, bias=nmx[:, h:h + 1],
                             scale=DA ** -0.5, accum_out=sums[:, h:h + 1])
                c.then_inc(p_ready, 1)

            def v_copy(n):
                u, tt = n // NT, n % NT
                act.wait_ge(pj_done, G_VM + n + 1)
                func(vm4[:, tt, 2 * u:2 * u + 2, 0:DH],
                     bank(n % 2, 2 * DH).rearrange("p (a e) -> p a e", a=2), ACT.Copy).then_inc(pj_free[n % 2], 1)

            def decays(c0, a):
                b = a % 2
                act.wait_ge(nm_masked, after(c0, a))
                for h in range(H):
                    c = func(dm[:, b, h, :], dm[:, b, h, :], ACT.Exp, bias=col(c0, 0, a, h))
                c.then_inc(d_ready, 1)

            def col(c0, r, a, h):
                return cols[:, :, :].rearrange("p r n -> p (r n)")[:, bass.ds(c0 * H + (r * NT * H + a * H + h), 1)]

            probabilities(0)
            act.wait_ge(cv_out, after(0, 7))
            for b in range(NT):
                v_copy(2 * b)
                act.wait_ge(pt2_done, after(0, b))
                act.wait_ge(oc_done, after(0, b - 1))
                func(pct[:, HALF:2 * HALF], bank(5), ACT.Copy).then_inc(pa_ev, 1)
                if b < NT - 1:
                    v_copy(2 * b + 1)
                if b == NT // 2 - 1:
                    for a in range(2):
                        high(a, 1 + T_VM // 2, G_VM + NT)
                if b < NT - 1:
                    probabilities(b + 1)
                act.wait_ge(ssc_ready, after(0, b - 1))
                func(sqc[:, 0:H, :].rearrange("p h e -> p (h e)"), os_[:, b, :, :].rearrange("p h e -> p (h e)"),
                     ACT.Square)
                act.wait_ge(oc_done, after(0, b))
                func(sqc[:, H:2 * H, :].rearrange("p h e -> p (h e)"), bank(6, H * DA), ACT.Square
                     ).then_inc(sqc_ready, 1)
                if b == NT - 1:
                    decays(0, 0)
                act.wait_ge(ssc_ready, after(0, b))
                chain(func(l8[:, :], u8[:, :], ACT.Ln, bias=epsc[:, :], scale=1.0 / DA))
                func(l8[:, :], l8[:, :], ACT.Exp, scale=-0.5).then_inc(rsc_ready, 1)

            def weighted_keys(c0, a):
                b = a % 2
                act.wait_ge(kt_done, after(c0, a))
                act.wait_ge(kv_done, after(c0, a - 2))
                for h in range(H):
                    c = func(kw[:, b, h, :], bank(1, P, P * h), ACT.Copy, scale=col(c0, 1, a, h))
                c.then_inc(kw_ready, 1)

            def numerators(c0, a):
                act.wait_ge(n_done, after(c0, a))
                act.wait_ge(hnm_ready, after(c0, a - 2))
                func(ns[:, a, :, :].rearrange("p (b h) e -> p b (h e)", b=2),
                     ps[:, 4 * HALF:6 * HALF].rearrange("p (b n) -> p b n", b=2)[:, :, 0:2 * VW], ACT.Copy
                     ).then_inc(ns_ready, 1)
                act.wait_ge(ns_ready, after(c0, a))
                act.wait_ge(ssm_ready, after(c0, a - 1))
                func(sqm[:, :, :], ns[:, a, :, 0:DH], ACT.Square).then_inc(sqm_ready, 1)

            def head_rms(c0, a):
                act.wait_ge(ssm_ready, after(c0, a))
                chain(func(l4[:, :], u4[:, :], ACT.Ln, bias=epsc[:, :], scale=1.0 / DH))
                func(l4[:, :], l4[:, :], ACT.Exp, scale=-0.5).then_inc(rsm_ready, 1)

            def chunk_round(c0, half_tile, final=False):
                for a in range(2):
                    more = not (final and a == 1)
                    if more:
                        decays(c0, a + 1)
                    numerators(c0, a)
                    if more:
                        weighted_keys(c0, a + 1)
                    high(a, half_tile, G_END, bass.ds(c0 * P + a * P, P))
                    head_rms(c0, a)

            v_copy(2 * NT - 1)
            weighted_keys(0, 0)
            chunk_round(0, T_OUT // 2)
            with act.Fori(1, ROUNDS - 1) as it:
                chain.loop(it, 2, 1)
                chunk_round(it * 2, it + T_OUT // 2)
            chain.end(ROUNDS - 1)

            def y_high(reg, a):
                act.wait_ge(yo_done, after(reg * 2, a - 2))
                func(y_first[0][:, :, :] if a == 0 else whi[:, :, P:2 * P], yg[:, :, bass.ds(reg * 256 + a * P, P)],
                     ACT.Copy).then_inc(y_hi, 1)

            y_high(0, 0)
            chunk_round(NT - 2, ROUNDS - 1 + T_OUT // 2, final=True)
            act.wait_ge(ygm_done, after(0, NT - 1))

            def out_rms(it, a):
                act.wait_ge(yo_done, after(it * 2, a))
                chain(func(sq_out[:, :], ps[:, 2 * a * HALF:(2 * a + 2) * HALF], ACT.Square, accum_out=sso[:, a:a + 1]))
                chain(func(sso[:, a:a + 1], sso[:, a:a + 1], ACT.Ln, bias=epsc[:, :], scale=1.0 / D))
                act.wait_ge(on_ready, after(it * 2, a - 2))
                func(rso[:, a:a + 1], sso[:, a:a + 1], ACT.Exp, scale=-0.5).then_inc(rso_ready, 1)

            y_high(0, 1)
            act.wait_ge(s_gp, 16)
            with act.Fori(0, ROUNDS - 1) as it:
                chain.loop(it, 4)
                for a in range(2):
                    out_rms(it, a)
                    y_high(it + 1, a)
            chain.end(ROUNDS - 1)
            out_rms(ROUNDS - 1, 0)
            act.wait_ge(yo_half, 2 * (ROUNDS - 1))
            chain(func(sq_out[:, 0:HALF], bank(2), ACT.Square, accum_out=sso[:, 1:2]))
            act.wait_ge(yo_done, after(0, NT - 1))
            chain(func(sq_out[:, HALF:D], bank(3), ACT.Square, accum_out=sso_half[:, :]))
            chain(func(sso[:, 1:2], sso_half[:, :], ACT.Identity, bias=sso[:, 1:2]))
            chain(func(sso[:, 1:2], sso[:, 1:2], ACT.Ln, bias=epsc[:, :], scale=1.0 / D))
            act.wait_ge(on_ready, after(0, NT - 3))
            func(rso[:, 1:2], sso[:, 1:2], ACT.Exp, scale=-0.5).then_inc(rso_ready, 1)

        @block.vector
        def _(dve):
            start(dve, "dve")
            chain = Chain(dve, self_dve)

            def squares(i):
                dve.wait_ge(s_x[i], 16)
                if i:
                    dve.wait_ge(sq_odd, min(i, 2))
                dve.scalar_tensor_tensor(out=sq_odd_out[:, :], in0=xr[:, 2 * i + 1, :], scalar=1.0,
                                         in1=xr[:, 2 * i + 1, :], op0=ALU.mult, op1=ALU.mult,
                                         accum_out=ssx[:, 2 * i + 1:2 * i + 2]).then_inc(sq_odd, 1)

            def scale(i, src, t, at0):
                dve.wait_ge(rs_ready, i + 1)
                for k in range(2):
                    dve.tensor_scalar(src[:, t + k, :], src[:, t + k, :], rsx[:, at0 + k:at0 + k + 1], None,
                                      ALU.mult).then_inc(xn_ready, 1)

            def x_low(h2):
                for k in range(KT):
                    n = 8 + 8 * h2 + k
                    dve.wait_ge(hi_done, n + 1)
                    tok = slice(HALF * h2, HALF * h2 + HALF)
                    dve.scalar_tensor_tensor(out=ht_lo[:, k, tok], in0=bank(2 + n % 6),
                                             scalar=pt[:, PT_GPRE + k:PT_GPRE + k + 1],
                                             in1=ht_hi[:, k, tok].bitcast(F32), op0=ALU.mult, op1=ALU.subtract
                                             ).then_inc(lo_done, 1)

            scale(0, mraw, 0, 8)
            dve.wait_ge(pt_ready, 1)
            for k in range(KT):
                dve.wait_ge(hi_done, k + 1)
                dve.scalar_tensor_tensor(out=mt_lo[:, k, :], in0=bank(2 + k % 6, NM),
                                         scalar=pt[:, PT_GMEM + k:PT_GMEM + k + 1],
                                         in1=mt_hi[:, k, :].bitcast(F32), op0=ALU.mult, op1=ALU.subtract
                                         ).then_inc(lo_done, 1)
            squares(0)
            squares(1)
            scale(1, xr, 0, 0)
            scale(2, xr, 2, 2)
            for n in range(2):
                dve.wait_ge(pj_done, n + 1)
                dve.tensor_copy(k_c[:, n, :], bank(n, NM)).then_inc(pj_free[n], 1)
            x_low(0)
            squares(3)
            scale(3, xr, 4, 4)
            scale(4, xr, 6, 6)
            for n in range(2):
                dve.wait_ge(pj_done, n + 3)
                dve.tensor_copy(v_c[:, n, :], bank(n, NM)).then_inc(pj_free[n], 1)
            x_low(1)
            def low(n):
                dve.wait_ge(w_hi, n + 1)
                dve.tensor_tensor(wlo[:, :, P:2 * P], wraw[:, :, P:2 * P], whi[:, :, P:2 * P].bitcast(F32),
                                  ALU.subtract).then_inc(dve_low, 1)

            for n in range(4):
                b, cols_ = n % 2, slice(HALF * n, HALF * n + HALF)
                dve.wait_ge(ks_high, n + 1)
                dve.tensor_tensor(k_s_lo[:, cols_], bank(b), k_s_hi[:, cols_].bitcast(F32), ALU.subtract
                                  ).then_inc(pj_free[b], 1)
            low(T_VS + 1)
            for tt in range(NT):
                dve.wait_ge(pj_done, G_VS + tt + 1)
                dve.tensor_copy(gt[:, tt, :], bank(tt % 2, 8, 256)).then_inc(gt_ready, 1)
                dve.tensor_copy(v_s[:, tt, :], bank(tt % 2, 256)).then_inc(pj_free[tt % 2], 1)

            step = Chain(dve, row_dve)
            flat = lambda r: r[:, :, :].rearrange("h c t -> h (c t)")
            dve.wait_ge(row_act, 2)
            step(dve.scalar_tensor_tensor(out=flat(row_b), in0=flat(row_m), scalar=-1.0, in1=flat(row_m),
                                          op0=ALU.mult, op1=ALU.max))
            step(dve.memset(flat(row_d), 1.0))
            step(dve.memset(row_d[:, :, 0:1], 0.0))
            step(dve.memset(flat(row_e), 0.0))
            dve.wait_ge(row_act, 4)
            step(dve.scalar_tensor_tensor(out=flat(row_m), in0=flat(row_m), scalar=0.0, in1=flat(row_b),
                                          op0=ALU.min, op1=ALU.subtract))
            step(dve.tensor_tensor_scan(flat(row_b), flat(row_d), flat(row_m), 0.0, ALU.mult, ALU.add))
            step(dve.tensor_tensor(flat(row_a), flat(row_a), flat(row_b), ALU.subtract))
            step(dve.tensor_copy(bl_[:, :], row_b[:, :, P - 1]))
            step(dve.tensor_copy(row_e[:, 1:NT, 0], bl_[:, 0:NT - 1]))
            step(dve.tensor_tensor_scan(flat(row_m), flat(row_e), flat(row_a), 0.0, ALU.add, ALU.max))
            step(dve.tensor_copy(ml[:, :], row_m[:, :, P - 1]))
            step(dve.memset(mp[:, 0:1], 0.0))
            step(dve.tensor_tensor(mp[:, 1:NT], bl_[:, 0:NT - 1], ml[:, 0:NT - 1], ALU.add))
            step(dve.tensor_tensor(row_d[:, :, :], row_a[:, :, :], ml[:, :].unsqueeze(2).broadcast_to([H, NT, P]),
                                   ALU.subtract))
            step(dve.scalar_tensor_tensor(out=flat(row_b), in0=flat(row_b), scalar=-1.0, in1=flat(row_m),
                                          op0=ALU.mult, op1=ALU.subtract))
            step(dve.tensor_tensor(row_iw[:, :, :], mp[:, :].unsqueeze(2).broadcast_to([H, NT, P]), row_m[:, :, :],
                                   ALU.subtract))
            step(dve.tensor_scalar(flat(row_m), flat(row_m), -1.0, None, ALU.mult))
            dve.wait_ge(s_rows[1], 16)
            with dve.Fori(0, 2) as hp:
                chain.loop(hp, 16 + 4)
                ygf = yg[:, :, :].rearrange("p m t -> p (m t)")

                def shares(j):
                    hh, n = j % 2, P * (j // 2 + 1)
                    dve.wait_ge(kp_ready, after(hp * 16, j))
                    chain(dve.tensor_tensor_scan(keep[:, hh, n - 1::-1], keep[:, hh, n - 1::-1], keep[:, hh, n - 1::-1],
                                                 1.0, ALU.mult, ALU.bypass))
                    dve.wait_ge(sg_ready, after(hp * 16, j))
                    dve.tensor_tensor(beta[:, hh, 0:n - 1], beta[:, hh, 0:n - 1], keep[:, hh, 1:n], ALU.mult
                                      ).then_inc(a_ready, 1)

                def gates(j):
                    tile, half = j // 2, j % 2
                    if tile in (2, 3):
                        dve.wait_ge(gs_ready, after(hp * 6, j - 4))
                        m = hp * 2 + (tile - 2)
                        chain(dve.scalar_tensor_tensor(out=ts[:, half, :], in0=bank(half),
                                                       scalar=pt[:, bass.ds(m + PT_GM, 1)], in1=ts[:, half, :],
                                                       op0=ALU.mult, op1=ALU.mult))
                        dve.sem_inc(pj_free[half], 1)
                        y = ygf[:, bass.ds(hp * (2 * S) + ((tile - 2) * S + half * HALF), HALF)]
                        dve.tensor_tensor(y, y, ts[:, half, :], ALU.mult).then_inc(ts_free, 1)
                    elif tile == 4:
                        dve.wait_ge(gs_ready, after(hp * 6, j - 4))
                        y = ygf[:, bass.ds(hp * S + (6 * S + half * HALF), HALF)]
                        dve.scalar_tensor_tensor(out=y, in0=bank(half), scalar=pt[:, bass.ds(hp + PT_GC, 1)], in1=y,
                                                 op0=ALU.mult, op1=ALU.mult).then_inc(pj_free[half], 1)
                    elif tile == 5:
                        dve.wait_ge(pj_done, hp * 12 + (G_SB + j + 1))
                        dve.tensor_copy(q_c[:, :, :].rearrange("p m t -> p (m t)")[
                            :, bass.ds(hp * S + half * HALF, HALF)], bank(half)).then_inc(pj_free[half], 1)

                late = None
                for what, j, part in order:
                    i, hh = j // 2, j % 2
                    if what == "scores" and j == 0:
                        shares(0)
                    if what == "turn":
                        g = seg_index[(j, part)]
                        n = P * (min(4 * part + 4, i + 1) - 4 * part)
                        dve.wait_ge(t_ready, after(hp * NSEG, g))
                        dve.wait_ge(av_done, after(hp * NSEG, g - 2))
                        dve.tensor_copy(at_[:, g % 2, 0:n], bank(6, n)).then_inc(t_ev, 1)
                        if late is not None:
                            gates(late)
                            late = None
                    if what == "values" and (i < 4 or part == 1):
                        if j < 15:
                            shares(j + 1)
                        g = seg_index[(j, part)]
                        dve.wait_ge(av_done, after(hp * NSEG, g))
                        dve.tensor_copy(os_[:, :, :, :].rearrange("p i h e -> p (i h e)")[
                            :, bass.ds(hp * (2 * DA) + (i * H * DA + hh * DA), DA)], bank(7, DA)).then_inc(o_ev, 1)
                    if what == "proj" and part == PARTS - 1:
                        if late is not None:
                            gates(late)
                        late = j
                if late is not None:
                    gates(late)
            chain.end(2)
            for n in range(4):
                a, half = n // 2, n % 2
                y = yg[:, 4 + a, HALF * half:HALF * half + HALF]
                dve.wait_ge(zs_sig, n + 1)
                dve.scalar_tensor_tensor(out=y, in0=y, scalar=pt[:, PT_GS + a:PT_GS + a + 1], in1=ts[:, n % 2, :],
                                         op0=ALU.mult, op1=ALU.mult).then_inc(zs_gate, 1)
            dve.wait_ge(av_done, after(0, 2 * NSEG - 1))
            dve.memset(cb[:, :, 0:3], 0.0).then_inc(cb_zero, 1)

            def maximum(b):
                dve.wait_ge(sc_done, after(0, b))
                chain(dve.tensor_reduce(mx[:, :], ps[:, 2 * HALF:4 * HALF].rearrange("p (h m) -> p h m", h=H),
                                        AX_X, ALU.max))
                dve.tensor_scalar(nmx[:, :], mx[:, :], -(DA ** -0.5), None, ALU.mult).then_inc(mx_ready, 1)

            def conv_tile(it, a, final=False):
                m = it * 2 + a
                qk = qkm[:, :, :].rearrange("p m t -> p (m t)")[:, bass.ds(m * S, S)]
                dve.wait_ge(cv_first, after(it * 2, a))
                for j in (2, 1, 0):
                    c = dve.scalar_tensor_tensor(out=qk, in0=cb[:, a, j:j + S],
                                                 scalar=pt[:, bass.ds(m + (PT_CW + j * KT), 1)], in1=qk,
                                                 op0=ALU.mult, op1=ALU.add)
                    if j:
                        chain(c)
                c.then_inc(cv_sum, 1)
                if final:
                    maximum(0)
                dve.wait_ge(cv_sig, after(it * 2, a))
                dve.scalar_tensor_tensor(out=qk, in0=qk, scalar=ks[:, bass.ds(m, 1)], in1=sg[:, a, :],
                                         op0=ALU.mult, op1=ALU.mult).then_inc(cv_out, 1)

            with dve.Fori(0, 3) as it:
                chain.loop(it, 4)
                for a in range(2):
                    conv_tile(it, a)
            chain.end(3)
            for a in range(2):
                conv_tile(3, a, final=(a == 1))
            def gate(b):
                dve.wait_ge(yt_done, after(0, b))
                y = yg[:, 4:8, P * b:P * b + P]
                dve.tensor_tensor(y, y, bank(7).rearrange("p (m t) -> p m t", m=4), ALU.mult).then_inc(y_done, 1)

            for b in range(NT):
                dve.wait_ge(p_ready, after(0, b))
                chain(dve.reciprocal(r8[:, H:2 * H], sums[:, :]))
                dve.wait_ge(pt2_done, after(0, b))
                dve.wait_ge(oc_done, after(0, b - 1))
                dve.tensor_copy(pct[:, 0:HALF], bank(4)).then_inc(pd_ev, 1)
                if b < NT - 1:
                    maximum(b + 1)
                if b == NT // 2 - 1:
                    low(T_VM + 3)
                if b:
                    gate(b - 1)
                dve.wait_ge(sqc_ready, after(0, b))
                chain(dve.tensor_reduce(ss8[:, :], sqc[:, :, :], AX_X, ALU.add))
                chain(dve.tensor_tensor(ss8[:, :], ss8[:, :], r8[:, :], ALU.mult))
                dve.tensor_tensor(u8[:, :], ss8[:, :], r8[:, :], ALU.mult).then_inc(ssc_ready, 1)
                dve.wait_ge(rsc_ready, after(0, b))
                chain(dve.tensor_tensor(cf8[:, :], l8[:, :], r8[:, :], ALU.mult))
                dve.wait_ge(yt_done, after(0, b - 1))
                dve.tensor_tensor(hnc[:, 0:H, :], os_[:, :, :, :].rearrange("p i h e -> p (i h) e")[
                    :, H * b:H * b + H, :], cf8[:, 0:H].unsqueeze(2).broadcast_to([P, H, DA]), ALU.mult)
                dve.tensor_tensor(hnc[:, H:2 * H, :], bank(6, H * DA).rearrange("p (h e) -> p h e", h=H),
                                  cf8[:, H:2 * H].unsqueeze(2).broadcast_to([P, H, DA]), ALU.mult).then_inc(hn_ready, 1)
            dve.wait_ge(pj_done, G_END)
            chain(dve.memset(cst[:, :, :], 0.0))
            dve.sem_inc(cst_zero, 1)
            dve.wait_ge(s_dec, 16)

            def decayed_scores(c0, a):
                b = a % 2
                dve.wait_ge(d_ready, after(c0, a))
                dve.wait_ge(st_done, after(c0, a))
                dve.wait_ge(n_done, after(c0, a - 2))
                dve.tensor_tensor(sd[:, b, :, :], bank(0).rearrange("p (h t) -> p h t", h=H), dm[:, b, :, :],
                                  ALU.mult).then_inc(sd_ready, 1)

            def denominators(c0, a):
                dve.wait_ge(ns_ready, after(c0, a))
                chain(dve.scalar_tensor_tensor(out=den[:, :], in0=ns[:, a, :, DH], scalar=-1.0, in1=ns[:, a, :, DH],
                                               op0=ALU.mult, op1=ALU.max))
                chain(dve.tensor_tensor(den[:, :], den[:, :], cols[:, 2, bass.ds(c0 * H + a * H, H)], ALU.max))
                chain(dve.reciprocal(r4[:, :], den[:, :]))

            def new_state(c0, a):
                dve.wait_ge(kv_done, after(c0, a))
                decf = dec[:, :, :].rearrange("p h c -> p (h c)")
                for h in range(H):
                    c = dve.scalar_tensor_tensor(out=cst[:, h, :], in0=cst[:, h, :],
                                                 scalar=decf[:, bass.ds(c0 + (h * NT + a), 1)],
                                                 in1=bank(6 + h // 2, VW, VW * (h % 2)), op0=ALU.mult, op1=ALU.add)
                c.then_inc(c_upd, 1)

            def mean_squares(c0, a):
                dve.wait_ge(sqm_ready, after(c0, a))
                chain(dve.tensor_reduce(ss4[:, :], sqm[:, :, :], AX_X, ALU.add))
                chain(dve.tensor_tensor(ss4[:, :], ss4[:, :], r4[:, :], ALU.mult))
                dve.tensor_tensor(u4[:, :], ss4[:, :], r4[:, :], ALU.mult).then_inc(ssm_ready, 1)

            def normed(c0, a):
                dve.wait_ge(rsm_ready, after(c0, a))
                chain(dve.tensor_tensor(cf4[:, :], l4[:, :], r4[:, :], ALU.mult))
                dve.wait_ge(ym_done, after(c0, a - 2))
                dve.tensor_tensor(hnm[:, a, :, :], ns[:, a, :, 0:DH], cf4[:, :].unsqueeze(2).broadcast_to([P, H, DH]),
                                  ALU.mult).then_inc(hnm_ready, 1)

            def gated(c0, a):
                b = a % 2
                dve.wait_ge(ym_done, after(c0, a))
                y = yg[:, 0:H, bass.ds(c0 * P + a * P, P)]
                dve.tensor_tensor(y, y, bank(2 + b).rearrange("p (h t) -> p h t", h=H), ALU.mult).then_inc(ygm_done, 1)

            def chunk_round(c0, first=False, final=False):
                for a in range(2):
                    new_state(c0, a)
                    if not (final and a == 1):
                        decayed_scores(c0, a + 1)
                    denominators(c0, a)
                    mean_squares(c0, a)
                    if not (first and a == 0):
                        gated(c0, a - 1)
                    normed(c0, a)

            decayed_scores(0, 0)
            gate(NT - 1)
            chunk_round(0, first=True)
            with dve.Fori(1, ROUNDS - 1) as it:
                chain.loop(it, 2 * 6, 1)
                chunk_round(it * 2)
            chain.end(ROUNDS - 1)

            def y_low(reg, a):
                hi, lo = (y_first[0][:, :, :], y_first[1][:, :, :]) if a == 0 else (whi[:, :, P:2 * P], wlo[:, :, P:2 * P])
                dve.wait_ge(y_hi, after(reg * 2, a))
                dve.tensor_tensor(lo, yg[:, :, bass.ds(reg * 256 + a * P, P)], hi.bitcast(F32), ALU.subtract
                                  ).then_inc(y_lo, 1)

            y_low(0, 0)
            chunk_round(NT - 2, final=True)
            gated(NT - 2, 1)

            def out_norm(it, a):
                dve.wait_ge(rso_ready, after(it * 2, a))
                dve.wait_ge(s_out[a], it * 16 + 16)
                dve.scalar_tensor_tensor(out=ot[:, a, :], in0=ps[:, 2 * a * HALF:(2 * a + 2) * HALF],
                                         scalar=rso[:, a:a + 1], in1=gpost[:, :], op0=ALU.mult, op1=ALU.mult
                                         ).then_inc(on_ready, 1)

            y_low(0, 1)
            dve.wait_ge(s_gp, 16)
            with dve.Fori(0, ROUNDS - 1) as it:
                for a in range(2):
                    out_norm(it, a)
                    y_low(it + 1, a)
            out_norm(ROUNDS - 1, 0)
            dve.wait_ge(rso_ready, after(0, NT - 1))
            dve.wait_ge(s_out[1], 16 * ROUNDS)
            for half in (1, 0):
                cols_ = slice(HALF * half, HALF * half + HALF)
                c = dve.scalar_tensor_tensor(out=ot[:, 1, cols_], in0=bank(2 + half), scalar=rso[:, 1:2],
                                             in1=gpost[:, cols_], op0=ALU.mult, op1=ALU.mult)
                if half:
                    c.then_inc(on_ready, 1)
                else:
                    chain(c)
            dve.wait_ge(s_xt[1], 16 * ROUNDS)
            dve.tensor_tensor(ot[:, 1, 0:HALF], ot[:, 1, 0:HALF], xt[:, 1, 0:HALF], ALU.add).then_inc(ot_last, 1)


_INS = ["x", "mem", "g_pre", "w_in", "conv_w", "conv_b", "i_bias", "f_bias", "g_mlstm_head", "g_sb_head",
        "g_mem_head", "g_mem", "w_mem_kv", "w_out", "g_post"]


def kernel(**inputs):
    import numpy as _np
    import concourse.bacc as _bacc
    from concourse import mybir as _mybir
    from concourse.bass_utils import run_bass_kernel_spmd as _run

    nc = _bacc.Bacc("TRN2", target_bir_lowering=False, num_devices=1)
    arrays, args = {}, []
    for name in _INS:
        a = _np.ascontiguousarray(inputs[name])
        arrays[f"in_{name}_dram"] = a
        args.append(nc.dram_tensor(f"in_{name}_dram", a.shape, _mybir.dt.from_np(a.dtype), kind="ExternalInput").ap())
    args.append(nc.dram_tensor("out_dram", (1, S, D), _mybir.dt.float32, kind="ExternalOutput").ap())
    args.append(nc.dram_tensor("rows_dram", (2, H, S), _mybir.dt.float32, kind="Internal").ap())
    hybrid_layer(nc, *args)
    r = _run(nc, [arrays], core_ids=[0])
    return r.results[0]["out_dram"]
```
